# Optimizing a Trainium2 kernel written in Bass

```python
import math
import jax, jax.numpy as jnp
from jax import lax
import numpy as np

D_MODEL = 1024
BATCH = 1
SEQ = 2048
DEPTH = 1
DEC_BATCH = 8
DEC_SEQ = 8
PAST_LEN = 1024
PAGE_SIZE = 128

D_MIX = D_MODEL
H_M = 5
HD_M = 128
D_M = H_M * HD_M
H_A = 6
HD_A = 64
D_A = H_A * HD_A
CONV_W = 4
MLSTM_CHUNK = 64
DILATED_PATTERNS = ((128, 1), (512, 4), (2048, 16))
MAX_WINDOW = 2048
D_FF = ((8 * D_MODEL + 767) // 768) * 256
N_IN = 4 * D_M + 2 * H_M + 3 * D_A
EPS = 1e-6

kernel_name = "hymba_mlstm_dilated_swa_decoder_step"

def rms_norm(x, g):
    xf = x.astype(jnp.float32)
    y = xf * lax.rsqrt(jnp.mean(xf * xf, axis=-1, keepdims=True) + EPS)
    return (y * g.astype(jnp.float32)).astype(x.dtype)

def alibi_slopes():
    return 2.0 ** (-8.0 * jnp.arange(1, H_A + 1, dtype=jnp.float32) / H_A)

def causal_conv(u, buf, w):
    T = u.shape[1]
    cat = jnp.concatenate([buf.astype(u.dtype), u], axis=1)
    out = sum(cat[:, i:i + T] * w[i] for i in range(CONV_W))
    return out, cat[:, T:]

def mlstm_chunkwise(q, k, v, ig, lf, C0, n0, m0):
    B, T, H, D = q.shape
    lc = math.gcd(T, MLSTM_CHUNK)
    nc = T // lc
    f32 = jnp.float32

    def chunks(a):
        a = a.astype(f32)
        return jnp.swapaxes(a.reshape((B, nc, lc) + a.shape[2:]), 0, 1)

    causal = jnp.tril(jnp.ones((lc, lc), dtype=bool))

    def step(carry, inp):
        C, n, m = carry
        qc, kc, vc, ic, fc = inp
        b = jnp.swapaxes(jnp.cumsum(fc, axis=1), 1, 2)
        ih = jnp.swapaxes(ic, 1, 2)
        dlog = jnp.where(causal, b[..., :, None] - b[..., None, :] + ih[..., None, :], -jnp.inf)
        inter = b + m[..., None]
        mt = jnp.maximum(inter, jnp.max(dlog, axis=-1))
        s = jnp.einsum('bthd,bshd->bhts', qc, kc) * jnp.exp(dlog - mt[..., None])
        e_inter = jnp.exp(inter - mt)
        num = jnp.einsum('bhts,bshd->bhtd', s, vc) + e_inter[..., None] * jnp.einsum('bhvk,bthk->bhtv', C, qc)
        den = jnp.sum(s, axis=-1) + e_inter * jnp.einsum('bhk,bthk->bht', n, qc)
        h = num / jnp.maximum(jnp.abs(den), jnp.exp(-mt))[..., None]
        b_last = b[..., -1]
        wlog = b_last[..., None] - b + ih
        m_new = jnp.maximum(b_last + m, jnp.max(wlog, axis=-1))
        w = jnp.exp(wlog - m_new[..., None])
        decay = jnp.exp(b_last + m - m_new)
        C_new = decay[..., None, None] * C + jnp.einsum('bhs,bshv,bshk->bhvk', w, vc, kc)
        n_new = decay[..., None] * n + jnp.einsum('bhs,bshk->bhk', w, kc)
        return (C_new, n_new, m_new), jnp.swapaxes(h, 1, 2)

    init = (C0.astype(f32), n0.astype(f32), m0.astype(f32))
    (C, n, m), hs = lax.scan(step, init, (chunks(q), chunks(k), chunks(v), chunks(ig), chunks(lf)))
    h = jnp.swapaxes(hs, 0, 1).reshape(B, T, H, D)
    return h, C, n, m

def combine_patterns(outs, lses):
    w = jax.nn.softmax(jnp.stack(lses, axis=0), axis=0)
    return jnp.sum(w[..., None] * jnp.stack(outs, axis=0), axis=0)

def dilated_attention_prompt(q, k, v, slopes):
    B, S, H, D = q.shape
    f32 = jnp.float32
    scale = HD_A ** -0.5
    outs, lses = [], []
    for win, dil in DILATED_PATTERNS:
        nw = win // dil
        L = S // dil
        nb = -(-L // nw)
        lp = nb * nw

        def to_blocks(a):
            a = jnp.transpose(a.reshape(B, L, dil, H, D), (0, 2, 1, 3, 4))
            a = jnp.pad(a, ((0, 0), (0, 0), (0, lp - L), (0, 0), (0, 0)))
            return a.reshape(B, dil, nb, nw, H, D)

        qb, kb, vb = to_blocks(q), to_blocks(k), to_blocks(v)
        pad_prev = ((0, 0), (0, 0), (1, 0), (0, 0), (0, 0), (0, 0))
        kc = jnp.concatenate([jnp.pad(kb, pad_prev)[:, :, :-1], kb], axis=3)
        vc = jnp.concatenate([jnp.pad(vb, pad_prev)[:, :, :-1], vb], axis=3)
        qi = jnp.arange(nw)[:, None]
        ki = jnp.arange(2 * nw)[None, :]
        dist = qi + nw - ki
        band = (dist >= 0) & (dist <= nw)
        valid = band[None] & ((jnp.arange(nb)[:, None, None] > 0) | (ki[None] >= nw))
        bias = -slopes[:, None, None] * (dist * dil).astype(f32)[None]
        s = jnp.einsum('brnqhd,brnkhd->brnhqk', qb, kc).astype(f32) * scale + bias
        s = jnp.where(valid[:, None], s, -jnp.inf)
        mx = jnp.max(s, axis=-1, keepdims=True)
        p = jnp.exp(s - mx)
        den = jnp.sum(p, axis=-1)
        o = jnp.einsum('brnhqk,brnkhd->brnqhd', p, vc.astype(f32)) / jnp.moveaxis(den, 3, 4)[..., None]
        lse = jnp.moveaxis(mx[..., 0] + jnp.log(den), 3, 4)
        o = jnp.transpose(o.reshape(B, dil, lp, H, D)[:, :, :L], (0, 2, 1, 3, 4)).reshape(B, S, H, D)
        lse = jnp.transpose(lse.reshape(B, dil, lp, H)[:, :, :L], (0, 2, 1, 3)).reshape(B, S, H)
        outs.append(o)
        lses.append(lse)
    return combine_patterns(outs, lses)

def dilated_attention_sample(q, k_all, v_all, slopes):
    B, T, H, D = q.shape
    f32 = jnp.float32
    scale = HD_A ** -0.5
    wb = k_all.shape[1] - T
    outs, lses = [], []
    for win, dil in DILATED_PATTERNS:
        nw = win // dil
        j = jnp.arange(nw + 1)
        idx = wb + jnp.arange(T)[:, None] - j[None, :] * dil
        valid = idx >= 0
        idx = jnp.maximum(idx, 0)
        kg = k_all[:, idx]
        vg = v_all[:, idx]
        bias = -slopes[:, None, None] * (j * dil).astype(f32)[None, None, :]
        s = jnp.einsum('bthd,btjhd->bhtj', q, kg).astype(f32) * scale + bias
        s = jnp.where(valid, s, -jnp.inf)
        mx = jnp.max(s, axis=-1, keepdims=True)
        p = jnp.exp(s - mx)
        den = jnp.sum(p, axis=-1)
        o = jnp.einsum('bhtj,btjhd->bthd', p, vg.astype(f32)) / jnp.swapaxes(den, 1, 2)[..., None]
        lse = jnp.swapaxes(mx[..., 0] + jnp.log(den), 1, 2)
        outs.append(o)
        lses.append(lse)
    return combine_patterns(outs, lses)

def hybrid_layer(x, params, conv_buf, C0, n0, m0, kv_past):
    (g_mix_pre, g_mix_post, g_ffn_pre, g_ffn_post, w_in, b_gates, w_conv, g_mh,
     w_out, w_gate, w_up, w_down) = params
    B, T, _ = x.shape
    f32 = jnp.float32
    a = rms_norm(x, g_mix_pre)
    z = a @ w_in
    cuts = [2 * D_M, 3 * D_M, 4 * D_M, 4 * D_M + 2 * H_M,
            4 * D_M + 2 * H_M + D_A, 4 * D_M + 2 * H_M + 2 * D_A]
    qk_pre, v_m, o_m, gates, q_a, k_a, v_a = jnp.split(z, cuts, axis=-1)

    qk, new_conv = causal_conv(qk_pre, conv_buf, w_conv)
    qk = jax.nn.silu(qk)
    q_m = qk[..., :D_M].reshape(B, T, H_M, HD_M)
    k_m = qk[..., D_M:].reshape(B, T, H_M, HD_M) * (HD_M ** -0.5)
    gates = gates.astype(f32) + b_gates.astype(f32)
    h_m, C, n, m = mlstm_chunkwise(q_m, k_m, v_m.reshape(B, T, H_M, HD_M),
                                   gates[..., :H_M], jax.nn.log_sigmoid(gates[..., H_M:]),
                                   C0, n0, m0)
    h_m = rms_norm(h_m.astype(x.dtype), g_mh.reshape(H_M, HD_M)).reshape(B, T, D_M)
    h_m = jax.nn.sigmoid(o_m) * h_m

    q_a = q_a.reshape(B, T, H_A, HD_A)
    k_a = k_a.reshape(B, T, H_A, HD_A)
    v_a = v_a.reshape(B, T, H_A, HD_A)
    slopes = alibi_slopes()
    if kv_past is None:
        h_a = dilated_attention_prompt(q_a, k_a, v_a, slopes)
        kv_new = jnp.stack([k_a, v_a], axis=2)[:, T - min(MAX_WINDOW, T):]
    else:
        k_all = jnp.concatenate([kv_past[:, :, 0].astype(k_a.dtype), k_a], axis=1)
        v_all = jnp.concatenate([kv_past[:, :, 1].astype(v_a.dtype), v_a], axis=1)
        h_a = dilated_attention_sample(q_a, k_all, v_all, slopes)
        kv_new = jnp.stack([k_a, v_a], axis=2)

    mix = jnp.concatenate([h_m, h_a.astype(x.dtype).reshape(B, T, D_A)], axis=-1) @ w_out
    x = x + rms_norm(mix, g_mix_post)
    hf = rms_norm(x, g_ffn_pre)
    f = (jax.nn.silu(hf @ w_gate) * (hf @ w_up)) @ w_down
    x = x + rms_norm(f, g_ffn_post)
    return x, kv_new, C, n, m, new_conv

def setup_inputs(seed: int = 0) -> dict:
    key = jax.random.key(seed)
    ks = jax.random.split(key, 24)
    f32 = jnp.float32
    wb = min(MAX_WINDOW, PAST_LEN)

    def nrm(k, shape, s=1.0):
        return s * jax.random.normal(k, shape, f32)

    return {
        "x_prompt": nrm(ks[0], (BATCH, SEQ, D_MODEL)),
        "x_sample": nrm(ks[1], (DEC_BATCH, DEC_SEQ, D_MODEL)),
        "cache_kv": nrm(ks[2], (DEPTH, DEC_BATCH, wb, 2, H_A, HD_A)),
        "state_C": nrm(ks[3], (DEPTH, DEC_BATCH, H_M, HD_M, HD_M), 0.05),
        "state_n": nrm(ks[4], (DEPTH, DEC_BATCH, H_M, HD_M), 0.1),
        "state_m": nrm(ks[5], (DEPTH, DEC_BATCH, H_M), 0.5),
        "state_conv": nrm(ks[6], (DEPTH, DEC_BATCH, CONV_W - 1, 2 * D_M)),
        "g_mix_pre": 1.0 + nrm(ks[7], (DEPTH, D_MODEL), 0.02),
        "g_mix_post": 1.0 + nrm(ks[8], (DEPTH, D_MODEL), 0.02),
        "g_ffn_pre": 1.0 + nrm(ks[9], (DEPTH, D_MODEL), 0.02),
        "g_ffn_post": 1.0 + nrm(ks[10], (DEPTH, D_MODEL), 0.02),
        "w_in": nrm(ks[11], (DEPTH, D_MODEL, N_IN), D_MODEL ** -0.5),
        "b_gates": jnp.concatenate(
            [nrm(ks[12], (DEPTH, H_M), 0.1),
             jnp.linspace(3.0, 6.0, H_M, dtype=f32)[None] + nrm(ks[13], (DEPTH, H_M), 0.1)], axis=-1),
        "w_conv": nrm(ks[14], (DEPTH, CONV_W, 2 * D_M), CONV_W ** -0.5),
        "g_mh": 1.0 + nrm(ks[15], (DEPTH, D_M), 0.02),
        "w_out": nrm(ks[16], (DEPTH, D_MIX, D_MODEL), D_MIX ** -0.5),
        "w_gate": nrm(ks[17], (DEPTH, D_MODEL, D_FF), D_MODEL ** -0.5),
        "w_up": nrm(ks[18], (DEPTH, D_MODEL, D_FF), D_MODEL ** -0.5),
        "w_down": nrm(ks[19], (DEPTH, D_FF, D_MODEL), D_FF ** -0.5),
    }

def reference(x_prompt, x_sample, cache_kv, state_C, state_n, state_m, state_conv,
              g_mix_pre, g_mix_post, g_ffn_pre, g_ffn_post, w_in, b_gates, w_conv, g_mh,
              w_out, w_gate, w_up, w_down):
    f32 = jnp.float32
    B = x_prompt.shape[0]
    hp, hs = x_prompt, x_sample
    kv_p, C_p, n_p, m_p, cv_p = [], [], [], [], []
    kv_s, C_s, n_s, m_s, cv_s = [], [], [], [], []
    for l in range(DEPTH):
        params = (g_mix_pre[l], g_mix_post[l], g_ffn_pre[l], g_ffn_post[l], w_in[l], b_gates[l],
                  w_conv[l], g_mh[l], w_out[l], w_gate[l], w_up[l], w_down[l])
        hp, kv, C, n, m, cv = hybrid_layer(
            hp, params,
            jnp.zeros((B, CONV_W - 1, 2 * D_M), hp.dtype),
            jnp.zeros((B, H_M, HD_M, HD_M), f32),
            jnp.zeros((B, H_M, HD_M), f32),
            jnp.zeros((B, H_M), f32),
            None)
        kv_p.append(kv); C_p.append(C); n_p.append(n); m_p.append(m); cv_p.append(cv)
        hs, kv, C, n, m, cv = hybrid_layer(
            hs, params, state_conv[l], state_C[l], state_n[l], state_m[l], cache_kv[l])
        kv_s.append(kv); C_s.append(C); n_s.append(n); m_s.append(m); cv_s.append(cv)
    return (hp, hs,
            jnp.stack(kv_p), jnp.stack(kv_s),
            jnp.stack(C_p), jnp.stack(n_p), jnp.stack(m_p), jnp.stack(cv_p),
            jnp.stack(C_s), jnp.stack(n_s), jnp.stack(m_s), jnp.stack(cv_s))


_drawn_inputs = setup_inputs


def setup_inputs(seed=0):
    import zlib

    import numpy as np

    out = dict(_drawn_inputs(seed))
    spreads = {}
    factors = {'g_mix_post': 3.604, 'g_ffn_pre': 3.429, 'g_ffn_post': 5.047, 'g_mh': 3.737}
    for name, (base, spread) in spreads.items():
        noise = np.random.default_rng([zlib.crc32(name.encode()), seed]).standard_normal(out[name].shape)
        drawn = base * np.exp(spread * noise) if base else spread * noise
        out[name] = __import__('jax').numpy.asarray(drawn.astype(out[name].dtype))
    for name, factor in factors.items():
        out[name] = (out[name] * factor).astype(out[name].dtype)
    return out
```

```python
from contextlib import ExitStack

import concourse.bass as bass
from concourse import mybir

F32 = mybir.dt.float32
BF16 = mybir.dt.bfloat16
ALU = mybir.AluOpType
ACT = mybir.ActivationFunctionType
ds = bass.ds

P = 128
D_MODEL = 1024
SEQ = 2048
DEC_BATCH = 8
DEC_SEQ = 8
PAST_LEN = 1024
H_M, HD_M = 5, 128
H_A, HD_A = 6, 64
D_M = H_M * HD_M
D_A = H_A * HD_A
CONV_W = 4
HIST = CONV_W - 1
D_FF = ((8 * D_MODEL + 767) // 768) * 256
EPS = 1e-6

NSAMP = DEC_BATCH * DEC_SEQ
NTOK = SEQ + NSAMP
TILES = SEQ // P
SAMPLE_TILE = TILES
KT = D_MODEL // P
CHUNK = 512
CHUNKS = [(c * CHUNK, CHUNK) for c in range(SEQ // CHUNK)] + [(SEQ, NSAMP)]
NC = len(CHUNKS)

COL_Q, COL_K, COL_V, COL_O = 0, D_M, 2 * D_M, 3 * D_M
COL_GATES = 4 * D_M
COL_QA = COL_GATES + 2 * H_M
COL_KA = COL_QA + D_A
PAIRS = H_A // 2
F_GATE_ROW = 32
GATE_ROWS = F_GATE_ROW + H_M
SEGMENTS = TILES + DEC_BATCH

FAR = PAST_LEN - 512
FAR_STRIDE = 16
FAR_TILES = FAR * DEC_SEQ // FAR_STRIDE // P
NEAR_TILES = (PAST_LEN - FAR) // P
CACHE_TILES = FAR_TILES + NEAR_TILES
KEYS = CACHE_TILES * P + DEC_SEQ
HT = H_A * DEC_SEQ


CONSTANTS = ("ident", "attn_bias", "sample_bias", "causal", "sample_causal", "member", "carries", "own_head")


class Program:

    def __init__(self, dram):
        (self.x_prompt, self.x_sample, self.cache_kv, self.state_C, self.state_n, self.state_m, self.state_conv,
         self.g_mix_pre, self.g_mix_post, self.g_ffn_pre, self.g_ffn_post, self.w_in, self.b_gates, self.w_conv, self.g_mh,
         self.w_out, self.w_gate, self.w_up, self.w_down) = [dram[name] for name in views()]
        (self.y_prompt, self.y_sample, self.kv_prompt, self.kv_sample, self.C_prompt, self.n_prompt, self.m_prompt,
         self.conv_prompt, self.C_sample, self.n_sample, self.m_sample,
         self.conv_sample) = [dram[name] for name in output_shapes()]
        (self.ident_dram, self.attn_bias, self.sample_bias, self.causal, self.sample_causal, self.member, self.carries,
         self.own_head) = [dram[name] for name in CONSTANTS]


class Sems:

    def __init__(self, nc):
        self._nc, self._taken = nc, []

    def new(self, *names):
        made = [self._nc.alloc_semaphore(name=n) for n in names]
        self._taken += made
        return made

    def give_back(self):
        self._nc.clear_and_free_semaphores(self._taken)
        self._nc.all_engine_barrier()
        self._taken = []


def wait_before(engine, settled, sem, value):
    value = engine.to_reg(value)
    engine.wait_ge(*settled)
    engine.wait_ge(sem, value)


def token_tiles(engine, body):
    with engine.Fori(0, TILES // 2 - 1) as pair:
        for slot in range(2):
            body(pair * 2 + slot, slot, P, pair)
    last = TILES // 2 - 1
    for slot in range(2):
        body(2 * last + slot, slot, P, last)
    body(SAMPLE_TILE, 0, NSAMP, last + 1)


def product(pe, out, w_hi, w_lo, x_hi, x_lo, first, last):
    pe.matmul(out, w_hi, x_hi, start=first, stop=False)
    pe.matmul(out, w_hi, x_lo, start=False, stop=False)
    return pe.matmul(out, w_lo, x_hi, start=False, stop=last)


def stage_normalise_inputs(nc, g, sems):
    with ExitStack() as ctx:
        sb = lambda n, s, d=F32: ctx.enter_context(nc.sbuf_tensor(n, s, d))
        x = [sb(f"nx{i}", [P, D_MODEL]) for i in range(2)]
        xn = [sb(f"nxn{i}", [P, D_MODEL]) for i in range(2)]
        squares = sb("nsq", [P, D_MODEL])
        gain = sb("ngain", [P, D_MODEL])
        sumsq = [sb(f"nss{i}", [P, 1]) for i in range(2)]
        meansq = [sb(f"nms{i}", [P, 1]) for i in range(2)]
        rstd = [sb(f"nrstd{i}", [P, 1]) for i in range(2)]
        power = sb("npower", [P, 1])
        turned = [ctx.enter_context(nc.psum_tensor(f"nturned{i}", [P, KT, P], F32)) for i in range(2)]
        x_in0, x_in1, gain_in, ident_in, ss_ready, power_ready, ms_ready, rstd_ready, xn_ready, turned_ready, hi_ready, \
            turned_free, split_done = sems.new(
                "n_x_in0", "n_x_in1", "n_gain_in", "n_ident_in", "n_ss_ready", "n_power_ready", "n_ms_ready",
                "n_rstd_ready", "n_xn_ready", "n_turned_ready", "n_hi_ready", "n_turned_free", "n_split_done")
        x_in = [x_in0, x_in1]

        with nc.Block() as block:
            @block.sync
            def _(sp):
                sp.dma_start(x[0][:, :], g.x_prompt[0:P, :]).then_inc(x_in[0], 16)
                sp.dma_start(gain[:, :], g.g_mix_pre.to_broadcast([P, D_MODEL])).then_inc(gain_in, 16)
                sp.dma_start(x[1][:, :], g.x_prompt[P:2 * P, :]).then_inc(x_in[1], 16)
                sp.dma_start(g.ident[:, :], g.ident_dram).then_inc(ident_in, 16)
                with sp.Fori(1, TILES // 2) as pair:
                    for slot in range(2):
                        wait_before(sp, (gain_in, 16), xn_ready, pair * 2 + slot - 1)
                        sp.dma_start(x[slot][:, :], g.x_prompt[ds((pair * 2 + slot) * P, P), :]).then_inc(x_in[slot], 16)
                sp.wait_ge(xn_ready, TILES - 1)
                sp.dma_start(x[0][0:NSAMP, :], g.x_sample).then_inc(x_in[0], 16)

            @block.scalar
            def _(act):
                def sum_squares(t, s, n, nth):
                    act.wait_ge(x_in[s], nth * 16 + 16)
                    act.wait_ge(ss_ready, t)
                    nc.scalar.activation(squares[0:n, :], x[s][0:n, :], ACT.Square,
                                         accum_out=sumsq[s][0:n, :]).then_inc(ss_ready, 1)

                def keep_high(t, s, n):
                    act.wait_ge(turned_ready, t + 1)
                    nc.scalar.activation(g.act_hi[:, :, ds(t * P, n)], turned[s][:, :, 0:n],
                                         ACT.Copy).then_inc(hi_ready, 1)

                sum_squares(0, 0, P, 0)
                with act.Fori(0, TILES // 2 - 1) as pair:
                    for s in range(2):
                        sum_squares(pair * 2 + s + 1, 1 - s, P, pair + s)
                        keep_high(pair * 2 + s, s, P)
                last = TILES // 2 - 1
                sum_squares(TILES - 1, 1, P, last)
                keep_high(TILES - 2, 0, P)
                sum_squares(TILES, 0, NSAMP, last + 1)
                keep_high(TILES - 1, 1, P)
                keep_high(TILES, 0, NSAMP)

            @block.gpsimd
            def _(pool):
                nc.gpsimd.memset(power[:, :], -0.5).then_inc(power_ready, 1)
                pool.wait_ge(power_ready, 1)

                def inverse_rms(t, s, n, nth):
                    wait_before(pool, (power_ready, 1), ss_ready, t + 1)
                    nc.gpsimd.tensor_scalar(meansq[s][0:n, :], sumsq[s][0:n, :], 1.0 / D_MODEL, EPS, ALU.mult,
                                            ALU.add).then_inc(ms_ready, 1)
                    pool.wait_ge(ms_ready, t + 1)
                    nc.gpsimd.tensor_tensor(rstd[s][0:n, :], meansq[s][0:n, :], power[0:n, :],
                                            ALU.pow).then_inc(rstd_ready, 1)
                token_tiles(pool, inverse_rms)

            @block.vector
            def _(dve):
                dve.wait_ge(gain_in, 16)

                def scale(t, s, n, nth):
                    dve.wait_ge(rstd_ready, t + 1)
                    nc.vector.scalar_tensor_tensor(xn[s][0:n, :], x[s][0:n, :], rstd[s][0:n, 0:1], gain[0:n, :],
                                                   ALU.mult, ALU.mult).then_inc(xn_ready, 1)

                def keep_low(t, s, n):
                    dve.wait_ge(hi_ready, t + 1)
                    cols = ds(t * P, n)
                    nc.vector.tensor_tensor(g.act_lo[:, :, cols], turned[s][:, :, 0:n], g.act_hi[:, :, cols],
                                            ALU.subtract).then_inc(turned_free, 1)

                scale(0, 0, P, 0)
                with dve.Fori(0, TILES // 2 - 1) as pair:
                    for s in range(2):
                        scale(pair * 2 + s + 1, 1 - s, P, None)
                        keep_low(pair * 2 + s, s, P)
                scale(TILES - 1, 1, P, None)
                keep_low(TILES - 2, 0, P)
                scale(TILES, 0, NSAMP, None)
                keep_low(TILES - 1, 1, P)
                keep_low(TILES, 0, NSAMP)

            @block.tensor
            def _(pe):
                pe.wait_ge(ident_in, 16)
                pe.sem_inc(turned_free, 2)

                def turn(t, s, n, nth):
                    pe.wait_ge(xn_ready, t + 1)
                    pe.wait_ge(turned_free, t + 1)
                    for k in range(KT):
                        mm = nc.tensor.transpose(turned[s][:, k, 0:n], xn[s][0:n, k * P:(k + 1) * P],
                                                 g.ident[0:n, 0:n])
                    mm.then_inc(turned_ready, 1)
                token_tiles(pe, turn)


def stage_prompt_attention(nc, g, sems):
    units, blocks = [], []
    for t in range(TILES):
        for a in range(2):
            first = len(units)
            for c in range(t // 4 + 1):
                units.append((t, a, c, min(CHUNK, (t + 1) * P - c * CHUNK)))
            blocks.append(list(range(first, len(units))))
    block_of = lambda t, a: 2 * t + a
    n_units, n_blocks = len(units), len(blocks)
    n_q, n_rows = NC, TILES + 1
    turns = [("K", 0)]
    for t in range(TILES):
        turns += [("K", t + 1)] + [("X", t - 1)] * (t > 0)
    turns += [("X", TILES - 1)]
    turn_no = {turn: n for n, turn in enumerate(turns)}
    n_turns = len(turns)
    assert n_units % 2 == 0
    half_units = n_units // 2
    turns_before = {}
    seen = 1
    for t in range(TILES):
        for a in range(2):
            seen += a == 0
            for u in blocks[block_of(t, a)]:
                turns_before[u] = seen
            seen += a == 0 and t > 0

    with ExitStack() as ctx:
        sb = lambda n, s, d=F32: ctx.enter_context(nc.sbuf_tensor(n, s, d))
        pb = lambda n, s: ctx.enter_context(nc.psum_tensor(n, s, F32))
        w_raw = [sb(f"a_w_raw{i}", [P, KT, P]) for i in range(3)]
        w_hi, w_lo = sb("a_w_hi", [P, KT, 3, P], BF16), sb("a_w_lo", [P, KT, 3, P], BF16)
        q_st = sb("a_q_st", [P, 2, NTOK], BF16)
        k_hi, k_lo = sb("a_k_hi", [P, 2, SEQ], BF16), sb("a_k_lo", [P, 2, SEQ], BF16)
        v = sb("a_v", [P, TILES, P])
        kv = [sb(f"a_kv{i}", [P, 2, P]) for i in range(2)]
        k_twice = [sb(f"a_k_twice{i}", [P, 2 * P]) for i in range(2)]
        bias = [sb(f"a_bias{i}", [P, SEQ]) for i in range(2)]
        probs = [sb(f"a_probs{i}", [P, SEQ]) for i in range(2)]
        low = [sb(f"a_low{i}", [P, TILES // 4]) for i in range(2)]
        den = [sb(f"a_den{i}", [P, 1]) for i in range(2)]
        rden = sb("a_rden", [P, 1])
        out = sb("a_out", [P, 2, HD_A])
        probs_t = [sb(f"a_probs_t{i}", [P, CHUNK]) for i in range(4)]
        ps_rows = [pb(f"a_ps_rows{i}", [P, CHUNK]) for i in range(2)]
        ps_s = [pb(f"a_ps_s{i}", [P, CHUNK]) for i in range(2)]
        ps_t = [pb(f"a_ps_t{i}", [P, CHUNK]) for i in range(2)]
        ps_o = [pb(f"a_ps_o{i}", [P, CHUNK]) for i in range(2)]
        w_in0, w_in1, w_in2, bias_in0, bias_in1, store0, store1 = sems.new(
            "a_w_in0", "a_w_in1", "a_w_in2", "a_bias_in0", "a_bias_in1", "a_store0", "a_store1")
        w_in, bias_in, store = [w_in0, w_in1, w_in2], [bias_in0, bias_in1], [store0, store1]
        (w_hi_done, w_split, q_ready, q_hi_done, q_done, rows_ready, rows_done, v_done, s_ready, s_done, exp_done,
         unit_turned, even_kept, odd_kept, turn_ready, turn_hi, turn_done, pv_done, rden_done, o_done, zeroed) = sems.new(
            "a_w_hi_done", "a_w_split", "a_q_ready", "a_q_hi_done", "a_q_done", "a_rows_ready", "a_rows_done",
            "a_v_done", "a_s_ready", "a_s_done", "a_exp_done", "a_unit_turned", "a_even_kept", "a_odd_kept", "a_turn_ready",
            "a_turn_hi", "a_turn_done", "a_pv_done", "a_rden_done", "a_o_done", "a_zeroed")
        kept = [even_kept, odd_kept]
        stores_of = [TILES // 2 + 1, TILES // 2]
        cols = [COL_QA, COL_KA, COL_KA + D_A]
        rows_of = lambda t: P if t < TILES else NSAMP

        with nc.Block() as block:
            @block.sync
            def _(sp):
                with sp.Fori(0, PAIRS) as p:
                    for a in range(2):
                        wait_before(sp, (w_split, 3), s_done, p * n_units)
                        sp.dma_start(bias[a][:, :], g.attn_bias[ds(p * 2 + a, 1), :, :].rearrange("h p c -> (h p) c"))\
                            .then_inc(bias_in[a], 16)
                    for t in range(TILES + 1):
                        s, n = t % 2, rows_of(t)
                        wait_before(sp, (rows_done, 1), rows_done, p * n_rows + t + 1)
                        dst = g.kv_prompt[t * P:(t + 1) * P, :] if t < TILES else g.kv_sample
                        dst = dst.rearrange("n (v c) -> n v c", v=2)[:, :, ds(p * P, P)]
                        sp.dma_start(dst, kv[s][0:n, :, :]).then_inc(store[s], 16)
                for s in range(2):
                    sp.wait_ge(store[s], PAIRS * stores_of[s] * 16)

            @block.gpsimd
            def _(pool):
                with pool.Fori(0, PAIRS) as p:
                    for i in range(3):
                        wait_before(pool, (w_split, 3), w_split, p * 3 + i + 1)
                        src = g.w_in[:, ds(p * P + cols[i], P)].rearrange("(k p) c -> p k c", p=P)
                        pool.dma_start(w_raw[i][:, :, :], src).then_inc(w_in[i], 16)

            @block.tensor
            def _(pe):
                with pe.Fori(0, PAIRS) as p:
                    def rows_part(t, k):
                        n = rows_of(t)
                        if k == 0:
                            pe.wait_ge(*((rows_done, p * n_rows + t - 1) if t >= 2 else (q_done, p * n_q + 4 + (t == 0))))
                        toks = slice(t * P, t * P + n)
                        mm = product(nc.tensor, ps_rows[t % 2][0:n, 0:2 * P], g.act_hi[:, k, toks], g.act_lo[:, k, toks],
                                     w_hi[:, k, 1:3, :], w_lo[:, k, 1:3, :], k == 0, k == KT - 1)
                        if k == KT - 1:
                            mm.then_inc(rows_ready, 1)

                    def start_turn(kind, i, odd_units):
                        pe.wait_ge(kept[1], p * half_units + odd_units)
                        pe.wait_ge(turn_done, p * n_turns + turn_no[kind, i])
                        return ps_t[1]

                    def odd_before(t, a):
                        return blocks[block_of(t, a)][0] // 2

                    def turn_k(t):
                        n = rows_of(t)
                        bank = start_turn("K", t, odd_before(t - 1, 0) if t else 0)
                        wait_before(pe, (w_split, 3), rows_done, p * n_rows + t + 1)
                        if t < TILES:
                            for a in range(2):
                                mm = nc.tensor.transpose(bank[:, a * P:(a + 1) * P], k_twice[t % 2][:, a * P:(a + 1) * P],
                                                         g.ident[:, :])
                        else:
                            mm = nc.tensor.transpose(bank[:, 0:n], kv[t % 2][0:n, 0, :], g.ident[0:n, 0:n])
                        mm.then_inc(turn_ready, 1)

                    def turn_out(t):
                        pe.wait_ge(o_done, p * n_blocks + 2 * t + 2)
                        bank = start_turn("X", t, odd_before(t + 1, 1) if t + 1 < TILES else half_units)
                        nc.tensor.transpose(bank[:, 0:P], out[:, :, :].rearrange("p a d -> p (a d)"),
                                            g.ident[:, :]).then_inc(turn_ready, 1)

                    def scores(u):
                        t, a, c, w = units[u]
                        if c == 0:
                            pe.wait_ge(turn_done, p * n_turns + turn_no["K", t] + 1)
                        pe.wait_ge(s_done, p * n_units + max(u - 1, 0))
                        q = q_st[:, a, t * P:(t + 1) * P]
                        keys = slice(c * CHUNK, c * CHUNK + w)
                        nc.tensor.matmul(ps_s[u % 2][:, 0:w], q, k_hi[:, a, keys], start=True, stop=False)
                        nc.tensor.matmul(ps_s[u % 2][:, 0:w], q, k_lo[:, a, keys], start=False,
                                         stop=True).then_inc(s_ready, 1)

                    def turn_probs(u):
                        t, a, c, w = units[u]
                        pe.wait_ge(exp_done, p * n_blocks + block_of(t, a) + 1)
                        pe.wait_ge(kept[u % 2], p * half_units + u // 2)
                        if u % 2:
                            pe.wait_ge(turn_done, p * n_turns + turns_before[u])
                        bank = ps_t[u % 2]
                        for i in range(w // P):
                            at = c * CHUNK + i * P
                            mm = nc.tensor.transpose(bank[:, i * P:(i + 1) * P], probs[a][:, at:at + P], g.ident[:, :])
                        mm.then_inc(unit_turned, 1)

                    def weigh_values(u):
                        t, a, c, w = units[u]
                        pe.wait_ge(kept[u % 2], p * half_units + u // 2 + 1)
                        if c == 0:
                            pe.wait_ge(v_done, p * TILES + t + 1)
                            pe.wait_ge(o_done, p * n_blocks + max(block_of(t, a) - 1, 0))
                        for i in range(w // P):
                            kt = c * 4 + i
                            mm = nc.tensor.matmul(ps_o[a][:, 0:HD_A], probs_t[u % 4][:, i * P:(i + 1) * P],
                                                  v[:, kt, a * HD_A:(a + 1) * HD_A], start=(kt == 0), stop=(kt == t),
                                                  skip_group_check=True)
                        mm.then_inc(pv_done, 1)

                    for i, (c0, n) in enumerate(CHUNKS):
                        if i == 0:
                            pe.wait_ge(w_split, 3 + p * 3 + 1)
                        pe.wait_ge(*((q_done, p * n_q + i - 1) if i >= 2 else (rows_done, p * n_rows)))
                        for k in range(KT):
                            mm = product(nc.tensor, ps_rows[i % 2][:, 0:n], w_hi[:, k, 0, :], w_lo[:, k, 0, :],
                                         g.act_hi[:, k, c0:c0 + n], g.act_lo[:, k, c0:c0 + n], k == 0, k == KT - 1)
                        mm.then_inc(q_ready, 1)
                    pe.wait_ge(w_split, 3 + p * 3 + 3)
                    for t in range(2):
                        for k in range(KT):
                            rows_part(t, k)
                    turn_k(0)
                    scores(0)
                    for j, mine in enumerate(blocks):
                        t, a = units[mine[0]][0:2]
                        ahead = blocks[j + 1] if j + 1 < n_blocks else []
                        for u in ahead[0:1]:
                            scores(u)
                        if j:
                            weigh_values(mine[0] - 1)
                        if t + 2 <= TILES:
                            for k in range(a * KT // 2, (a + 1) * KT // 2):
                                rows_part(t + 2, k)
                        if a == 0:
                            turn_k(t + 1)
                        for i, u in enumerate(mine):
                            for after in ahead[i + 1:i + 2]:
                                scores(after)
                            turn_probs(u)
                            if i:
                                weigh_values(u - 1)
                        for after in ahead[len(mine) + 1:]:
                            scores(after)
                        if a == 0 and t:
                            turn_out(t - 1)
                    weigh_values(n_units - 1)
                    turn_out(TILES - 1)

            @block.scalar
            def _(act):
                with act.Fori(0, PAIRS) as p:
                    def keep_rows(t):
                        n = rows_of(t)
                        act.wait_ge(rows_ready, p * n_rows + t + 1)
                        act.wait_ge(store[t % 2], (p * stores_of[t % 2] + t // 2) * 16)
                        act.wait_ge(v_done, p * TILES + max(t - 1, 0))
                        if t < TILES:
                            k = ps_rows[t % 2][:, 0:P].rearrange("p (a d) -> p a d", a=2)
                            for a in range(2):
                                twice = k[:, a:a + 1, :].to_broadcast([P, 2, HD_A])
                                nc.scalar.activation(k_twice[t % 2][:, a * P:(a + 1) * P]
                                                     .rearrange("p (r d) -> p r d", r=2), twice, ACT.Copy)
                        nc.scalar.activation(kv[t % 2][0:n, :, :], ps_rows[t % 2][0:n, 0:2 * P]
                                             .rearrange("p (v c) -> p v c", v=2), ACT.Copy).then_inc(rows_done, 1)

                    def turned(kind, i):
                        n = turn_no[kind, i]
                        act.wait_ge(turn_ready, p * n_turns + n + 1)
                        return ps_t[1]

                    def keep_k(t):
                        if t < TILES:
                            bank = turned("K", t)
                            nc.scalar.activation(k_hi[:, :, t * P:(t + 1) * P],
                                                 bank[:, 0:2 * P].rearrange("p (a n) -> p a n", a=2),
                                                 ACT.Copy).then_inc(turn_hi, 1)

                    def exponentials(t, a):
                        j = block_of(t, a)
                        act.wait_ge(s_done, p * n_units + blocks[j][-1] + 1)
                        act.wait_ge(o_done, p * n_blocks + max(j - 1, 0))
                        w = (t + 1) * P
                        nc.scalar.activation(probs[a][:, 0:w], probs[a][:, 0:w], ACT.Exp, bias=low[a][:, t // 4:t // 4 + 1],
                                             scale=-1.0, accum_out=den[a][:, :]).then_inc(exp_done, 1)

                    for i in range(3):
                        act.wait_ge(w_in[i], p * 16 + 16)
                        nc.scalar.activation(w_hi[:, :, i, :], w_raw[i][:, :, :], ACT.Copy).then_inc(w_hi_done, 1)
                    for i, (c0, n) in enumerate(CHUNKS):
                        act.wait_ge(q_ready, p * n_q + i + 1)
                        for a in range(2):
                            last = nc.scalar.activation(q_st[0:HD_A, a, c0:c0 + n],
                                                        ps_rows[i % 2][a * HD_A:(a + 1) * HD_A, 0:n], ACT.Copy,
                                                        scale=HD_A ** -0.5)
                        last.then_inc(q_hi_done, 1)
                    keep_rows(0)
                    keep_rows(1)
                    keep_k(0)
                    exponentials(0, 0)
                    for j, mine in enumerate(blocks):
                        t, a = units[mine[0]][0:2]
                        if a == 0:
                            keep_k(t + 1)
                        else:
                            if t:
                                bank = turned("X", t - 1)
                                nc.scalar.activation(g.mix_a_hi[:, ds(p * NTOK + (t - 1) * P, P)], bank[:, 0:P],
                                                     ACT.Copy).then_inc(turn_hi, 1)
                            if t + 2 <= TILES:
                                keep_rows(t + 2)
                        for u in mine:
                            if u % 2 == 0:
                                act.wait_ge(unit_turned, p * n_units + u + 1)
                                act.wait_ge(pv_done, p * n_units + max(u - 3, 0))
                                w = units[u][3]
                                nc.scalar.activation(probs_t[u % 4][:, 0:w], ps_t[0][:, 0:w], ACT.Copy).then_inc(even_kept, 1)
                        if j + 1 < n_blocks:
                            exponentials(*units[blocks[j + 1][0]][0:2])
                    bank = turned("X", TILES - 1)
                    nc.scalar.activation(g.mix_a_hi[:, ds(p * NTOK + (TILES - 1) * P, P)], bank[:, 0:P],
                                         ACT.Copy).then_inc(turn_hi, 1)

            @block.vector
            def _(dve):
                nc.vector.memset(g.q_pairs[:, :], 0.0).then_inc(zeroed, 1)
                dve.wait_ge(zeroed, 1)
                dve.sem_inc(w_split, 3)
                with dve.Fori(0, PAIRS) as p:
                    def keep_v(t):
                        dve.wait_ge(rows_done, p * n_rows + t + 1)
                        nc.vector.tensor_copy(v[:, t, :], kv[t % 2][:, 1, :]).then_inc(v_done, 1)

                    def turned(kind, i):
                        n = turn_no[kind, i]
                        dve.wait_ge(turn_hi, p * (n_turns - 1) + n + 1 - (n > turn_no["K", TILES]))
                        return ps_t[1]

                    def keep_k(t):
                        if t < TILES:
                            bank = turned("K", t)
                            here = slice(t * P, (t + 1) * P)
                            nc.vector.tensor_tensor(k_lo[:, :, here], bank[:, 0:2 * P].rearrange("p (a n) -> p a n", a=2),
                                                    k_hi[:, :, here], ALU.subtract).then_inc(turn_done, 1)
                        else:
                            n = turn_no["K", t]
                            dve.wait_ge(turn_ready, p * n_turns + n + 1)
                            nc.vector.tensor_copy(g.k_new[:, ds(p * NSAMP, NSAMP)],
                                                  ps_t[1][:, 0:NSAMP]).then_inc(turn_done, 1)

                    def mask_scores(u):
                        t, a, c, w = units[u]
                        if t == 0:
                            dve.wait_ge(bias_in[a], p * 16 + 16)
                        if c:
                            dve.wait_ge(s_done, p * n_units + u)
                        wait_before(dve, (bias_in[a], 16), s_ready, p * n_units + u + 1)
                        at = c * CHUNK
                        off = (TILES - 1 - t) * P + at
                        nc.vector.tensor_tensor_reduce(
                            probs[a][:, at:at + w], ps_s[u % 2][:, 0:w], bias[a][:, off:off + w], -1.0,
                            low[a][:, c - 1:c] if c else 3e38, ALU.add, ALU.min, low[a][:, c:c + 1]).then_inc(s_done, 1)

                    def keep_output(t, a):
                        j = block_of(t, a)
                        dve.wait_ge(exp_done, p * n_blocks + j + 1)
                        dve.wait_ge(o_done, p * n_blocks + j)
                        nc.vector.reciprocal(rden[:, :], den[a][:, :]).then_inc(rden_done, 1)
                        dve.wait_ge(pv_done, p * n_units + blocks[j][-1] + 1)
                        dve.wait_ge(rden_done, p * n_blocks + j + 1)
                        nc.vector.tensor_scalar(out[:, a, :], ps_o[a][:, 0:HD_A], rden[:, 0:1], None,
                                                ALU.mult).then_inc(o_done, 1)

                    for i in range(3):
                        dve.wait_ge(w_hi_done, p * 3 + i + 1)
                        nc.vector.tensor_tensor(w_lo[:, :, i, :], w_raw[i][:, :, :], w_hi[:, :, i, :],
                                                ALU.subtract).then_inc(w_split, 1)
                    for i, (c0, n) in enumerate(CHUNKS):
                        dve.wait_ge(q_hi_done, p * n_q + i + 1)
                        for a in range(2):
                            src = ps_rows[i % 2][a * HD_A:(a + 1) * HD_A, 0:n]
                            last = nc.vector.scalar_tensor_tensor(q_st[HD_A:P, a, c0:c0 + n], src, HD_A ** -0.5,
                                                                  q_st[0:HD_A, a, c0:c0 + n], ALU.mult, ALU.subtract)
                            if n < CHUNK:
                                own = g.q_pairs[a * HD_A:(a + 1) * HD_A, ds(p * (DEC_BATCH * HT + 2 * DEC_SEQ), DEC_BATCH * HT)]
                                own = own.rearrange("p (b c) -> p b c", b=DEC_BATCH)[:, :, a * DEC_SEQ:(a + 1) * DEC_SEQ]
                                last = nc.vector.tensor_scalar(own, src.rearrange("p (b t) -> p b t", b=DEC_BATCH),
                                                               HD_A ** -0.5, None, ALU.mult)
                        last.then_inc(q_done, 1)
                    keep_v(0)
                    keep_v(1)
                    keep_k(0)
                    mask_scores(0)
                    for j, mine in enumerate(blocks):
                        t, a = units[mine[0]][0:2]
                        ahead = blocks[j + 1] if j + 1 < n_blocks else []
                        for u in ahead[0:1]:
                            mask_scores(u)
                        if a and t:
                            bank = turned("X", t - 1)
                            at = ds(p * NTOK + (t - 1) * P, P)
                            nc.vector.tensor_tensor(g.mix_a_lo[:, at], bank[:, 0:P], g.mix_a_hi[:, at],
                                                    ALU.subtract).then_inc(turn_done, 1)
                        if j:
                            keep_output(*units[mine[0] - 1][0:2])
                        if a == 0:
                            keep_k(t + 1)
                        for i, u in enumerate(mine):
                            for after in ahead[i + 1:i + 2]:
                                mask_scores(after)
                            if u % 2:
                                dve.wait_ge(unit_turned, p * n_units + u + 1)
                                dve.wait_ge(pv_done, p * n_units + max(u - 3, 0))
                                w = units[u][3]
                                nc.vector.tensor_copy(probs_t[u % 4][:, 0:w], ps_t[1][:, 0:w]).then_inc(odd_kept, 1)
                        for after in ahead[len(mine) + 1:]:
                            mask_scores(after)
                        if a and t + 2 < TILES:
                            keep_v(t + 2)
                    keep_output(TILES - 1, 1)
                    bank = turned("X", TILES - 1)
                    at = ds(p * NTOK + (TILES - 1) * P, P)
                    nc.vector.tensor_tensor(g.mix_a_lo[:, at], bank[:, 0:P], g.mix_a_hi[:, at],
                                            ALU.subtract).then_inc(turn_done, 1)
def stage_sample_attention(nc, g, sems):
    NEW = CACHE_TILES * P
    BIG = CHUNK // P
    with ExitStack() as ctx:
        sb = lambda n, s, d=F32: ctx.enter_context(nc.sbuf_tensor(n, s, d))
        pb = lambda n, s: ctx.enter_context(nc.psum_tensor(n, s, F32))
        two = lambda n, s, d=F32: [sb(f"{n}{i}", s, d) for i in range(2)]
        kv = two("s_kv", [P, CACHE_TILES, 2 * D_A])
        v_new = sb("s_v_new", [DEC_SEQ, DEC_BATCH, D_A])
        bias = sb("s_bias", [HT, KEYS])
        k_t = two("s_k_t", [P, PAIRS, KEYS])
        q = two("s_q", [P, PAIRS, HT])
        probs = two("s_probs", [HT, KEYS])
        low = two("s_low", [HT, 2])
        den, rden = two("s_den", [HT, 1]), two("s_rden", [HT, 1])
        p_t = two("s_p_t", [P, (CACHE_TILES + 1) * HT])
        v_now = two("s_v_now", [DEC_SEQ, D_A])
        ps_big = [pb(f"s_ps_big{i}", [P, CHUNK]) for i in range(2)]
        ps_small = [pb(f"s_ps_small{i}", [P, CHUNK]) for i in range(2)]
        ps_s = [pb(f"s_ps_s{i}", [P, CHUNK]) for i in range(2)]
        ps_p, ps_o = pb("s_ps_p", [P, CHUNK]), pb("s_ps_o", [P, CHUNK])
        (kv_in0, kv_in1, bias_in, v_new_in, k_turned, big_done, small_done, ready, s_ready, s_done, exp_done, rden_done,
         p_done, p_turned, p_kept, o_done, o_hi, o_lo, mix_out) = sems.new(
            "s_kv_in0", "s_kv_in1", "s_bias_in", "s_v_new_in", "s_k_turned", "s_big_done", "s_small_done",
            "s_operands_ready", "s_s_ready", "s_s_done", "s_exp_done", "s_rden_done", "s_p_done", "s_p_turned", "s_p_kept",
            "s_o_done", "s_o_hi", "s_o_lo", "s_mix_out")
        kv_in = [kv_in0, kv_in1]

        def batches(engine, step):
            with engine.Fori(0, DEC_BATCH // 2 - 1) as two_:
                for slot in range(2):
                    step(two_ * 2 + slot, slot, two_, True)
            last = DEC_BATCH // 2 - 1
            step(2 * last, 0, last, True)
            step(2 * last + 1, 1, last, False)

        with nc.Block() as block:
            @block.sync
            def _(sp):
                mix = [m[:, :].rearrange("p (q n) -> p q n", q=PAIRS) for m in (g.mix_a_hi, g.mix_a_lo)]
                mix_dram = g.mix_a_dram.rearrange("i p (q n) -> i p q n", q=PAIRS)

                def load(b, slot):
                    far = g.cache_kv[ds(b, 1), 0:FAR, :].rearrange("o (f n r) c -> (o f) n r c", f=FAR_TILES, r=FAR_STRIDE)
                    for f in range(FAR_TILES):
                        sp.dma_start(kv[slot][:, f, :], far[f, :, 0:DEC_SEQ, :]).then_inc(kv_in[slot], 16)
                    near = g.cache_kv[ds(b, 1), FAR:, :].rearrange("o (t p) c -> p (o t) c", p=P)
                    sp.dma_start(kv[slot][:, FAR_TILES:, :], near).then_inc(kv_in[slot], 16)

                load(0, 0)
                sp.dma_start(bias[:, :], g.sample_bias).then_inc(bias_in, 16)
                sp.dma_start(v_new[:, :, :], g.kv_sample[:, D_A:].rearrange("(b t) c -> t b c", b=DEC_BATCH))\
                    .then_inc(v_new_in, 16)
                load(1, 1)
                for part in range(2):
                    sp.dma_start(mix_dram[part, :, :, 0:SEQ], mix[part][:, :, 0:SEQ]).then_inc(mix_out, 16)
                sp.wait_ge(bias_in, 16)
                with sp.Fori(1, DEC_BATCH // 2) as two_:
                    for slot in range(2):
                        wait_before(sp, (bias_in, 16), o_done, two_ * 2 + slot - 1)
                        load(two_ * 2 + slot, slot)
                sp.wait_ge(o_hi, 2 * PAIRS)
                sp.wait_ge(o_lo, 2 * PAIRS)
                for part in range(2):
                    sp.dma_start(mix_dram[part, :, :, SEQ:], mix[part][:, :, SEQ:]).then_inc(mix_out, 16)
                sp.wait_ge(mix_out, 64)

            @block.tensor
            def _(pe):
                pe.wait_ge(v_new_in, 16)

                def hold(sem, value):
                    wait_before(pe, (v_new_in, 16), sem, value)

                def turn_k(b, slot, nth, first=False):
                    hold(kv_in[slot], (nth + 1) * (FAR_TILES + 1) * 16)
                    for pair in range(PAIRS):
                        i, bank = b * PAIRS + pair, (slot * PAIRS + pair) % 2
                        if not (first and pair < 2):
                            hold(big_done, i - 1)
                            hold(small_done, i - 1)
                        for tile in range(CACHE_TILES):
                            to = ps_big[bank] if tile < BIG else ps_small[bank]
                            at = tile % BIG * P
                            mm = nc.tensor.transpose(to[:, at:at + P], kv[slot][:, tile, pair * P:(pair + 1) * P],
                                                     g.ident[:, :])
                        mm.then_inc(k_turned, 1)

                def attend(b, slot, nth, more):
                    hold(big_done, b * PAIRS + PAIRS)
                    hold(small_done, b * PAIRS + PAIRS)
                    hold(ready, b + 1)
                    for pair in range(PAIRS):
                        for half, (c0, c1) in enumerate(((0, CHUNK), (CHUNK, KEYS))):
                            mm = nc.tensor.matmul(ps_s[half][0:HT, 0:c1 - c0], q[slot][:, pair, :], k_t[slot][:, pair, c0:c1],
                                                  start=(pair == 0), stop=(pair == PAIRS - 1), skip_group_check=True)
                    mm.then_inc(s_ready, 1)
                    if more:
                        turn_k(b + 1, 1 - slot, nth + slot)
                    hold(p_done, b + 1)
                    for tile in range(CACHE_TILES + 1):
                        n = P if tile < CACHE_TILES else DEC_SEQ
                        mm = nc.tensor.transpose(ps_p[0:n, tile * HT:(tile + 1) * HT], probs[slot][:, tile * P:tile * P + n],
                                                 g.ident[0:HT, 0:HT])
                    mm.then_inc(p_turned, 1)
                    hold(p_kept, b + 1)
                    for pair in range(PAIRS):
                        cols = slice(pair * P, (pair + 1) * P)
                        for tile in range(CACHE_TILES + 1):
                            n = P if tile < CACHE_TILES else DEC_SEQ
                            v = kv[slot][:, tile, D_A + pair * P:D_A + (pair + 1) * P] if tile < CACHE_TILES else \
                                v_now[slot][:, cols]
                            own = slice(tile * HT + pair * 2 * DEC_SEQ, tile * HT + (pair + 1) * 2 * DEC_SEQ)
                            mm = nc.tensor.matmul(ps_o[:, ds(b * HT + pair * 2 * DEC_SEQ, 2 * DEC_SEQ)], v, p_t[slot][0:n, own],
                                                  start=(tile == 0), stop=(tile == CACHE_TILES), skip_group_check=True)
                    mm.then_inc(o_done, 1)

                turn_k(0, 0, 0, True)
                batches(pe, attend)

            @block.scalar
            def _(act):
                def keep_k(b, slot):
                    for pair in range(PAIRS):
                        act.wait_ge(k_turned, b * PAIRS + pair + 1)
                        nc.scalar.activation(k_t[slot][:, pair, 0:CHUNK], ps_big[(slot * PAIRS + pair) % 2][:, :],
                                             ACT.Copy).then_inc(big_done, 1)

                def attend(b, slot, nth, more):
                    act.wait_ge(s_done, b * 2 + 2)
                    nc.scalar.activation(probs[slot][:, :], probs[slot][:, :], ACT.Exp, bias=low[slot][:, 1:2], scale=-1.0,
                                         accum_out=den[slot][:, :]).then_inc(exp_done, 1)
                    if more:
                        keep_k(b + 1, 1 - slot)
                    act.wait_ge(p_turned, b + 1)
                    new = CACHE_TILES * HT
                    nc.scalar.activation(p_t[slot][:, 0:new], ps_p[:, 0:new], ACT.Copy)
                    nc.scalar.activation(p_t[slot][0:DEC_SEQ, new:], ps_p[0:DEC_SEQ, new:new + HT], ACT.Copy).then_inc(p_kept, 1)

                keep_k(0, 0)
                batches(act, attend)
                act.wait_ge(o_done, DEC_BATCH)
                for a in range(2):
                    rows = slice(a * HD_A, (a + 1) * HD_A)
                    out = ps_o[rows, 0:DEC_BATCH * HT].rearrange("p (b q a t) -> p a q b t", q=PAIRS, a=2, t=DEC_SEQ)
                    for pair in range(PAIRS):
                        to = g.mix_a_hi[rows, pair * NTOK + SEQ:(pair + 1) * NTOK].rearrange("p (b t) -> p b t", t=DEC_SEQ)
                        nc.scalar.activation(to, out[:, a, pair, :, :], ACT.Copy).then_inc(o_hi, 1)

            @block.vector
            def _(dve):
                def prepare(b, slot):
                    for pair in range(PAIRS):
                        dve.wait_ge(k_turned, b * PAIRS + pair + 1)
                        nc.vector.tensor_copy(k_t[slot][:, pair, CHUNK:NEW],
                                              ps_small[(slot * PAIRS + pair) % 2][:, 0:NEW - CHUNK]).then_inc(small_done, 1)
                    k_new = g.k_new[:, :].rearrange("p (q n) -> p q n", q=PAIRS)[:, :, ds(b * DEC_SEQ, DEC_SEQ)]
                    nc.vector.tensor_copy(k_t[slot][:, :, NEW:], k_new)
                    own = g.q_pairs[:, 0:PAIRS * DEC_BATCH * HT].rearrange("p (q n) -> p q n", q=PAIRS)[:, :, ds(b * HT, HT)]
                    nc.vector.tensor_copy(v_now[slot][:, :], v_new[:, ds(b, 1), :].rearrange("t o c -> t (o c)"))
                    nc.vector.tensor_copy(q[slot][:, :, :], own).then_inc(ready, 1)

                def attend(b, slot, nth, more):
                    wait_before(dve, (bias_in, 16), s_ready, b + 1)
                    for half, (c0, c1) in enumerate(((0, CHUNK), (CHUNK, KEYS))):
                        if half:
                            wait_before(dve, (bias_in, 16), s_done, b * 2 + 1)
                        nc.vector.tensor_tensor_reduce(
                            probs[slot][:, c0:c1], ps_s[half][0:HT, 0:c1 - c0], bias[:, c0:c1], -1.0,
                            low[slot][:, 0:1] if half else 3e38, ALU.add, ALU.min, low[slot][:, half:half + 1])\
                            .then_inc(s_done, 1)
                    if more:
                        prepare(b + 1, 1 - slot)
                    dve.wait_ge(exp_done, b + 1)
                    nc.vector.reciprocal(rden[slot][:, :], den[slot][:, :]).then_inc(rden_done, 1)
                    dve.wait_ge(rden_done, b + 1)
                    nc.vector.tensor_scalar(probs[slot][:, :], probs[slot][:, :], rden[slot][:, 0:1], None,
                                            ALU.mult).then_inc(p_done, 1)

                dve.wait_ge(bias_in, 16)
                dve.wait_ge(v_new_in, 16)
                prepare(0, 0)
                batches(dve, attend)
                dve.wait_ge(o_hi, 2 * PAIRS)
                for a in range(2):
                    rows = slice(a * HD_A, (a + 1) * HD_A)
                    out = ps_o[rows, 0:DEC_BATCH * HT].rearrange("p (b q a t) -> p a q b t", q=PAIRS, a=2, t=DEC_SEQ)
                    for pair in range(PAIRS):
                        here = slice(pair * NTOK + SEQ, (pair + 1) * NTOK)
                        nc.vector.tensor_tensor(g.mix_a_lo[rows, here].rearrange("p (b t) -> p b t", t=DEC_SEQ),
                                                out[:, a, pair, :, :],
                                                g.mix_a_hi[rows, here].rearrange("p (b t) -> p b t", t=DEC_SEQ),
                                                ALU.subtract).then_inc(o_lo, 1)


TAB_LOG, TAB_SIZE = 0, 4
TAB_DECAY = (TILES + 1) * TAB_SIZE
TAB_CONV = TAB_DECAY + SEGMENTS
TAB_GAIN = TAB_CONV + 2 * CONV_W
TAB_HIST = TAB_GAIN + 1
TAB_N = TAB_HIST + 2 * DEC_BATCH * HIST
TAB = TAB_N + DEC_BATCH
K_SCALE = HD_M ** -0.5
ROW_W, ROW_E, ROW_M = 32, 64, 96


def stage_gates(nc, g, sems):
    with ExitStack() as ctx:
        sb = lambda n, s, d=F32: ctx.enter_context(nc.sbuf_tensor(n, s, d))
        pb = lambda n, s: ctx.enter_context(nc.psum_tensor(n, s, F32))
        raw = sb("g_raw", [P, KT, GATE_ROWS])
        w_hi, w_lo = sb("g_w_hi", [P, KT, GATE_ROWS], BF16), sb("g_w_lo", [P, KT, GATE_ROWS], BF16)
        bias = sb("g_bias", [GATE_ROWS, 1])
        gates = sb("g_gates", [GATE_ROWS, NTOK])
        row = lambda n, w=NTOK: sb(n, [H_M, w])
        fgate, soft, lf, carries, b, m, u = [row(f"g_{n}") for n in ("fgate", "soft", "lf", "carries", "b", "m", "u")]
        log_w, log_e = row("g_log_w"), row("g_log_e")
        m_state = row("g_m_state", DEC_BATCH)
        m_in, m_end, b_end, shift, decay = [row(f"g_{n}", SEGMENTS) for n in ("m_in", "m_end", "b_end", "shift", "decay")]
        own = sb("g_own", [H_M, H_M, SEGMENTS])
        own_decay = sb("g_own_decay", [H_M, H_M, SEGMENTS])
        ones = sb("g_ones", [H_M, P])
        stack = sb("g_stack", [P, NTOK])
        conv_rows = sb("g_conv_rows", [CONV_W * 2 * H_M, P])
        gain_rows = sb("g_gain_rows", [H_M, P])
        hist_rows = sb("g_hist_rows", [DEC_BATCH * HIST, 2 * D_M])
        n_rows = sb("g_n_rows", [DEC_BATCH * H_M, HD_M])
        ps_gate = [pb(f"g_ps_gate{i}", [P, CHUNK]) for i in range(2)]
        ps_a, ps_b, ps_c = pb("g_ps_a", [P, CHUNK]), pb("g_ps_b", [P, CHUNK]), pb("g_ps_c", [P, CHUNK])
        ps_tok = [pb(f"g_ps_tok{i}", [P, CHUNK]) for i in range(2)]
        (w_dma, tab_dma, zeroed, w_ready, unit_ready, gates_done, vec, act_done, tables_ready, tok_ready, tok_done,
         decay_ready, out_dma, tables_done) = sems.new(
            "g_w_dma", "g_tab_dma", "g_zeroed", "g_w_ready", "g_unit_ready", "g_gates_done", "g_vec", "g_act_done",
            "g_tables_ready", "g_tok_ready", "g_tok_done", "g_decay_ready", "g_out_dma", "g_tables_done")
        prompt = lambda r: r[:, 0:SEQ].rearrange("h (s n) -> h s n", n=P)
        sample = lambda r: r[:, SEQ:].rearrange("h (s n) -> h s n", n=DEC_SEQ)
        tab = g.table

        with nc.Block() as block:
            @block.sync
            def _(sp):
                sp.wait_ge(zeroed, 4)
                w_cols = lambda c: g.w_in[:, c:c + H_M].rearrange("(k p) c -> p k c", p=P)
                sp.dma_start(raw[:, :, 0:H_M], w_cols(COL_GATES)).then_inc(w_dma, 16)
                sp.dma_start(raw[:, :, F_GATE_ROW:], w_cols(COL_GATES + H_M)).then_inc(w_dma, 16)
                sp.dma_start(bias[0:H_M, :], g.b_gates[0:H_M, :]).then_inc(w_dma, 16)
                sp.dma_start(bias[F_GATE_ROW:, :], g.b_gates[H_M:, :]).then_inc(w_dma, 16)
                with nc.allow_non_contiguous_dma(reason="a transposed state of 40 numbers"):
                    sp.dma_start(m_state[:, :], g.state_m.rearrange("b h -> h b")).then_inc(tab_dma, 16)
                sp.dma_start(carries[:, :], g.carries).then_inc(tab_dma, 16)
                sp.dma_start(own[:, :, :], g.own_head).then_inc(tab_dma, 16)
                conv_src = g.w_conv.rearrange("i (c p) -> i c p", p=P)
                for i in range(CONV_W):
                    sp.dma_start(conv_rows[i * 2 * H_M:(i + 1) * 2 * H_M, :], conv_src[i, :, :]).then_inc(tab_dma, 16)
                sp.dma_start(gain_rows[:, :], g.g_mh).then_inc(tab_dma, 16)
                sp.dma_start(hist_rows[:, :], g.state_conv).then_inc(tab_dma, 16)
                sp.dma_start(n_rows[:, :], g.state_n).then_inc(tab_dma, 16)
                sp.wait_ge(vec, 3 + DEC_BATCH + 8)
                sp.dma_start(g.u_dram, u[:, :]).then_inc(out_dma, 16)
                with nc.allow_non_contiguous_dma(reason="45 numbers"):
                    sp.dma_start(g.m_prompt.rearrange("o h -> h o"), m_end[:, TILES - 1:TILES]).then_inc(out_dma, 16)
                    sp.dma_start(g.m_sample.rearrange("b h -> h b"), m_end[:, TILES:]).then_inc(out_dma, 16)
                sp.wait_ge(out_dma, 48)

            @block.gpsimd
            def _(pool):
                nc.gpsimd.memset(tab[:, :, TILES * TAB_SIZE:TAB_DECAY], 0.0).then_inc(zeroed, 1)
                nc.gpsimd.memset(raw[:, :, :], 0.0).then_inc(zeroed, 1)
                nc.gpsimd.memset(bias[:, :], 0.0).then_inc(zeroed, 1)
                nc.gpsimd.memset(ones[:, :], 1.0).then_inc(zeroed, 1)
                nc.gpsimd.memset(stack[:, :], 0.0).then_inc(zeroed, 1)

            @block.tensor
            def _(pe):
                pe.wait_ge(tab_dma, 160)
                nc.tensor.transpose(ps_a[:, 0:CONV_W * 2 * H_M], conv_rows[:, :], g.ident[0:CONV_W * 2 * H_M, 0:CONV_W * 2 * H_M])
                nc.tensor.transpose(ps_a[:, 64:64 + H_M], gain_rows[:, :], g.ident[0:H_M, 0:H_M])
                nc.tensor.transpose(ps_a[:, 128:128 + DEC_BATCH * H_M], n_rows[:, :],
                                    g.ident[0:DEC_BATCH * H_M, 0:DEC_BATCH * H_M]).then_inc(tables_ready, 1)
                n = DEC_BATCH * HIST
                for c in range(2 * H_M):
                    mm = nc.tensor.transpose(ps_b[:, c * n:(c + 1) * n], hist_rows[:, c * P:(c + 1) * P], g.ident[0:n, 0:n])
                mm.then_inc(tables_ready, 1)
                pe.wait_ge(w_ready, 2)
                for i, (c0, n) in enumerate(CHUNKS):
                    if i >= 2:
                        pe.wait_ge(gates_done, i - 1)
                    for k in range(KT):
                        mm = product(nc.tensor, ps_gate[i % 2][0:GATE_ROWS, 0:n], w_hi[:, k, :], w_lo[:, k, :],
                                     g.act_hi[:, k, c0:c0 + n], g.act_lo[:, k, c0:c0 + n], k == 0, k == KT - 1)
                    mm.then_inc(unit_ready, 1)
                pe.wait_ge(zeroed, 4)
                pe.wait_ge(vec, 3 + DEC_BATCH + 12)
                nc.tensor.matmul(ps_c[:, 0:H_M * SEGMENTS], ones[:, :], own_decay[:, :, :].rearrange("k h s -> k (h s)"),
                                 start=True, stop=True).then_inc(decay_ready, 1)
                pe.wait_ge(act_done, 7)
                for t in range(TILES + 1):
                    n = P if t < TILES else NSAMP
                    if t >= 2:
                        pe.wait_ge(tok_done, t - 1)
                    nc.tensor.transpose(ps_tok[t % 2][0:n, 0:P], stack[:, t * P:t * P + n], g.ident[:, :]).then_inc(tok_ready, 1)

            @block.scalar
            def _(act):
                for i, (c0, n) in enumerate(CHUNKS):
                    act.wait_ge(unit_ready, i + 1)
                    nc.scalar.activation(gates[:, c0:c0 + n], ps_gate[i % 2][0:GATE_ROWS, 0:n], ACT.Identity,
                                         bias=bias[:, 0:1]).then_inc(gates_done, 1)
                act.wait_ge(gates_done, NC)
                nc.scalar.activation(soft[:, :], gates[F_GATE_ROW:, :], ACT.Abs).then_inc(act_done, 1)
                act.wait_ge(act_done, 1)
                nc.scalar.activation(soft[:, :], soft[:, :], ACT.Exp, scale=-1.0).then_inc(act_done, 1)
                act.wait_ge(act_done, 2)
                nc.scalar.activation(soft[:, :], soft[:, :], ACT.Ln, bias=1.0).then_inc(act_done, 1)
                act.wait_ge(vec, 3 + DEC_BATCH + 9)
                nc.scalar.activation(decay[:, :], decay[:, :], ACT.Exp).then_inc(act_done, 1)
                act.wait_ge(zeroed, 5)
                nc.scalar.activation(stack[ROW_M:ROW_M + H_M, :], m[:, :], ACT.Exp, scale=-1.0).then_inc(act_done, 1)
                act.wait_ge(vec, 3 + DEC_BATCH + 10)
                nc.scalar.activation(stack[ROW_W:ROW_W + H_M, :], log_w[:, :], ACT.Exp).then_inc(act_done, 1)
                act.wait_ge(vec, 3 + DEC_BATCH + 11)
                nc.scalar.activation(stack[ROW_E:ROW_E + H_M, :], log_e[:, :], ACT.Exp).then_inc(act_done, 1)

            @block.vector
            def _(dve):
                done = [0]

                def step(*instructions):
                    instructions[-1].then_inc(vec, 1)
                    done[0] += 1
                    dve.wait_ge(vec, done[0])

                dve.wait_ge(w_dma, 64)
                nc.vector.tensor_copy(w_hi[:, :, :], raw[:, :, :]).then_inc(w_ready, 1)
                dve.wait_ge(w_ready, 1)
                nc.vector.tensor_tensor(w_lo[:, :, :], raw[:, :, :], w_hi[:, :, :], ALU.subtract).then_inc(w_ready, 1)
                dve.wait_ge(tables_ready, 2)
                taps = ps_a[:, 0:CONV_W * 2 * H_M].rearrange("p (i j h) -> p h j i", i=CONV_W, j=2)
                conv = tab[:, :, TAB_CONV:TAB_CONV + 2 * CONV_W].rearrange("p h (j i) -> p h j i", j=2)
                nc.vector.tensor_scalar(conv[:, :, 0, :], taps[:, :, 0, :], 0.5, None, ALU.mult)
                nc.vector.tensor_scalar(conv[:, :, 1, :], taps[:, :, 1, :], 0.5 * K_SCALE, None, ALU.mult)
                nc.vector.tensor_scalar(tab[:, :, TAB_GAIN], ps_a[:, 64:64 + H_M], 0.5, None, ALU.mult)
                nc.vector.tensor_copy(tab[:, :, TAB_N:], ps_a[:, 128:128 + DEC_BATCH * H_M].rearrange("p (b h) -> p h b", h=H_M))
                hist = ps_b[:, 0:2 * H_M * DEC_BATCH * HIST].rearrange("p (j h r) -> p j h r", j=2, h=H_M)
                for j in range(2):
                    at = TAB_HIST + j * DEC_BATCH * HIST
                    last = nc.vector.tensor_copy(tab[:, :, at:at + DEC_BATCH * HIST], hist[:, j, :, :])
                last.then_inc(tables_done, 1)
                dve.wait_ge(gates_done, NC)
                step(nc.vector.tensor_copy(fgate[:, :], gates[F_GATE_ROW:, :]))
                dve.wait_ge(act_done, 3)
                step(nc.vector.scalar_tensor_tensor(lf[:, :], fgate[:, :], 0.0, soft[:, :], ALU.min, ALU.subtract))
                igate = gates[0:H_M, :]
                step(nc.vector.tensor_tensor_scan(m[:, 0:SEQ], lf[:, 0:SEQ], igate[:, 0:SEQ], 0.0, ALU.add, ALU.max))
                for s in range(DEC_BATCH):
                    here = slice(SEQ + s * DEC_SEQ, SEQ + (s + 1) * DEC_SEQ)
                    step(nc.vector.tensor_tensor_scan(m[:, here], lf[:, here], igate[:, here], m_state[:, s:s + 1],
                                                      ALU.add, ALU.max))
                step(nc.vector.tensor_tensor_scan(b[:, :], carries[:, :], lf[:, :], 0.0, ALU.mult, ALU.add))
                step(nc.vector.memset(m_in[:, 0:1], 0.0))
                nc.vector.tensor_copy(m_in[:, 1:TILES], prompt(m)[:, 0:TILES - 1, P - 1])
                step(nc.vector.tensor_copy(m_in[:, TILES:], m_state[:, :]))
                nc.vector.tensor_copy(m_end[:, 0:TILES], prompt(m)[:, :, P - 1])
                step(nc.vector.tensor_copy(m_end[:, TILES:], sample(m)[:, :, DEC_SEQ - 1]))
                nc.vector.tensor_copy(b_end[:, 0:TILES], prompt(b)[:, :, P - 1])
                step(nc.vector.tensor_copy(b_end[:, TILES:], sample(b)[:, :, DEC_SEQ - 1]))
                step(nc.vector.tensor_tensor(shift[:, :], b_end[:, :], m_end[:, :], ALU.subtract))
                dve.wait_ge(zeroed, 5)
                step(nc.vector.tensor_tensor(stack[0:H_M, :], igate, b[:, :], ALU.subtract))
                step(nc.vector.tensor_tensor(u[:, :], b[:, :], m[:, :], ALU.subtract))
                step(nc.vector.tensor_tensor(decay[:, :], shift[:, :], m_in[:, :], ALU.add))
                for row_, plus, out in ((stack, shift, log_w), (u, m_in, log_e)):
                    rows = row_[0:H_M, :]
                    nc.vector.tensor_tensor(prompt(out), prompt(rows),
                                            plus[:, 0:TILES].unsqueeze(2).to_broadcast([H_M, TILES, P]), ALU.add)
                    step(nc.vector.tensor_tensor(sample(out), sample(rows),
                                                 plus[:, TILES:].unsqueeze(2).to_broadcast([H_M, DEC_BATCH, DEC_SEQ]), ALU.add))
                dve.wait_ge(act_done, 4)
                step(nc.vector.tensor_tensor(own_decay[:, :, :], own[:, :, :],
                                             decay[:, :].unsqueeze(1).to_broadcast([H_M, H_M, SEGMENTS]), ALU.mult))
                dve.wait_ge(decay_ready, 1)
                nc.vector.tensor_copy(tab[:, :, TAB_DECAY:TAB_DECAY + SEGMENTS],
                                      ps_c[:, 0:H_M * SEGMENTS].rearrange("p (h s) -> p h s", h=H_M))
                for t in range(TILES + 1):
                    n = P if t < TILES else NSAMP
                    dve.wait_ge(tok_ready, t + 1)
                    src = ps_tok[t % 2][0:n, 0:P].rearrange("p (q r) -> p r q", q=TAB_SIZE)[:, 0:H_M, :]
                    nc.vector.tensor_copy(tab[0:n, :, t * TAB_SIZE:(t + 1) * TAB_SIZE], src).then_inc(tok_done, 1)
def stage_mlstm(nc, g, sems):
    n_units, n_steps = 2 * NC, TILES + 1
    SAMPLE = SEQ
    V_SLOTS = 3
    with ExitStack() as ctx:
        sb = lambda n, s, d=F32: ctx.enter_context(nc.sbuf_tensor(n, s, d))
        pb = lambda n, s: ctx.enter_context(nc.psum_tensor(n, s, F32))
        two = lambda n, s, d=F32: [sb(f"{n}{i}", s, d) for i in range(2)]
        w_raw = two("m_w_raw", [P, KT, P])
        w_hi, w_lo = sb("m_w_hi", [P, KT, 4, P], BF16), sb("m_w_lo", [P, KT, 4, P], BF16)
        hd = sb("m_hd", [P, TAB])
        causal, sample_causal = sb("m_causal", [P, P]), sb("m_sample_causal", [NSAMP, NSAMP])
        member = sb("m_member", [NSAMP, DEC_BATCH])
        power = sb("m_power", [P, 1])
        no_past = sb("m_no_past", [P, HIST])
        z = two("m_z", [P, HIST + CHUNK])
        zs = sb("m_zs", [P, DEC_BATCH, HIST + DEC_SEQ])
        y, th = two("m_y", [P, CHUNK]), two("m_th", [P, CHUNK])
        last_rows = sb("m_last_rows", [P, HIST + DEC_BATCH * HIST])
        conv_out = two("m_conv_out", [HIST + DEC_BATCH * HIST, P])
        qk = two("m_qk", [P, NTOK])
        q, k = qk
        u = sb("m_u", [P, NTOK])
        v1 = sb("m_v1", [P, V_SLOTS, HD_M + 1])
        o_tanh = sb("m_o_tanh", [P, V_SLOTS, HD_M])
        state = sb("m_state", [P, HD_M + 1])
        expd, sm, kn = two("m_expd", [P, P]), two("m_sm", [P, P]), two("m_kn", [P, P])
        wv, inter, tot = two("m_wv", [P, HD_M + 1]), two("m_inter", [P, HD_M + 1]), two("m_tot", [P, HD_M + 1])
        x, hn = two("m_x", [P, HD_M]), two("m_hn", [P, HD_M])
        squares = sb("m_squares", [P, HD_M])
        den, rden, ss, msq, ms, rs, r = [two(f"m_{n}", [P, 1]) for n in ("den", "rden", "ss", "msq", "ms", "rs", "r")]
        c_state, c_turned = sb("m_c_state", [P, DEC_BATCH, HD_M]), sb("m_c_turned", [P, DEC_BATCH, HD_M])
        own_w = sb("m_own_w", [NSAMP, DEC_BATCH])
        own_wv = sb("m_own_wv", [NSAMP, DEC_BATCH, HD_M])
        inter_t = sb("m_inter_t", [P, NSAMP])
        den_all, den_own = sb("m_den_all", [NSAMP, DEC_BATCH]), sb("m_den_own", [NSAMP, 1])
        n_decayed, n_new = sb("m_n_decayed", [P, DEC_BATCH]), sb("m_n_new", [P, DEC_BATCH])
        n_out, c_out = sb("m_n_out", [DEC_BATCH, HD_M]), sb("m_c_out", [P, HD_M])
        ps_p = [pb(f"m_ps_p{i}", [P, CHUNK]) for i in range(2)]
        ps_s, ps_k, ps_i, ps_n, ps_u, ps_h = [pb(f"m_ps_{n}", [P, CHUNK]) for n in "skinuh"]

        w_in0, w_in1, u_in, const_in, c_in, conv_dma0, conv_dma1, c_store, n_store, cp_store, np_store = sems.new(
            "m_w_in0", "m_w_in1", "m_u_in", "m_const_in", "m_c_in", "m_conv_dma0", "m_conv_dma1", "m_c_store", "m_n_store",
            "m_cp_store", "m_np_store")
        w_in, conv_dma = [w_in0, w_in1], [conv_dma0, conv_dma1]
        (w_hi_done, w_split, set_up, power_ready, hd_ready, u_ready, unit_ready, unit_kept, taps_done, y_ready,
         th_ready, silu_done, last_ready, last_turned, conv_kept, rows_ready, rows_done, s_ready, kn_ready,
         in_ready, exp_done, sm_done, kn_done, wv_done, num_ready, upd_ready, state_done, inter_done, tot_done,
         den_done, rden_done, ss_done, msq_done, ms_done, rs_done, r_done, x_done, hn_done, ht_ready, mh_done,
         ml_done, ct_ready, ct_done_a, ct_done_v, it_ready, it_done, itt_ready, own_done, own_den_done,
         nt_ready, decayed, n_done, n_turned, n_kept, cs_done, fin_ready, fin_kept) = sems.new(
            "m_w_hi_done", "m_w_split", "m_set_up", "m_power_ready", "m_hd_ready", "m_u_ready", "m_unit_ready",
            "m_unit_kept", "m_taps_done", "m_y_ready", "m_th_ready", "m_silu_done", "m_last_ready",
            "m_last_turned", "m_conv_kept", "m_rows_ready", "m_rows_done", "m_s_ready", "m_kn_ready",
            "m_in_ready", "m_exp_done", "m_sm_done", "m_kn_done", "m_wv_done", "m_num_ready", "m_upd_ready",
            "m_state_done", "m_inter_done", "m_tot_done", "m_den_done", "m_rden_done", "m_ss_done",
            "m_msq_done", "m_ms_done", "m_rs_done", "m_r_done", "m_x_done", "m_hn_done", "m_ht_ready",
            "m_mh_done", "m_ml_done", "m_ct_ready", "m_ct_done_a", "m_ct_done_v", "m_it_ready", "m_it_done",
            "m_itt_ready", "m_own_done", "m_own_den_done", "m_nt_ready", "m_decayed", "m_n_done", "m_n_turned",
            "m_n_kept", "m_cs_done", "m_fin_ready", "m_fin_kept")

        def heads(engine, body):
            with engine.Fori(0, H_M - 1) as h:
                body(h, True)
            body(H_M - 1, False)

        with nc.Block() as block:
            @block.sync
            def _(sp):
                sp.dma_start(causal[:, :], g.causal).then_inc(const_in, 16)
                sp.dma_start(sample_causal[:, :], g.sample_causal).then_inc(const_in, 16)
                sp.dma_start(member[:, :], g.member).then_inc(const_in, 16)
                with sp.Fori(0, H_M) as h:
                    def weights(i, col):
                        wait_before(sp, (const_in, 48), w_split, h * 4 + i + 1)
                        sp.dma_start(w_raw[i % 2][:, :, :], g.w_in[:, ds(h * P + col, P)]
                                     .rearrange("(k p) c -> p k c", p=P)).then_inc(w_in[i % 2], 16)
                    weights(0, COL_Q)
                    weights(1, COL_K)
                    wait_before(sp, (const_in, 48), exp_done, h * n_steps)
                    sp.dma_start(u[:, :], g.u_dram[ds(h, 1), :].to_broadcast([P, NTOK])).then_inc(u_in, 16)
                    weights(2, COL_V)
                    weights(3, COL_O)
                    wait_before(sp, (const_in, 48), c_store, h * 16)
                    sp.dma_start(c_state[:, :, :], g.state_C[:, ds(h, 1), :, :].rearrange("b h v k -> v (b h) k"))\
                        .then_inc(c_in, 16)

            @block.tensor
            def _(pe):
                def hold(sem, value):
                    wait_before(pe, (const_in, 48), sem, value)

                def head(h, more):
                    def unit(i, h=h):
                        j, (c0, n) = i // NC, CHUNKS[i % NC]
                        if i % NC == 0:
                            pe.wait_ge(w_split, 2 + h * 4 + j + 1)
                        if i < 2:
                            pe.wait_ge(cs_done, h * 2 if i else h * 2 - 1) if not isinstance(h, int) or h else None
                        else:
                            pe.wait_ge(unit_kept, h * n_units + i - 1)
                        for kt in range(KT):
                            mm = product(nc.tensor, ps_p[i % 2][:, 0:n], w_hi[:, kt, j, :], w_lo[:, kt, j, :],
                                         g.act_hi[:, kt, c0:c0 + n], g.act_lo[:, kt, c0:c0 + n], kt == 0, kt == KT - 1)
                        mm.then_inc(unit_ready, 1)

                    def turn_last(j):
                        pe.wait_ge(conv_kept, h * 2 + j)
                        pe.wait_ge(n_done, h)
                        hold(last_ready, h * 2 + j + 1)
                        n = HIST + DEC_BATCH * HIST
                        nc.tensor.transpose(ps_k[0:n, 0:P], last_rows[:, :], g.ident[:, :]).then_inc(last_turned, 1)

                    def rows(t, k0, k1):
                        n = P if t < TILES else NSAMP
                        if k0 == 0:
                            if t == 0:
                                pe.wait_ge(w_split, 2 + h * 4 + 4)
                            pe.wait_ge(*((rows_done, h * n_steps + t - 1) if t >= 2 else
                                         (unit_kept, h * n_units + 9 + t)))
                        for kt in range(k0, k1):
                            mm = product(nc.tensor, ps_p[t % 2][0:n, 0:2 * P], g.act_hi[:, kt, t * P:t * P + n],
                                         g.act_lo[:, kt, t * P:t * P + n], w_hi[:, kt, 2:4, :], w_lo[:, kt, 2:4, :],
                                         kt == 0, kt == KT - 1)
                        if k1 == KT:
                            mm.then_inc(rows_ready, 1)

                    def turn_h(t):
                        n = P if t < TILES else NSAMP
                        if t == 0:
                            hold(n_kept, h)
                        hold(ml_done, h * n_steps + t)
                        hold(hn_done, h * n_steps + t + 1)
                        nc.tensor.transpose(ps_h[:, 0:n], hn[t % 2][0:n, :], g.ident[0:n, 0:n]).then_inc(ht_ready, 1)

                    for i in range(1, n_units):
                        unit(i)
                        if i == NC + 2:
                            turn_last(0)
                    rows(0, 0, KT)
                    turn_last(1)
                    base = h * n_steps
                    for t in range(TILES):
                        s, here = t % 2, slice(t * P, (t + 1) * P)
                        if here.start % CHUNK == 0:
                            pe.wait_ge(silu_done, h * n_units + NC + here.start // CHUNK + 1)
                        if t == 0:
                            pe.wait_ge(fin_kept, h)
                            pe.wait_ge(conv_kept, h * 2 + 2)
                        pe.wait_ge(sm_done, base + t)
                        nc.tensor.matmul(ps_s[:, 0:P], k[:, here], q[:, here], start=True, stop=True).then_inc(s_ready, 1)
                        pe.wait_ge(kn_done, base + t)
                        nc.tensor.transpose(ps_k[:, 0:P], k[:, here], g.ident[:, :]).then_inc(kn_ready, 1)
                        pe.wait_ge(inter_done, base + t)
                        pe.wait_ge(state_done, h * (TILES + 1) + t + 1)
                        nc.tensor.matmul(ps_i[:, 0:HD_M + 1], q[:, here], state[:, :], start=True,
                                         stop=True).then_inc(in_ready, 1)
                        rows(t + 1, 0, KT // 2)
                        pe.wait_ge(sm_done, base + t + 1)
                        pe.wait_ge(tot_done, base + t)
                        nc.tensor.matmul(ps_n[:, 0:HD_M + 1], sm[s][:, :], v1[:, t % V_SLOTS, :], start=True,
                                         stop=True).then_inc(num_ready, 1)
                        pe.wait_ge(kn_done, base + t + 1)
                        pe.wait_ge(wv_done, base + t + 1)
                        nc.tensor.matmul(ps_u[:, 0:HD_M + 1], kn[s][:, :], wv[s][:, :], start=True,
                                         stop=True).then_inc(upd_ready, 1)
                        rows(t + 1, KT // 2, KT)
                        if t:
                            turn_h(t - 1)
                    t, s = TILES, TILES % 2
                    q_s, k_s = q[:, SAMPLE:], k[:, SAMPLE:]
                    hold(silu_done, (h + 1) * n_units)
                    hold(sm_done, base + t)
                    hold(c_in, h * 16 + 16)
                    nc.tensor.matmul(ps_s[0:NSAMP, 0:NSAMP], k_s, q_s, start=True, stop=True).then_inc(s_ready, 1)
                    hold(kn_done, base + t)
                    nc.tensor.transpose(ps_k[0:NSAMP, 0:P], k_s, g.ident[:, :]).then_inc(kn_ready, 1)
                    hold(inter_done, base + t)
                    nc.tensor.matmul(ps_i[0:NSAMP, 0:DEC_BATCH], q_s, hd[:, TAB_N:], start=True, stop=True).then_inc(in_ready, 1)
                    hold(rows_done, base + t + 1)
                    for half in range(2):
                        for b in range(4):
                            mm = nc.tensor.transpose(ps_p[half][:, b * P:(b + 1) * P], c_state[:, half * 4 + b, :], g.ident[:, :])
                        mm.then_inc(ct_ready, 1)
                    hold(ct_done_a, h + 1)
                    hold(ct_done_v, h + 1)
                    hold(kn_done, base + t + 1)
                    hold(own_done, h + 1)
                    nc.tensor.matmul(ps_k[:, 0:DEC_BATCH], kn[s][0:NSAMP, :], own_w[:, :], start=True, stop=True).then_inc(nt_ready, 1)
                    for b in range(DEC_BATCH):
                        mm = nc.tensor.matmul(ps_p[b // 4][:, b % 4 * P:(b % 4 + 1) * P], own_wv[:, b, :], kn[s][0:NSAMP, :],
                                              start=True, stop=True)
                    mm.then_inc(upd_ready, 1)
                    hold(state_done, h * (TILES + 1) + TILES + 1)
                    for b in range(DEC_BATCH):
                        at = b * DEC_SEQ
                        mm = nc.tensor.matmul(ps_u[:, at:at + DEC_SEQ], c_turned[:, b, :], q_s[:, at:at + DEC_SEQ], start=True,
                                              stop=True)
                    mm.then_inc(it_ready, 1)
                    turn_h(TILES - 1)
                    hold(sm_done, base + t + 1)
                    hold(tot_done, base + t)
                    nc.tensor.matmul(ps_n[0:NSAMP, 0:HD_M + 1], sm[s][0:NSAMP, 0:NSAMP], v1[0:NSAMP, t % V_SLOTS, :], start=True,
                                     stop=True).then_inc(num_ready, 1)
                    hold(own_den_done, h * 2 + 1)
                    hold(it_done, h + 1)
                    nc.tensor.transpose(ps_i[0:NSAMP, P:2 * P], inter_t[:, :], g.ident[:, :]).then_inc(itt_ready, 1)
                    nc.tensor.transpose(ps_s[:, 0:P], state[:, 0:HD_M], g.ident[:, :]).then_inc(fin_ready, 1)
                    if more:
                        unit(0, h + 1)
                    turn_h(TILES)
                    hold(ml_done, base + t + 1)
                    hold(n_done, h + 1)
                    nc.tensor.transpose(ps_h[0:DEC_BATCH, 0:P], n_new[:, :], g.ident[:, :]).then_inc(n_turned, 1)

                pe.wait_ge(w_split, 2 + 1)
                for kt in range(KT):
                    mm = product(nc.tensor, ps_p[0][:, :], w_hi[:, kt, 0, :], w_lo[:, kt, 0, :], g.act_hi[:, kt, 0:CHUNK],
                                 g.act_lo[:, kt, 0:CHUNK], kt == 0, kt == KT - 1)
                mm.then_inc(unit_ready, 1)
                heads(pe, head)

            @block.scalar
            def _(act):
                def split(h, i):
                    act.wait_ge(w_in[i % 2], (h * 2 + i // 2 + 1) * 16)
                    nc.scalar.activation(w_hi[:, :, i, :], w_raw[i % 2][:, :, :], ACT.Copy).then_inc(w_hi_done, 1)

                def head(h, more):
                    base = h * n_steps

                    def keep_unit(i):
                        j, c = i // NC, i % NC
                        act.wait_ge(unit_ready, h * n_units + i + 1)
                        act.wait_ge(y_ready, h * n_units + max(i - 1, 0))
                        if c == NC - 1:
                            nc.scalar.activation(zs[:, :, HIST:], ps_p[i % 2][:, 0:NSAMP]
                                                 .rearrange("p (b t) -> p b t", b=DEC_BATCH), ACT.Copy).then_inc(unit_kept, 1)
                            return
                        if c == 0:
                            nc.scalar.activation(z[0][:, 0:HIST], no_past[:, :], ACT.Copy)
                        else:
                            act.wait_ge(unit_kept, h * n_units + i)
                            nc.scalar.activation(z[c % 2][:, 0:HIST], z[1 - c % 2][:, CHUNK:], ACT.Copy)
                        nc.scalar.activation(z[c % 2][:, HIST:], ps_p[i % 2][:, :], ACT.Copy).then_inc(unit_kept, 1)

                    def tanh_unit(i):
                        j, n = i // NC, CHUNKS[i % NC][1]
                        act.wait_ge(y_ready, h * n_units + i + 1)
                        act.wait_ge(silu_done, h * n_units + max(i - 1, 0))
                        nc.scalar.activation(th[i % 2][:, 0:n], y[i % 2][:, 0:n], ACT.Tanh,
                                             scale=1.0 if j == 0 else 1.0 / K_SCALE).then_inc(th_ready, 1)

                    def keep_last(j):
                        act.wait_ge(last_turned, h * 2 + j + 1)
                        act.wait_ge(conv_dma[j], h * 32)
                        n = HIST + DEC_BATCH * HIST
                        nc.scalar.activation(conv_out[j][:, :], ps_k[0:n, 0:P], ACT.Copy).then_inc(conv_kept, 1)

                    def keep_rows(t):
                        n = P if t < TILES else NSAMP
                        act.wait_ge(rows_ready, base + t + 1)
                        act.wait_ge(hn_done, base + max(t - V_SLOTS + 1, 0))
                        nc.scalar.activation(v1[0:n, t % V_SLOTS, 0:HD_M], ps_p[t % 2][0:n, 0:P], ACT.Copy)
                        nc.scalar.activation(o_tanh[0:n, t % V_SLOTS, :], ps_p[t % 2][0:n, P:2 * P], ACT.Tanh,
                                             scale=0.5).then_inc(rows_done, 1)

                    def exponential(t):
                        n = P if t < TILES else NSAMP
                        act.wait_ge(u_ready, h + 1)
                        act.wait_ge(sm_done, base + max(t - 1, 0))
                        nc.scalar.activation(expd[t % 2][0:n, 0:n], u[0:n, t * P:t * P + n], ACT.Exp,
                                             bias=hd[0:n, t * TAB_SIZE:t * TAB_SIZE + 1]).then_inc(exp_done, 1)

                    def scale_inter(t):
                        n = P if t < TILES else NSAMP
                        width = HD_M + 1 if t < TILES else HD_M
                        at = 0 if t < TILES else P
                        act.wait_ge(*((in_ready, base + t + 1) if t < TILES else (itt_ready, h + 1)))
                        act.wait_ge(tot_done, base + max(t - 1, 0))
                        col = t * TAB_SIZE + 2
                        nc.scalar.activation(inter[t % 2][0:n, 0:width], ps_i[0:n, at:at + width], ACT.Copy,
                                             scale=hd[0:n, col:col + 1]).then_inc(inter_done, 1)

                    def sum_squares(t):
                        n = P if t < TILES else NSAMP
                        act.wait_ge(tot_done, base + t + 1)
                        act.wait_ge(msq_done, base + max(t - 1, 0))
                        act.wait_ge(ss_done, base + t)
                        nc.scalar.activation(squares[0:n, :], tot[t % 2][0:n, 0:HD_M], ACT.Square,
                                             accum_out=ss[t % 2][0:n, :]).then_inc(ss_done, 1)

                    def normalise(t):
                        n = P if t < TILES else NSAMP
                        act.wait_ge(r_done, base + t + 1)
                        act.wait_ge(hn_done, base + max(t - 1, 0))
                        nc.scalar.activation(x[t % 2][0:n, :], tot[t % 2][0:n, 0:HD_M], ACT.Copy,
                                             scale=r[t % 2][0:n, 0:1]).then_inc(x_done, 1)

                    def keep_h(t):
                        n = P if t < TILES else NSAMP
                        act.wait_ge(ht_ready, base + t + 1)
                        nc.scalar.activation(g.mix_m_hi[:, ds(h * NTOK + t * P, n)], ps_h[:, 0:n], ACT.Copy,
                                             scale=hd[:, TAB_GAIN:TAB_GAIN + 1]).then_inc(mh_done, 1)

                    for i in range(n_units):
                        keep_unit(i)
                        if i:
                            tanh_unit(i - 1)
                        if i in (2, 4):
                            split(h, i // 2 + 1)
                        if i == NC + 3:
                            keep_last(0)
                    tanh_unit(n_units - 1)
                    act.wait_ge(set_up, 2)
                    act.wait_ge(hd_ready, h + 1)
                    keep_rows(0)
                    keep_last(1)
                    for t in range(TILES):
                        exponential(t)
                        scale_inter(t)
                        if t:
                            normalise(t - 1)
                        keep_rows(t + 1)
                        sum_squares(t)
                        if t:
                            keep_h(t - 1)
                        if more and t in (8, 10):
                            split(h + 1, t // 2 - 4)
                    t = TILES
                    exponential(t)
                    normalise(t - 1)
                    act.wait_ge(ct_ready, h * 2 + 1)
                    nc.scalar.activation(c_turned[:, 0:4, :], ps_p[0][:, :].rearrange("p (b k) -> p b k", b=4),
                                         ACT.Copy).then_inc(ct_done_a, 1)
                    keep_h(t - 1)
                    act.wait_ge(it_ready, h + 1)
                    nc.scalar.activation(inter_t[:, :], ps_u[:, 0:NSAMP], ACT.Copy).then_inc(it_done, 1)
                    scale_inter(t)
                    sum_squares(t)
                    act.wait_ge(fin_ready, h + 1)
                    act.wait_ge(cp_store, h * 16)
                    nc.scalar.activation(c_out[:, :], ps_s[:, 0:P], ACT.Copy).then_inc(fin_kept, 1)
                    normalise(t)
                    keep_h(t)
                    act.wait_ge(n_turned, h + 1)
                    act.wait_ge(n_store, h * 16)
                    nc.scalar.activation(n_out[:, :], ps_h[0:DEC_BATCH, 0:P], ACT.Copy).then_inc(n_kept, 1)

                split(0, 0)
                split(0, 1)
                heads(act, head)

            @block.gpsimd
            def _(pool):
                nc.gpsimd.memset(power[:, :], -0.5).then_inc(power_ready, 1)
                pool.wait_ge(power_ready, 1)
                with pool.Fori(0, H_M) as h:
                    base = h * n_steps
                    for j in range(2):
                        wait_before(pool, (power_ready, 1), conv_kept, h * 2 + j + 1)
                        cols = ds(h * P + j * D_M, P)
                        pool.dma_start(g.conv_prompt[:, cols], conv_out[j][0:HIST, :]).then_inc(conv_dma[j], 16)
                        pool.dma_start(g.conv_sample[:, cols], conv_out[j][HIST:, :]).then_inc(conv_dma[j], 16)
                    for t in range(n_steps):
                        n, s = (P if t < TILES else NSAMP), t % 2
                        wait_before(pool, (power_ready, 1), rs_done, base + max(t - 1, 0))
                        wait_before(pool, (power_ready, 1), msq_done, base + t + 1)
                        nc.gpsimd.tensor_scalar(ms[s][0:n, :], msq[s][0:n, :], 1.0 / HD_M, EPS, ALU.mult,
                                                ALU.add).then_inc(ms_done, 1)
                        pool.wait_ge(ms_done, base + t + 1)
                        pool.wait_ge(r_done, base + max(t - 1, 0))
                        nc.gpsimd.tensor_tensor(rs[s][0:n, :], ms[s][0:n, :], power[0:n, :], ALU.pow).then_inc(rs_done, 1)
                        pool.wait_ge(rs_done, base + t + 1)
                        pool.wait_ge(x_done, base + max(t - 1, 0))
                        nc.gpsimd.tensor_tensor(r[s][0:n, :], rs[s][0:n, :], rden[s][0:n, :], ALU.mult).then_inc(r_done, 1)
                    wait_before(pool, (power_ready, 1), fin_kept, h + 1)
                    pool.dma_start(g.C_prompt[ds(h, 1), :, :].rearrange("h v k -> (h v) k"), c_out[:, :]).then_inc(cp_store, 16)
                    with nc.allow_non_contiguous_dma(reason="one column of 128 numbers"):
                        pool.dma_start(g.n_prompt[ds(h, 1), :].rearrange("h k -> k h"), state[:, HD_M:]).then_inc(np_store, 16)
                    wait_before(pool, (power_ready, 1), cs_done, h * 2 + 2)
                    pool.dma_start(g.C_sample[:, ds(h, 1), :, :].rearrange("b h v k -> v (b h) k"),
                                   c_state[:, :, :]).then_inc(c_store, 16)
                    wait_before(pool, (power_ready, 1), n_kept, h + 1)
                    pool.dma_start(g.n_sample[:, ds(h, 1), :].rearrange("b h k -> (b h) k"), n_out[:, :]).then_inc(n_store, 16)
                for sem, n in ((cp_store, 1), (np_store, 1), (n_store, 1), (c_store, 1), (conv_dma0, 2), (conv_dma1, 2)):
                    pool.wait_ge(sem, H_M * n * 16)

            @block.vector
            def _(dve):
                nc.vector.memset(no_past[:, :], 0.0)
                nc.vector.memset(v1[:, :, HD_M:], 1.0).then_inc(set_up, 1)
                nc.vector.memset(last_rows[:, :], 0.0).then_inc(set_up, 1)
                dve.wait_ge(const_in, 48)
                dve.wait_ge(set_up, 2)
                dve.sem_inc(w_split, 2)

                def split(h, i):
                    dve.wait_ge(w_hi_done, h * 4 + i + 1)
                    nc.vector.tensor_tensor(w_lo[:, :, i, :], w_raw[i % 2][:, :, :], w_hi[:, :, i, :],
                                            ALU.subtract).then_inc(w_split, 1)

                def head(h, more):
                    base = h * n_steps

                    def convolve(i):
                        j, c = i // NC, i % NC
                        (c0, n), at = CHUNKS[c], h * n_units + i
                        dve.wait_ge(unit_kept, at + 1)
                        dve.wait_ge(silu_done, h * n_units + max(i - 1, 0))
                        out = y[i % 2][:, 0:n]
                        if c == NC - 1:
                            dve.wait_ge(last_turned, h * 2 + j)
                            col = TAB_HIST + j * DEC_BATCH * HIST
                            nc.vector.tensor_copy(zs[:, :, 0:HIST], hd[:, col:col + DEC_BATCH * HIST]
                                                  .rearrange("p (b r) -> p b r", b=DEC_BATCH)).then_inc(taps_done, 1)
                            nc.vector.tensor_copy(last_rows[:, 0:HIST], z[(NC - 2) % 2][:, CHUNK:])
                            nc.vector.tensor_copy(last_rows[:, HIST:].rearrange("p (b r) -> p b r", b=DEC_BATCH),
                                                  zs[:, :, DEC_SEQ:]).then_inc(last_ready, 1)
                            out = out.rearrange("p (b t) -> p b t", b=DEC_BATCH)
                        taps_at = h * (n_units * HIST + 2) + i * HIST + j + (c == NC - 1)
                        if c == NC - 1:
                            dve.wait_ge(taps_done, taps_at)
                        for tap in range(CONV_W):
                            src = z[c % 2][:, tap:tap + n] if c < NC - 1 else zs[:, :, tap:tap + DEC_SEQ]
                            w = hd[:, TAB_CONV + j * CONV_W + tap:TAB_CONV + j * CONV_W + tap + 1]
                            if tap == 0:
                                ins = nc.vector.tensor_scalar(out, src, w, None, ALU.mult)
                            else:
                                dve.wait_ge(taps_done, taps_at + tap)
                                ins = nc.vector.scalar_tensor_tensor(out, src, w, out, ALU.mult, ALU.add)
                            if tap < CONV_W - 1:
                                ins.then_inc(taps_done, 1)
                        ins.then_inc(y_ready, 1)

                    def silu(i):
                        j, (c0, n) = i // NC, CHUNKS[i % NC]
                        dve.wait_ge(th_ready, h * n_units + i + 1)
                        nc.vector.scalar_tensor_tensor(qk[j][:, c0:c0 + n], th[i % 2][:, 0:n], 1.0, y[i % 2][:, 0:n], ALU.add,
                                                       ALU.mult).then_inc(silu_done, 1)

                    def total(t):
                        n, s = (P if t < TILES else NSAMP), t % 2
                        dve.wait_ge(inter_done, base + t + 1)
                        dve.wait_ge(num_ready, base + t + 1)
                        dve.wait_ge(x_done, base + max(t - 1, 0))
                        nc.vector.tensor_tensor(tot[s][0:n, :], ps_n[0:n, 0:HD_M + 1], inter[s][0:n, :],
                                                ALU.add).then_inc(tot_done, 1)
                        dve.wait_ge(tot_done, base + t + 1)
                        dve.wait_ge(rden_done, base + max(t - 1, 0))
                        col = t * TAB_SIZE + 3
                        nc.vector.scalar_tensor_tensor(den[s][0:n, :], tot[s][0:n, HD_M:], -1.0, hd[0:n, col:col + 1],
                                                       ALU.mult, ALU.max).then_inc(den_done, 1)
                        dve.wait_ge(den_done, (base + t) * 2 + 1)
                        nc.vector.tensor_tensor(den[s][0:n, :], den[s][0:n, :], tot[s][0:n, HD_M:],
                                                ALU.max).then_inc(den_done, 1)
                        dve.wait_ge(den_done, (base + t) * 2 + 2)
                        dve.wait_ge(r_done, base + max(t - 1, 0))
                        nc.vector.reciprocal(rden[s][0:n, :], den[s][0:n, :]).then_inc(rden_done, 1)

                    def mean_square(t):
                        n, s = (P if t < TILES else NSAMP), t % 2
                        dve.wait_ge(rden_done, base + t + 1)
                        dve.wait_ge(ss_done, base + t + 1)
                        dve.wait_ge(ms_done, base + max(t - 1, 0))
                        nc.vector.scalar_tensor_tensor(msq[s][0:n, :], ss[s][0:n, :], rden[s][0:n, 0:1], rden[s][0:n, :],
                                                       ALU.mult, ALU.mult).then_inc(msq_done, 1)

                    def gate_output(t):
                        n, s = (P if t < TILES else NSAMP), t % 2
                        dve.wait_ge(x_done, base + t + 1)
                        dve.wait_ge(ht_ready, base + max(t - 1, 0))
                        dve.wait_ge(rows_done, base + t + 1)
                        nc.vector.scalar_tensor_tensor(hn[s][0:n, :], o_tanh[0:n, t % V_SLOTS, :], 1.0, x[s][0:n, :], ALU.add,
                                                       ALU.mult).then_inc(hn_done, 1)

                    def keep_low(t):
                        n = P if t < TILES else NSAMP
                        dve.wait_ge(mh_done, base + t + 1)
                        at = ds(h * NTOK + t * P, n)
                        nc.vector.scalar_tensor_tensor(g.mix_m_lo[:, at], ps_h[:, 0:n], hd[:, TAB_GAIN:TAB_GAIN + 1],
                                                       g.mix_m_hi[:, at], ALU.mult, ALU.subtract).then_inc(ml_done, 1)

                    def weigh(t):
                        n, s = (P if t < TILES else NSAMP), t % 2
                        dve.wait_ge(s_ready, base + t + 1)
                        dve.wait_ge(exp_done, base + t + 1)
                        dve.wait_ge(num_ready, base + max(t - 1, 0))
                        nc.vector.tensor_tensor(sm[s][0:n, 0:n], ps_s[0:n, 0:n], expd[s][0:n, 0:n], ALU.mult).then_inc(sm_done, 1)
                        dve.wait_ge(kn_ready, base + t + 1)
                        dve.wait_ge(upd_ready, base + max(t - 1, 0))
                        nc.vector.tensor_copy(kn[s][0:n, :], ps_k[0:n, 0:P]).then_inc(kn_done, 1)

                    dve.wait_ge(ml_done, base)
                    dve.wait_ge(cs_done, h * 2)
                    dve.wait_ge(n_kept, h)
                    nc.vector.tensor_copy(hd[:, :], g.table[:, ds(h, 1), :].rearrange("p h c -> p (h c)")).then_inc(hd_ready, 1)
                    dve.wait_ge(np_store, h * 16)
                    dve.wait_ge(fin_ready, h)
                    nc.vector.memset(state[:, :], 0.0).then_inc(state_done, 1)
                    dve.wait_ge(hd_ready, h + 1)
                    for i in range(n_units):
                        convolve(i)
                        if i:
                            silu(i - 1)
                        if i in (2, 4):
                            split(h, i // 2 + 1)
                        if i == NC:
                            dve.wait_ge(u_in, h * 16 + 16)
                            up = u[:, 0:SEQ].rearrange("p (t n) -> p t n", n=P)
                            nc.vector.tensor_tensor(up, up, causal[:, :].unsqueeze(1).to_broadcast([P, TILES, P]), ALU.add)
                            nc.vector.tensor_tensor(u[0:NSAMP, SAMPLE:], u[0:NSAMP, SAMPLE:], sample_causal[:, :],
                                                    ALU.add).then_inc(u_ready, 1)
                    silu(n_units - 1)
                    for t in range(TILES):
                        s = t % 2
                        weigh(t)
                        dve.wait_ge(rows_done, base + t + 1)
                        col = t * TAB_SIZE + 1
                        nc.vector.tensor_scalar(wv[s][:, :], v1[:, t % V_SLOTS, :], hd[:, col:col + 1], None, ALU.mult).then_inc(wv_done, 1)
                        if t:
                            gate_output(t - 1)
                        dve.wait_ge(upd_ready, base + t + 1)
                        dve.wait_ge(in_ready, base + t + 1)
                        dve.wait_ge(state_done, h * (TILES + 1) + t + 1)
                        nc.vector.scalar_tensor_tensor(state[:, :], state[:, :], hd[:, TAB_DECAY + t:TAB_DECAY + t + 1],
                                                       ps_u[:, 0:HD_M + 1], ALU.mult, ALU.add).then_inc(state_done, 1)
                        total(t)
                        mean_square(t)
                        if t:
                            keep_low(t - 1)
                        if more and t in (8, 10):
                            split(h + 1, t // 2 - 4)
                    t, s = TILES, TILES % 2
                    weigh(t)
                    gate_output(t - 1)
                    dve.wait_ge(ct_ready, h * 2 + 2)
                    nc.vector.tensor_copy(c_turned[:, 4:, :], ps_p[1][:, :].rearrange("p (b k) -> p b k", b=4)).then_inc(ct_done_v, 1)
                    dve.wait_ge(rows_done, base + t + 1)
                    col = t * TAB_SIZE + 1
                    nc.vector.tensor_scalar(own_w[:, :], member[:, :], hd[0:NSAMP, col:col + 1], None, ALU.mult).then_inc(wv_done, 1)
                    dve.wait_ge(wv_done, base + t + 1)
                    nc.vector.tensor_tensor(own_wv[:, :, :], v1[0:NSAMP, t % V_SLOTS:t % V_SLOTS + 1, 0:HD_M].to_broadcast([NSAMP, DEC_BATCH, HD_M]),
                                            own_w[:, :].unsqueeze(2).to_broadcast([NSAMP, DEC_BATCH, HD_M]),
                                            ALU.mult).then_inc(own_done, 1)
                    dve.wait_ge(in_ready, base + t + 1)
                    nc.vector.tensor_tensor_reduce(den_all[:, :], ps_i[0:NSAMP, 0:DEC_BATCH], member[:, :], 1.0, 0.0, ALU.mult,
                                                   ALU.add, den_own[:, :]).then_inc(own_den_done, 1)
                    dve.wait_ge(own_den_done, h * 2 + 1)
                    nc.vector.tensor_scalar(inter[s][0:NSAMP, HD_M:], den_own[:, :], hd[0:NSAMP, col + 1:col + 2], None,
                                            ALU.mult).then_inc(own_den_done, 1)
                    nc.vector.tensor_tensor(n_decayed[:, :], hd[:, TAB_N:], hd[:, TAB_DECAY + TILES:TAB_DECAY + SEGMENTS],
                                            ALU.mult).then_inc(decayed, 1)
                    dve.wait_ge(decayed, h + 1)
                    dve.wait_ge(nt_ready, h + 1)
                    nc.vector.tensor_tensor(n_new[:, :], ps_k[:, 0:DEC_BATCH], n_decayed[:, :], ALU.add).then_inc(n_done, 1)
                    dve.wait_ge(upd_ready, base + t + 1)
                    for b in range(DEC_BATCH):
                        at = TAB_DECAY + TILES + b
                        last = nc.vector.scalar_tensor_tensor(c_state[:, b, :], c_state[:, b, :], hd[:, at:at + 1],
                                                              ps_p[b // 4][:, b % 4 * P:(b % 4 + 1) * P], ALU.mult, ALU.add)
                        if b % 4 == 3:
                            last.then_inc(cs_done, 1)
                    keep_low(t - 1)
                    dve.wait_ge(own_den_done, h * 2 + 2)
                    total(t)
                    mean_square(t)
                    gate_output(t)
                    keep_low(t)

                split(0, 0)
                split(0, 1)
                heads(dve, head)


def token_tiles_in_turn(engine, body):
    for slot in range(2):
        body(slot, slot, P, 0, slot == 0)
    with engine.Fori(1, TILES // 2) as pair:
        for slot in range(2):
            body(pair * 2 + slot, slot, P, pair, False)
    body(SAMPLE_TILE, 0, NSAMP, TILES // 2, False)


def token_rows(prompt, sample, t, n):
    return prompt[ds(t * P, P), :] if n == P else sample


def stage_mix_out(nc, g, sems):
    HALVES = D_MODEL // CHUNK
    with ExitStack() as ctx:
        sb = lambda n, s, d=F32: ctx.enter_context(nc.sbuf_tensor(n, s, d))
        two = lambda n, s, d=F32: [sb(f"{n}{i}", s, d) for i in range(2)]
        mix_a = [sb("o_mix_a_hi", [P, PAIRS * NTOK], BF16), sb("o_mix_a_lo", [P, PAIRS * NTOK], BF16)]
        w_hi, w_lo = sb("o_w_hi", [P, KT, D_MODEL], BF16), sb("o_w_lo", [P, KT, D_MODEL], BF16)
        gain_post, gain_pre = sb("o_gain_post", [P, D_MODEL]), sb("o_gain_pre", [P, D_MODEL])
        x, x1, xn = two("o_x", [P, D_MODEL]), two("o_x1", [P, D_MODEL]), two("o_xn", [P, D_MODEL])
        raw = xn
        power = sb("o_power", [P, 1])
        ss_y, ms_y, rstd_y, ss_x, ms_x, rstd_x = [two(f"o_{n}", [P, 1]) for n in
                                                  ("ss_y", "ms_y", "rstd_y", "ss_x", "ms_x", "rstd_x")]
        ps_y = [ctx.enter_context(nc.psum_tensor(f"o_ps_y{i}", [P, D_MODEL], F32)) for i in range(2)]
        turned = [ctx.enter_context(nc.psum_tensor(f"o_turned{i}", [P, KT, P], F32)) for i in range(2)]
        (x_in0, x_in1, raw_in0, raw_in1, mix_in, gain_in, store0, store1, w_hi_done, w_split, power_ready, y_ready, y_free,
         ss_y_done, ms_y_done, rstd_y_done, scaled, x1_done, ss_x_done, ms_x_done, rstd_x_done, xn_done, turned_ready,
         hi_done, turned_free) = sems.new(
            "o_x_in0", "o_x_in1", "o_raw_in0", "o_raw_in1", "o_mix_in", "o_gain_in", "o_store0", "o_store1", "o_w_hi_done",
            "o_w_split", "o_power_ready", "o_y_ready", "o_y_free", "o_ss_y_done", "o_ms_y_done", "o_rstd_y_done",
            "o_scaled", "o_x1_done", "o_ss_x_done", "o_ms_x_done", "o_rstd_x_done", "o_xn_done", "o_turned_ready",
            "o_hi_done", "o_turned_free")
        x_in, raw_in, store = [x_in0, x_in1], [raw_in0, raw_in1], [store0, store1]
        mix_hi = lambda k, t, n: (g.mix_m_hi[:, ds(k * NTOK + t * P, n)] if k < H_M else
                                  mix_a[0][:, ds((k - H_M) * NTOK + t * P, n)])
        mix_lo = lambda k, t, n: (g.mix_m_lo[:, ds(k * NTOK + t * P, n)] if k < H_M else
                                  mix_a[1][:, ds((k - H_M) * NTOK + t * P, n)])

        with nc.Block() as block:
            @block.sync
            def _(sp):
                for k in range(KT):
                    if k >= 2:
                        sp.wait_ge(w_split, k - 1)
                    sp.dma_start(raw[k % 2][:, :], g.w_out[k * P:(k + 1) * P, :]).then_inc(raw_in[k % 2], 16)
                    if k == 1:
                        for part in range(2):
                            sp.dma_start(mix_a[part][:, :], g.mix_a_dram[part, :, :]).then_inc(mix_in, 16)
                        sp.dma_start(x[0][:, :], g.x_prompt[0:P, :]).then_inc(x_in[0], 16)
                        sp.dma_start(x[1][:, :], g.x_prompt[P:2 * P, :]).then_inc(x_in[1], 16)
                        sp.dma_start(gain_post[:, :], g.g_mix_post.to_broadcast([P, D_MODEL])).then_inc(gain_in, 16)
                        sp.dma_start(gain_pre[:, :], g.g_ffn_pre.to_broadcast([P, D_MODEL])).then_inc(gain_in, 16)
                sp.wait_ge(gain_in, 32)

                def move(t, s, n, more):
                    wait_before(sp, (gain_in, 32), x1_done, t + 1)
                    sp.dma_start(token_rows(g.x1_dram[0:SEQ, :], g.x1_dram[SEQ:, :], t, n), x1[s][0:n, :]).then_inc(store[s], 16)
                    if more == P:
                        sp.dma_start(x[s][:, :], g.x_prompt[ds((t + 2) * P, P), :]).then_inc(x_in[s], 16)
                    elif more:
                        sp.dma_start(x[s][0:NSAMP, :], g.x_sample).then_inc(x_in[s], 16)

                with sp.Fori(0, TILES // 2 - 1) as pair:
                    for s in range(2):
                        move(pair * 2 + s, s, P, P)
                move(TILES - 2, 0, P, NSAMP)
                move(TILES - 1, 1, P, 0)
                move(TILES, 0, NSAMP, 0)
                sp.wait_ge(store[0], (TILES // 2 + 1) * 16)
                sp.wait_ge(store[1], TILES // 2 * 16)

            @block.tensor
            def _(pe):
                pe.wait_ge(mix_in, 32)
                pe.wait_ge(w_split, KT)

                def turn(t, s, n):
                    wait_before(pe, (w_split, KT), xn_done, t + 1)
                    wait_before(pe, (w_split, KT), turned_free, t + 1)
                    for k in range(KT):
                        mm = nc.tensor.transpose(turned[s][:, k, 0:n], xn[s][0:n, k * P:(k + 1) * P], g.ident[0:n, 0:n])
                    mm.then_inc(turned_ready, 1)

                def step(t, s, n, nth, first):
                    pe.wait_ge(y_free, t + 1)
                    for k in range(KT):
                        for half in range(HALVES):
                            cols = slice(half * CHUNK, (half + 1) * CHUNK)
                            mm = product(nc.tensor, ps_y[s][0:n, cols], mix_hi(k, t, n), mix_lo(k, t, n), w_hi[:, k, cols],
                                         w_lo[:, k, cols], k == 0, k == KT - 1)
                    mm.then_inc(y_ready, 1)
                    if not first:
                        turn(t - 1, 1 - s, P)
                token_tiles_in_turn(pe, step)
                turn(TILES, 0, NSAMP)

            @block.scalar
            def _(act):
                for k in range(KT):
                    act.wait_ge(raw_in[k % 2], (k // 2 + 1) * 16)
                    nc.scalar.activation(w_hi[:, k, :], raw[k % 2][:, :], ACT.Copy).then_inc(w_hi_done, 1)

                def keep_high(t, s, n):
                    act.wait_ge(turned_ready, t + 1)
                    nc.scalar.activation(g.act_hi[:, :, ds(t * P, n)], turned[s][:, :, 0:n], ACT.Copy).then_inc(hi_done, 1)

                def step(t, s, n, nth, first):
                    act.wait_ge(y_ready, t + 1)
                    act.wait_ge(store[s], nth * 16)
                    nc.scalar.activation(x1[s][0:n, :], ps_y[s][0:n, :], ACT.Square,
                                         accum_out=ss_y[s][0:n, :]).then_inc(ss_y_done, 1)
                    if not first:
                        keep_high(t - 1, 1 - s, P)
                    act.wait_ge(x1_done, t + 1)
                    nc.scalar.activation(xn[s][0:n, :], x1[s][0:n, :], ACT.Square,
                                         accum_out=ss_x[s][0:n, :]).then_inc(ss_x_done, 1)
                token_tiles_in_turn(act, step)
                keep_high(TILES, 0, NSAMP)

            @block.gpsimd
            def _(pool):
                nc.gpsimd.memset(power[:, :], -0.5).then_inc(power_ready, 1)
                pool.wait_ge(power_ready, 1)

                def step(t, s, n, nth, first):
                    for ss, ms, rstd, given, half_way, done in ((ss_y, ms_y, rstd_y, ss_y_done, ms_y_done, rstd_y_done),
                                                                (ss_x, ms_x, rstd_x, ss_x_done, ms_x_done, rstd_x_done)):
                        wait_before(pool, (power_ready, 1), given, t + 1)
                        nc.gpsimd.tensor_scalar(ms[s][0:n, :], ss[s][0:n, :], 1.0 / D_MODEL, EPS, ALU.mult,
                                                ALU.add).then_inc(half_way, 1)
                        pool.wait_ge(half_way, t + 1)
                        nc.gpsimd.tensor_tensor(rstd[s][0:n, :], ms[s][0:n, :], power[0:n, :], ALU.pow).then_inc(done, 1)
                token_tiles_in_turn(pool, step)

            @block.vector
            def _(dve):
                for k in range(KT):
                    dve.wait_ge(w_hi_done, k + 1)
                    nc.vector.tensor_tensor(w_lo[:, k, :], raw[k % 2][:, :], w_hi[:, k, :], ALU.subtract).then_inc(w_split, 1)
                dve.wait_ge(gain_in, 32)
                dve.sem_inc(y_free, 2)
                dve.sem_inc(turned_free, 2)

                def keep_low(t, s, n):
                    dve.wait_ge(hi_done, t + 1)
                    cols = ds(t * P, n)
                    nc.vector.tensor_tensor(g.act_lo[:, :, cols], turned[s][:, :, 0:n], g.act_hi[:, :, cols],
                                            ALU.subtract).then_inc(turned_free, 1)

                def step(t, s, n, nth, first):
                    dve.wait_ge(rstd_y_done, t + 1)
                    nc.vector.scalar_tensor_tensor(x1[s][0:n, :], ps_y[s][0:n, :], rstd_y[s][0:n, 0:1], gain_post[0:n, :],
                                                   ALU.mult, ALU.mult).then_inc(y_free, 1)
                    dve.wait_ge(x_in[s], (nth + 1) * 16)
                    dve.wait_ge(y_free, t + 3)
                    nc.vector.tensor_tensor(x1[s][0:n, :], x1[s][0:n, :], x[s][0:n, :], ALU.add).then_inc(x1_done, 1)
                    if not first:
                        keep_low(t - 1, 1 - s, P)
                    dve.wait_ge(rstd_x_done, t + 1)
                    nc.vector.scalar_tensor_tensor(xn[s][0:n, :], x1[s][0:n, :], rstd_x[s][0:n, 0:1], gain_pre[0:n, :],
                                                   ALU.mult, ALU.mult).then_inc(xn_done, 1)
                token_tiles_in_turn(dve, step)
                keep_low(TILES, 0, NSAMP)


HIDDEN_TILES = D_FF // P
PARTS = [4, 6, 6, 6]
PART_MAX = max(PARTS)
assert sum(PARTS) == HIDDEN_TILES and all(n % 2 == 0 for n in PARTS)


def stage_ffn(nc, g, sems):
    HALVES = D_MODEL // CHUNK
    n_down = TILES + 1
    firsts = [sum(PARTS[:i]) for i in range(len(PARTS))]
    LAST = len(PARTS) - 1
    with ExitStack() as ctx:
        sb = lambda n, s, d=F32: ctx.enter_context(nc.sbuf_tensor(n, s, d))
        two = lambda n, s, d=F32: [sb(f"{n}{i}", s, d) for i in range(2)]
        raw = [sb(f"f_raw_{n}", [P, D_MODEL]) for n in ("gate", "up", "down")]
        w_hi = [two(f"f_w_hi_{s}_", [P, KT, P], BF16) for s in range(2)]
        w_lo = [two(f"f_w_lo_{s}_", [P, KT, P], BF16) for s in range(2)]
        down_hi, down_lo = sb("f_down_hi", [P, PART_MAX, D_MODEL], BF16), sb("f_down_lo", [P, PART_MAX, D_MODEL], BF16)
        h_hi, h_lo = sb("f_h_hi", [P, PART_MAX * NTOK], BF16), sb("f_h_lo", [P, PART_MAX * NTOK], BF16)
        act_out, hidden = two("f_silu", [P, CHUNK]), two("f_hidden", [P, CHUNK])
        total, x1 = two("f_total", [P, D_MODEL]), two("f_x1", [P, D_MODEL])
        squares = sb("f_squares", [P, D_MODEL], BF16)
        gain = sb("f_gain", [P, D_MODEL])
        power = sb("f_power", [P, 1])
        ss, ms, rstd = two("f_ss", [P, 1]), two("f_ms", [P, 1]), two("f_rstd", [P, 1])
        pb = lambda n, w: ctx.enter_context(nc.psum_tensor(n, [P, w], F32))
        ps_gate, ps_up = [pb(f"f_ps_gate{i}", CHUNK) for i in range(2)], [pb(f"f_ps_up{i}", CHUNK) for i in range(2)]
        ps_y = [pb(f"f_ps_y{i}", D_MODEL) for i in range(2)]
        (raw_in0, raw_in1, raw_in2, gain_in, part_in0, part_in1, x1_in0, x1_in1, store0, store1, w_hi_done, w_split,
         down_hi_done, down_split, unit_ready, silu_done, hidden_done, h_hi_done, h_done, y_ready, total_done, power_ready,
         ss_done, ms_done, rstd_done, scaled, y_done) = sems.new(
            "f_raw_in0", "f_raw_in1", "f_raw_in2", "f_gain_in", "f_part_in0", "f_part_in1", "f_x1_in0", "f_x1_in1",
            "f_store0", "f_store1", "f_w_hi_done", "f_w_split", "f_down_hi_done", "f_down_split", "f_unit_ready",
            "f_silu_done", "f_hidden_done", "f_h_hi_done", "f_h_done", "f_y_ready", "f_total_done", "f_power_ready",
            "f_ss_done", "f_ms_done", "f_rstd_done", "f_scaled", "f_y_done")
        raw_in, part_in, x1_in, store = [raw_in0, raw_in1, raw_in2], [part_in0, part_in1], [x1_in0, x1_in1], [store0, store1]
        uses = [TILES // 2 + 1, TILES // 2]
        kt_rows = lambda raw_: raw_[:, :].rearrange("p (k c) -> p k c", k=KT)

        with nc.Block() as block:
            @block.sync
            def _(sp):
                sp.dma_start(gain[:, :], g.g_ffn_post.to_broadcast([P, D_MODEL])).then_inc(gain_in, 16)
                sp.wait_ge(gain_in, 16)

                def weights(m):
                    wait_before(sp, (gain_in, 16), w_split, m * 2 + 2)
                    for i, src in enumerate((g.w_gate, g.w_up)):
                        sp.dma_start(kt_rows(raw[i]), src[:, ds(m * P, P)].rearrange("(k p) c -> p k c", p=P))\
                            .then_inc(raw_in[i], 16)
                    wait_before(sp, (gain_in, 16), down_split, m + 1)
                    sp.dma_start(raw[2][:, :], g.w_down[ds(m * P, P), :]).then_inc(raw_in[2], 16)

                def down_loads(part, t, s, n, nth):
                    if part:
                        src = token_rows(g.y_part[0:SEQ, :], g.y_part[SEQ:, :], t, n)
                        sp.dma_start(total[s][0:n, :], src).then_inc(part_in[s], 16)
                    if part == LAST:
                        src = token_rows(g.x1_dram[0:SEQ, :], g.x1_dram[SEQ:, :], t, n)
                        sp.dma_start(x1[s][0:n, :], src).then_inc(x1_in[s], 16)

                def down_store(part, t, s, n):
                    if part < LAST:
                        wait_before(sp, (gain_in, 16), total_done, part * n_down + t + 1)
                        dst = token_rows(g.y_part[0:SEQ, :], g.y_part[SEQ:, :], t, n)
                        sp.dma_start(dst, total[s][0:n, :]).then_inc(store[s], 16)
                    else:
                        wait_before(sp, (gain_in, 16), y_done, t + 1)
                        sp.dma_start(token_rows(g.y_prompt, g.y_sample, t, n), x1[s][0:n, :]).then_inc(store[s], 16)

                weights(0)
                for part, n_tiles in enumerate(PARTS):
                    with sp.Fori(0, n_tiles - 1) as m:
                        weights(m + firsts[part] + 1)
                    if part < LAST:
                        weights(firsts[part + 1])
                    for s in range(2):
                        if part:
                            sp.wait_ge(store[0], part * uses[0] * 16)
                            sp.wait_ge(store[1], part * uses[1] * 16)
                        down_loads(part, s, s, P, 0)

                    def move(t, s, nth, more):
                        down_store(part, t, s, P)
                        if part and more:
                            wait_before(sp, (gain_in, 16), store[s], (part * uses[s] + nth + 1) * 16)
                            down_loads(part, t + 2, s, more, nth + 1)
                    with sp.Fori(0, TILES // 2 - 1) as pair:
                        for s in range(2):
                            move(pair * 2 + s, s, pair, P)
                    move(TILES - 2, 0, TILES // 2 - 1, NSAMP)
                    move(TILES - 1, 1, TILES // 2 - 1, 0)
                    down_store(part, TILES, 0, NSAMP)
                for s in range(2):
                    sp.wait_ge(store[s], len(PARTS) * uses[s] * 16)

            @block.tensor
            def _(pe):
                for part, n_tiles in enumerate(PARTS):
                    def up(m, slot):
                        pe.wait_ge(w_split, m * 2 + 4)
                        for c, (c0, n) in enumerate(CHUNKS):
                            unit = m * NC + c
                            u = (slot * NC + c) % 2
                            pe.wait_ge(hidden_done, unit + 1)
                            for i, ps in enumerate((ps_gate, ps_up)):
                                for k in range(KT):
                                    mm = product(nc.tensor, ps[u][:, 0:n], w_hi[slot][i][:, k, :], w_lo[slot][i][:, k, :],
                                                 g.act_hi[:, k, c0:c0 + n], g.act_lo[:, k, c0:c0 + n], k == 0, k == KT - 1)
                            mm.then_inc(unit_ready, 1)
                    with pe.Fori(0, n_tiles // 2) as pair:
                        for slot in range(2):
                            up(pair * 2 + (firsts[part] + slot), slot)

                    def down(t, s, n, nth):
                        if part or not isinstance(t, int) or t > 1:
                            pe.wait_ge(total_done, part * n_down + t - 1)
                        for k in range(n_tiles):
                            for half in range(HALVES):
                                cols = slice(half * CHUNK, (half + 1) * CHUNK)
                                at = ds(k * NTOK + t * P, n)
                                mm = product(nc.tensor, ps_y[s][0:n, cols], h_hi[:, at], h_lo[:, at], down_hi[:, k, cols],
                                             down_lo[:, k, cols], k == 0, k == n_tiles - 1)
                        mm.then_inc(y_ready, 1)
                    pe.wait_ge(down_split, 1 + firsts[part] + n_tiles)
                    pe.wait_ge(h_done, (firsts[part] + n_tiles) * NC)
                    down(0, 0, P, 0)
                    down(1, 1, P, 0)
                    with pe.Fori(1, TILES // 2) as pair:
                        for s in range(2):
                            down(pair * 2 + s, s, P, pair)
                    down(TILES, 0, NSAMP, TILES // 2)

            @block.scalar
            def _(act):
                def split_up(m, slot):
                    for i in range(2):
                        act.wait_ge(raw_in[i], (m + 1) * 16)
                        if not isinstance(m, int) or m > 1:
                            act.wait_ge(unit_ready, m * NC - NC)
                        nc.scalar.activation(w_hi[slot][i][:, :, :], kt_rows(raw[i]), ACT.Copy).then_inc(w_hi_done, 1)

                def split_down(m, k):
                    act.wait_ge(raw_in[2], (m + 1) * 16)
                    nc.scalar.activation(down_hi[:, ds(k, 1), :].rearrange("p o c -> p (o c)"), raw[2][:, :],
                                         ACT.Copy).then_inc(down_hi_done, 1)

                def units(m, slot, k):
                    for c, (c0, n) in enumerate(CHUNKS):
                        unit = m * NC + c
                        u = (slot * NC + c) % 2
                        act.wait_ge(unit_ready, unit + 1)
                        nc.scalar.activation(act_out[u][:, 0:n], ps_gate[u][:, 0:n], ACT.Silu).then_inc(silu_done, 1)
                        act.wait_ge(hidden_done, unit + 3)
                        nc.scalar.activation(h_hi[:, ds(k * NTOK + c0, n)], hidden[u][:, 0:n], ACT.Copy).then_inc(h_hi_done, 1)

                split_up(0, 0)
                for part, n_tiles in enumerate(PARTS):
                    first = firsts[part]
                    if part:
                        act.wait_ge(y_ready, part * n_down)

                    def tile(m, slot, k, more):
                        if more:
                            split_up(m + 1, 1 - slot)
                        split_down(m, k)
                        units(m, slot, k)
                    with act.Fori(0, n_tiles // 2 - 1) as pair:
                        for slot in range(2):
                            tile(pair * 2 + (first + slot), slot, pair * 2 + slot, True)
                    tile(first + n_tiles - 2, 0, n_tiles - 2, True)
                    tile(first + n_tiles - 1, 1, n_tiles - 1, part < LAST)
                    if part == LAST:
                        def square(t, s, n, nth, one):
                            act.wait_ge(total_done, part * n_down + t + 1)
                            act.wait_ge(ss_done, t)
                            nc.scalar.activation(squares[0:n, :], total[s][0:n, :], ACT.Square,
                                                 accum_out=ss[s][0:n, :]).then_inc(ss_done, 1)
                        token_tiles_in_turn(act, square)

            @block.gpsimd
            def _(pool):
                nc.gpsimd.memset(power[:, :], -0.5).then_inc(power_ready, 1)
                pool.wait_ge(power_ready, 1)

                def finish(t, s, n, nth, first):
                    wait_before(pool, (power_ready, 1), ss_done, t + 1)
                    nc.gpsimd.tensor_scalar(ms[s][0:n, :], ss[s][0:n, :], 1.0 / D_MODEL, EPS, ALU.mult,
                                            ALU.add).then_inc(ms_done, 1)
                    pool.wait_ge(ms_done, t + 1)
                    nc.gpsimd.tensor_tensor(rstd[s][0:n, :], ms[s][0:n, :], power[0:n, :], ALU.pow).then_inc(rstd_done, 1)
                token_tiles_in_turn(pool, finish)

            @block.vector
            def _(dve):
                def split_up(m, slot):
                    for i in range(2):
                        dve.wait_ge(w_hi_done, m * 2 + i + 1)
                        nc.vector.tensor_tensor(w_lo[slot][i][:, :, :], kt_rows(raw[i]), w_hi[slot][i][:, :, :],
                                                ALU.subtract).then_inc(w_split, 1)

                def split_down(m, k):
                    dve.wait_ge(down_hi_done, m + 1)
                    row = lambda w: w[:, ds(k, 1), :].rearrange("p o c -> p (o c)")
                    nc.vector.tensor_tensor(row(down_lo), raw[2][:, :], row(down_hi), ALU.subtract).then_inc(down_split, 1)

                def units(m, slot, k):
                    for c, (c0, n) in enumerate(CHUNKS):
                        unit = m * NC + c
                        u = (slot * NC + c) % 2
                        dve.wait_ge(silu_done, unit + 1)
                        nc.vector.tensor_tensor(hidden[u][:, 0:n], act_out[u][:, 0:n], ps_up[u][:, 0:n],
                                                ALU.mult).then_inc(hidden_done, 1)
                        dve.wait_ge(h_hi_done, unit + 1)
                        at = ds(k * NTOK + c0, n)
                        nc.vector.tensor_tensor(h_lo[:, at], hidden[u][:, 0:n], h_hi[:, at], ALU.subtract).then_inc(h_done, 1)

                dve.wait_ge(gain_in, 16)
                dve.sem_inc(w_split, 2)
                dve.sem_inc(down_split, 1)
                dve.sem_inc(hidden_done, 2)
                split_up(0, 0)
                for part, n_tiles in enumerate(PARTS):
                    first = firsts[part]

                    def tile(m, slot, k, more):
                        if more:
                            split_up(m + 1, 1 - slot)
                        split_down(m, k)
                        units(m, slot, k)
                    with dve.Fori(0, n_tiles // 2 - 1) as pair:
                        for slot in range(2):
                            tile(pair * 2 + (first + slot), slot, pair * 2 + slot, True)
                    tile(first + n_tiles - 2, 0, n_tiles - 2, True)
                    tile(first + n_tiles - 1, 1, n_tiles - 1, part < LAST)

                    def down(t, s, n, nth, one):
                        y = part * n_down + t
                        dve.wait_ge(y_ready, y + 1)
                        if part == 0:
                            dve.wait_ge(store[s], nth * 16)
                            nc.vector.tensor_copy(total[s][0:n, :], ps_y[s][0:n, :]).then_inc(total_done, 1)
                        else:
                            dve.wait_ge(part_in[s], ((part - 1) * uses[s] + nth + 1) * 16)
                            nc.vector.tensor_tensor(total[s][0:n, :], total[s][0:n, :], ps_y[s][0:n, :],
                                                    ALU.add).then_inc(total_done, 1)
                        if part == LAST:
                            dve.wait_ge(rstd_done, t + 1)
                            nc.vector.scalar_tensor_tensor(total[s][0:n, :], total[s][0:n, :], rstd[s][0:n, 0:1], gain[0:n, :],
                                                           ALU.mult, ALU.mult).then_inc(scaled, 1)
                            dve.wait_ge(scaled, t + 1)
                            dve.wait_ge(x1_in[s], (nth + 1) * 16)
                            nc.vector.tensor_tensor(x1[s][0:n, :], x1[s][0:n, :], total[s][0:n, :], ALU.add).then_inc(y_done, 1)
                    token_tiles_in_turn(dve, down)




N_IN = 4 * D_M + 2 * H_M + 3 * D_A


def views():
    return {
        "x_prompt": (SEQ, D_MODEL), "x_sample": (NSAMP, D_MODEL), "cache_kv": (DEC_BATCH, PAST_LEN, 2 * D_A),
        "state_C": (DEC_BATCH, H_M, HD_M, HD_M), "state_n": (DEC_BATCH * H_M, HD_M), "state_m": (DEC_BATCH, H_M),
        "state_conv": (DEC_BATCH * HIST, 2 * D_M), "g_mix_pre": (1, D_MODEL), "g_mix_post": (1, D_MODEL),
        "g_ffn_pre": (1, D_MODEL), "g_ffn_post": (1, D_MODEL), "w_in": (D_MODEL, N_IN), "b_gates": (2 * H_M, 1),
        "w_conv": (CONV_W, 2 * D_M), "g_mh": (H_M, HD_M), "w_out": (D_MODEL, D_MODEL), "w_gate": (D_MODEL, D_FF),
        "w_up": (D_MODEL, D_FF), "w_down": (D_FF, D_MODEL),
    }


def output_shapes():
    return {
        "y_prompt": (SEQ, D_MODEL), "y_sample": (NSAMP, D_MODEL), "kv_prompt": (SEQ, 2 * D_A),
        "kv_sample": (NSAMP, 2 * D_A), "C_prompt": (H_M, HD_M, HD_M), "n_prompt": (H_M, HD_M), "m_prompt": (1, H_M),
        "conv_prompt": (HIST, 2 * D_M), "C_sample": (DEC_BATCH, H_M, HD_M, HD_M), "n_sample": (DEC_BATCH, H_M, HD_M),
        "m_sample": (DEC_BATCH, H_M), "conv_sample": (DEC_BATCH * HIST, 2 * D_M),
    }


def returned_shapes():
    return {
        "y_prompt": (1, SEQ, D_MODEL), "y_sample": (DEC_BATCH, DEC_SEQ, D_MODEL), "kv_prompt": (1, 1, SEQ, 2, H_A, HD_A),
        "kv_sample": (1, DEC_BATCH, DEC_SEQ, 2, H_A, HD_A), "C_prompt": (1, 1, H_M, HD_M, HD_M),
        "n_prompt": (1, 1, H_M, HD_M), "m_prompt": (1, 1, H_M), "conv_prompt": (1, 1, HIST, 2 * D_M),
        "C_sample": (1, DEC_BATCH, H_M, HD_M, HD_M), "n_sample": (1, DEC_BATCH, H_M, HD_M),
        "m_sample": (1, DEC_BATCH, H_M), "conv_sample": (1, DEC_BATCH, HIST, 2 * D_M),
    }


def shape_constants():
    import numpy as np

    far_away = -1e30
    slopes = 2.0 ** (-8.0 * np.arange(1, H_A + 1) / H_A)

    def weight_log(dist):
        count = ((dist >= 0) & (dist <= 128)).astype(np.int64)
        count += (dist >= 0) & (dist <= 512) & (dist % 4 == 0)
        count += (dist >= 0) & (dist <= 2048) & (dist % 16 == 0)
        return np.where(count > 0, np.log(np.maximum(count, 1)), far_away)

    dist = np.arange(P)[:, None] + (TILES - 1) * P - np.arange(SEQ)[None, :]
    bias = np.stack([np.where(weight_log(dist) > far_away / 2, weight_log(dist) - s * dist, far_away) for s in slopes])
    far = [FAR_STRIDE * (j // DEC_SEQ) + j % DEC_SEQ for j in range(FAR_TILES * P)]
    keys = np.array(far + list(range(FAR, PAST_LEN + DEC_SEQ)))
    dist = (PAST_LEN + np.arange(DEC_SEQ))[:, None] - keys[None, :]
    w = weight_log(dist)
    sbias = np.concatenate([np.where(w > far_away / 2, w - s * dist, far_away) for s in slopes])
    causal = np.where(np.arange(P)[:, None] <= np.arange(P)[None, :], 0.0, far_away)
    a = np.arange(NSAMP)
    sees = (a[:, None] <= a[None, :]) & (a[:, None] // DEC_SEQ == a[None, :] // DEC_SEQ)
    member = (a[:, None] // DEC_SEQ == np.arange(DEC_BATCH)[None, :])
    chunk_of = np.concatenate([np.arange(SEQ) % P, a % DEC_SEQ]) != 0
    own = np.zeros((H_M, H_M, SEGMENTS))
    for h in range(H_M):
        own[h, h] = 1.0
    return {
        "ident": np.eye(P), "attn_bias": bias, "sample_bias": sbias, "causal": causal,
        "sample_causal": np.where(sees, 0.0, far_away), "member": member,
        "carries": np.broadcast_to(chunk_of, (H_M, NTOK)), "own_head": own,
    }


def build(nc, dram):
    with ExitStack() as ctx:
        sems = Sems(nc)
        g = Program(dram)
        internal = lambda name, shape, d=F32: nc.dram_tensor(name, shape, d, kind="Internal").ap()
        g.u_dram = internal("u_rows", (H_M, NTOK))
        g.mix_a_dram = internal("mix_a_rows", (2, P, PAIRS * NTOK), BF16)
        g.x1_dram, g.y_part = internal("x1_rows", (NTOK, D_MODEL)), internal("y_part_rows", (NTOK, D_MODEL))
        sb = lambda scope, n, s, d=F32: scope.enter_context(nc.sbuf_tensor(n, s, d))
        g.ident = sb(ctx, "ident", [P, P])
        g.act_hi, g.act_lo = sb(ctx, "act_hi", [P, KT, NTOK], BF16), sb(ctx, "act_lo", [P, KT, NTOK], BF16)
        stage_normalise_inputs(nc, g, sems)
        with ExitStack() as attention:
            g.mix_a_hi, g.mix_a_lo = [sb(attention, f"mix_a_{n}", [P, PAIRS * NTOK], BF16) for n in ("hi", "lo")]
            g.q_pairs = sb(attention, "q_pairs", [P, PAIRS * DEC_BATCH * HT + (PAIRS - 1) * 2 * DEC_SEQ])
            g.k_new = sb(attention, "k_new", [P, PAIRS * NSAMP])
            stage_prompt_attention(nc, g, sems)
            stage_sample_attention(nc, g, sems)
            sems.give_back()
        with ExitStack() as mix:
            g.table = sb(mix, "table", [P, H_M, TAB])
            stage_gates(nc, g, sems)
            g.mix_m_hi, g.mix_m_lo = [sb(mix, f"mix_m_{n}", [P, H_M * NTOK], BF16) for n in ("hi", "lo")]
            stage_mlstm(nc, g, sems)
            sems.give_back()
            stage_mix_out(nc, g, sems)
        stage_ffn(nc, g, sems)


def kernel(**inputs):
    import numpy as np
    import concourse.bacc as bacc
    from concourse.bass_utils import run_bass_kernel_spmd

    nc = bacc.Bacc("TRN2", target_bir_lowering=False, num_devices=1)
    arrays, dram = {}, {}
    for name, shape in views().items():
        arrays[f"in_{name}"] = np.ascontiguousarray(inputs[name]).reshape(shape)
        dram[name] = nc.dram_tensor(f"in_{name}", shape, F32, kind="ExternalInput").ap()
    for name, table in shape_constants().items():
        arrays[f"const_{name}"] = np.ascontiguousarray(table, dtype=np.float32)
        dram[name] = nc.dram_tensor(f"const_{name}", table.shape, F32, kind="ExternalInput").ap()
    for name, shape in output_shapes().items():
        dram[name] = nc.dram_tensor(f"out_{name}", shape, F32, kind="ExternalOutput").ap()
    build(nc, dram)
    got = run_bass_kernel_spmd(nc, [arrays], core_ids=[0]).results[0]
    return tuple(np.asarray(got[f"out_{name}"]).reshape(shape) for name, shape in returned_shapes().items())
```

```python
from contextlib import ExitStack

import concourse.bass as bass
from concourse import mybir

F32 = mybir.dt.float32
BF16 = mybir.dt.bfloat16
ALU = mybir.AluOpType
ACT = mybir.ActivationFunctionType
ds = bass.ds

P = 128
D_MODEL = 1024
SEQ = 2048
DEC_BATCH = 8
DEC_SEQ = 8
PAST_LEN = 1024
H_M, HD_M = 5, 128
H_A, HD_A = 6, 64
D_M = H_M * HD_M
D_A = H_A * HD_A
CONV_W = 4
HIST = CONV_W - 1
D_FF = ((8 * D_MODEL + 767) // 768) * 256
EPS = 1e-6

NSAMP = DEC_BATCH * DEC_SEQ
NTOK = SEQ + NSAMP
TILES = SEQ // P
SAMPLE_TILE = TILES
KT = D_MODEL // P
CHUNK = 512
CHUNKS = [(c * CHUNK, CHUNK) for c in range(SEQ // CHUNK)] + [(SEQ, NSAMP)]
NC = len(CHUNKS)

COL_Q, COL_K, COL_V, COL_O = 0, D_M, 2 * D_M, 3 * D_M
COL_GATES = 4 * D_M
COL_QA = COL_GATES + 2 * H_M
COL_KA = COL_QA + D_A
PAIRS = H_A // 2
F_GATE_ROW = 32
GATE_ROWS = F_GATE_ROW + H_M
SEGMENTS = TILES + DEC_BATCH

FAR = PAST_LEN - 512
FAR_STRIDE = 16
FAR_TILES = FAR * DEC_SEQ // FAR_STRIDE // P
NEAR_TILES = (PAST_LEN - FAR) // P
CACHE_TILES = FAR_TILES + NEAR_TILES
KEYS = CACHE_TILES * P + DEC_SEQ
HT = H_A * DEC_SEQ


CONSTANTS = ("ident", "attn_bias", "sample_bias", "causal", "sample_causal", "member", "carries", "own_head")


class Program:

    def __init__(self, dram):
        (self.x_prompt, self.x_sample, self.cache_kv, self.state_C, self.state_n, self.state_m, self.state_conv,
         self.g_mix_pre, self.g_mix_post, self.g_ffn_pre, self.g_ffn_post, self.w_in, self.b_gates, self.w_conv, self.g_mh,
         self.w_out, self.w_gate, self.w_up, self.w_down) = [dram[name] for name in views()]
        (self.y_prompt, self.y_sample, self.kv_prompt, self.kv_sample, self.C_prompt, self.n_prompt, self.m_prompt,
         self.conv_prompt, self.C_sample, self.n_sample, self.m_sample,
         self.conv_sample) = [dram[name] for name in output_shapes()]
        (self.ident_dram, self.attn_bias, self.sample_bias, self.causal, self.sample_causal, self.member, self.carries,
         self.own_head) = [dram[name] for name in CONSTANTS]


class Sems:

    def __init__(self, nc):
        self._nc, self._taken = nc, []

    def new(self, *names):
        made = [self._nc.alloc_semaphore(name=n) for n in names]
        self._taken += made
        return made

    def give_back(self):
        self._nc.clear_and_free_semaphores(self._taken)
        self._nc.all_engine_barrier()
        self._taken = []


def wait_before(engine, settled, sem, value):
    value = engine.to_reg(value)
    engine.wait_ge(*settled)
    engine.wait_ge(sem, value)


def token_tiles_in_turn(engine, body):
    for slot in range(2):
        body(slot, slot, P, 0, slot == 0)
    with engine.Fori(1, TILES // 2) as pair:
        for slot in range(2):
            body(pair * 2 + slot, slot, P, pair, False)
    body(SAMPLE_TILE, 0, NSAMP, TILES // 2, False)


def product(pe, out, w_hi, w_lo, x_hi, x_lo, first, last):
    pe.matmul(out, w_hi, x_hi, start=first, stop=False)
    pe.matmul(out, w_hi, x_lo, start=False, stop=False)
    return pe.matmul(out, w_lo, x_hi, start=False, stop=last)


def attention_weights(queue, g, pair, i):
    col = [COL_QA, COL_KA, COL_KA + D_A][i]
    src = g.w_in[:, ds(pair * P + col, P)].rearrange("(k p) c -> p k c", p=P)
    queue.dma_start(g.a_w_raw[i][:, :, :], src).then_inc(g.a_w_in[i], 16)


def stage_normalise_inputs(nc, g, sems):
    SLOTS = 4
    QUADS = TILES // SLOTS
    slots = range(SLOTS)

    def tiles(engine, body, looped=QUADS):
        for slot in slots:
            body(slot, slot, slot % 2, P, 0)
        with engine.Fori(1, looped) as quad:
            for slot in slots:
                body(quad * SLOTS + slot, slot, slot % 2, P, quad)
        for t in range(looped * SLOTS, TILES):
            body(t, t % SLOTS, t % 2, P, t // SLOTS)
        body(SAMPLE_TILE, 0, 0, NSAMP, QUADS)

    with ExitStack() as ctx:
        sb = lambda n, s, d=F32: ctx.enter_context(nc.sbuf_tensor(n, s, d))
        x = [sb(f"nx{i}", [P, D_MODEL]) for i in slots]
        xn = [sb(f"nxn{i}", [P, D_MODEL]) for i in range(2)]
        squares = sb("nsq", [P, D_MODEL])
        gain = sb("ngain", [P, D_MODEL])
        sumsq = [sb(f"nss{i}", [P, 1]) for i in slots]
        meansq = [sb(f"nms{i}", [P, 1]) for i in slots]
        rstd = [sb(f"nrstd{i}", [P, 1]) for i in slots]
        power = sb("npower", [P, 1])
        turned = [ctx.enter_context(nc.psum_tensor(f"nturned{i}", [P, KT, P], F32)) for i in range(2)]
        raw = sb("n_gate_raw", [P, KT, GATE_ROWS])
        w_hi, w_lo = sb("n_gate_hi", [P, KT, GATE_ROWS], BF16), sb("n_gate_lo", [P, KT, GATE_ROWS], BF16)
        bias = sb("n_gate_bias", [GATE_ROWS, 1])
        ps_gate = [ctx.enter_context(nc.psum_tensor(f"n_ps_gate{i}", [P, CHUNK], F32)) for i in range(2)]
        gate_in, zeroed, gate_w_ready, gate_ready, gate_kept = sems.new("n_gate_in", "n_zeroed", "n_gate_w_ready",
                                                                       "n_gate_ready", "n_gate_kept")
        x_in = sems.new(*(f"n_x_in{i}" for i in slots))
        gain_in, ident_in, ss_ready, power_ready, ms_ready, rstd_ready, xn_ready, turned_ready, hi_ready, \
            turned_free, split_done = sems.new(
                "n_gain_in", "n_ident_in", "n_ss_ready", "n_power_ready", "n_ms_ready",
                "n_rstd_ready", "n_xn_ready", "n_turned_ready", "n_hi_ready", "n_turned_free", "n_split_done")

        with nc.Block() as block:
            @block.sync
            def _(sp):
                sp.dma_start(x[0][:, :], g.x_prompt[0:P, :]).then_inc(x_in[0], 16)
                sp.dma_start(gain[:, :], g.g_mix_pre.to_broadcast([P, D_MODEL])).then_inc(gain_in, 16)
                sp.dma_start(g.ident[:, :], g.ident_dram).then_inc(ident_in, 16)
                for slot in range(1, SLOTS):
                    sp.dma_start(x[slot][:, :], g.x_prompt[slot * P:(slot + 1) * P, :]).then_inc(x_in[slot], 16)
                sp.wait_ge(zeroed, 2)
                w_cols = lambda c: g.w_in[:, c:c + H_M].rearrange("(k p) c -> p k c", p=P)
                sp.dma_start(raw[:, :, 0:H_M], w_cols(COL_GATES)).then_inc(gate_in, 16)
                sp.dma_start(raw[:, :, F_GATE_ROW:], w_cols(COL_GATES + H_M)).then_inc(gate_in, 16)
                sp.dma_start(bias[0:H_M, :], g.b_gates[0:H_M, :]).then_inc(gate_in, 16)
                sp.dma_start(bias[F_GATE_ROW:, :], g.b_gates[H_M:, :]).then_inc(gate_in, 16)
                with sp.Fori(1, QUADS) as quad:
                    for slot in slots:
                        wait_before(sp, (gain_in, 16), xn_ready, (quad - 1) * SLOTS + slot + 1)
                        sp.dma_start(x[slot][:, :], g.x_prompt[ds((quad * SLOTS + slot) * P, P), :]).then_inc(x_in[slot], 16)
                sp.wait_ge(xn_ready, TILES - SLOTS + 1)
                sp.dma_start(x[0][0:NSAMP, :], g.x_sample).then_inc(x_in[0], 16)
            @block.scalar
            def _(act):
                def sum_squares(t, slot, n, nth):
                    act.wait_ge(x_in[slot], nth * 16 + 16)
                    act.wait_ge(ss_ready, t)
                    nc.scalar.activation(squares[0:n, :], x[slot][0:n, :], ACT.Square,
                                         accum_out=sumsq[slot][0:n, :]).then_inc(ss_ready, 1)

                def keep_high(t, s, n):
                    act.wait_ge(turned_ready, t + 1)
                    nc.scalar.activation(g.act_hi[:, :, ds(t * P, n)], turned[s][:, :, 0:n],
                                         ACT.Copy).then_inc(hi_ready, 1)

                def keep_gates(t, s, n):
                    act.wait_ge(gate_ready, t + 1)
                    nc.scalar.activation(g.gates[:, ds(t * P, n)], ps_gate[s][0:GATE_ROWS, 0:n], ACT.Identity,
                                         bias=bias[:, 0:1]).then_inc(gate_kept, 1)

                def step(t, slot, s, n, nth):
                    first = isinstance(t, int) and t == 0
                    if not isinstance(t, int) or t + 2 <= TILES:
                        rows = NSAMP if isinstance(t, int) and t + 2 == TILES else P
                        sum_squares(t + 2, (slot + 2) % SLOTS, rows, nth + (slot >= SLOTS - 2))
                    keep_high(t, s, n)
                    if not first:
                        keep_gates(t - 1, 1 - s, P)

                sum_squares(0, 0, P, 0)
                sum_squares(1, 1, P, 0)
                act.wait_ge(gate_in, 64)
                tiles(act, step, QUADS - 1)
                keep_gates(TILES, 0, NSAMP)

            @block.gpsimd
            def _(pool):
                nc.gpsimd.memset(raw[:, :, :], 0.0).then_inc(zeroed, 1)
                nc.gpsimd.memset(bias[:, :], 0.0).then_inc(zeroed, 1)
                nc.gpsimd.memset(power[:, :], -0.5).then_inc(power_ready, 1)
                pool.wait_ge(power_ready, 1)

                def inverse_rms(t, slot, s, n, nth):
                    wait_before(pool, (power_ready, 1), ss_ready, t + 1)
                    nc.gpsimd.tensor_scalar(meansq[slot][0:n, :], sumsq[slot][0:n, :], 1.0 / D_MODEL, EPS, ALU.mult,
                                            ALU.add).then_inc(ms_ready, 1)
                    pool.wait_ge(ms_ready, t + 1)
                    nc.gpsimd.tensor_tensor(rstd[slot][0:n, :], meansq[slot][0:n, :], power[0:n, :],
                                            ALU.pow).then_inc(rstd_ready, 1)
                tiles(pool, inverse_rms)
                for i in range(3):
                    attention_weights(pool, g, 0, i)

            @block.vector
            def _(dve):
                dve.wait_ge(gain_in, 16)

                def scale(t, slot, s, n):
                    dve.wait_ge(rstd_ready, t + 1)
                    nc.vector.scalar_tensor_tensor(xn[s][0:n, :], x[slot][0:n, :], rstd[slot][0:n, 0:1], gain[0:n, :],
                                                   ALU.mult, ALU.mult).then_inc(xn_ready, 1)

                def keep_low(t, s, n):
                    dve.wait_ge(hi_ready, t + 1)
                    cols = ds(t * P, n)
                    nc.vector.tensor_tensor(g.act_lo[:, :, cols], turned[s][:, :, 0:n], g.act_hi[:, :, cols],
                                            ALU.subtract).then_inc(turned_free, 1)

                scale(0, 0, 0, P)
                dve.wait_ge(gate_in, 64)
                nc.vector.tensor_copy(w_hi[:, :, :], raw[:, :, :]).then_inc(gate_w_ready, 1)
                dve.wait_ge(gate_w_ready, 1)
                nc.vector.tensor_tensor(w_lo[:, :, :], raw[:, :, :], w_hi[:, :, :], ALU.subtract).then_inc(gate_w_ready, 1)

                def step(t, slot, s, n, nth):
                    if n == P:
                        last = isinstance(t, int) and t == TILES - 1
                        scale(t + 1, (slot + 1) % SLOTS, 1 - s, NSAMP if last else P)
                    keep_low(t, s, n)
                tiles(dve, step, QUADS - 1)

            @block.tensor
            def _(pe):
                pe.wait_ge(ident_in, 16)
                pe.sem_inc(turned_free, 2)

                def hold(sem, value):
                    wait_before(pe, (ident_in, 16), sem, value)

                def gate(t, s, n, bank_used):
                    hold(turned_free, t + 3)
                    if bank_used:
                        hold(gate_kept, t - 1)
                    for k in range(KT):
                        mm = product(nc.tensor, ps_gate[s][0:GATE_ROWS, 0:n], w_hi[:, k, :], w_lo[:, k, :],
                                     g.act_hi[:, k, ds(t * P, n)], g.act_lo[:, k, ds(t * P, n)], k == 0, k == KT - 1)
                    mm.then_inc(gate_ready, 1)

                def turn(t, slot, s, n, nth):
                    pe.wait_ge(xn_ready, t + 1)
                    pe.wait_ge(turned_free, t + 1)
                    for k in range(KT):
                        mm = nc.tensor.transpose(turned[s][:, k, 0:n], xn[s][0:n, k * P:(k + 1) * P],
                                                 g.ident[0:n, 0:n])
                    mm.then_inc(turned_ready, 1)
                    if isinstance(t, int) and t == 1:
                        pe.wait_ge(gate_w_ready, 2)
                    if not (isinstance(t, int) and t == 0):
                        gate(t - 1, 1 - s, P, not isinstance(t, int) or t > 2)
                tiles(pe, turn)
                gate(TILES, 0, NSAMP, True)


def stage_prompt_attention(nc, g, sems):
    units, blocks = [], []
    for t in range(TILES):
        for a in range(2):
            first = len(units)
            for c in range(t // 4 + 1):
                units.append((t, a, c, min(CHUNK, (t + 1) * P - c * CHUNK)))
            blocks.append(list(range(first, len(units))))
    block_of = lambda t, a: 2 * t + a
    n_units, n_blocks = len(units), len(blocks)
    n_q, n_rows = NC, TILES + 1
    turns = [("K", 0)]
    for t in range(TILES):
        turns += [("K", t + 1)] + [("X", t - 1)] * (t > 0)
    turns += [("X", TILES - 1)]
    turn_no = {turn: n for n, turn in enumerate(turns)}
    n_turns = len(turns)
    assert n_units % 2 == 0
    half_units = n_units // 2
    turns_before = {}
    seen = 1
    for t in range(TILES):
        for a in range(2):
            seen += a == 0
            for u in blocks[block_of(t, a)]:
                turns_before[u] = seen
            seen += a == 0 and t > 0

    with ExitStack() as ctx:
        sb = lambda n, s, d=F32: ctx.enter_context(nc.sbuf_tensor(n, s, d))
        pb = lambda n, s: ctx.enter_context(nc.psum_tensor(n, s, F32))
        w_raw, w_in = g.a_w_raw, g.a_w_in
        w_hi, w_lo = sb("a_w_hi", [P, KT, 3, P], BF16), sb("a_w_lo", [P, KT, 3, P], BF16)
        q_st = sb("a_q_st", [P, 2, NTOK], BF16)
        k_hi, k_lo = sb("a_k_hi", [P, 2, SEQ], BF16), sb("a_k_lo", [P, 2, SEQ], BF16)
        v = sb("a_v", [P, TILES, P])
        kv = [sb(f"a_kv{i}", [P, 2, P]) for i in range(2)]
        k_twice = [sb(f"a_k_twice{i}", [P, 2 * P]) for i in range(2)]
        bias = [sb(f"a_bias{i}", [P, SEQ]) for i in range(2)]
        probs = [sb(f"a_probs{i}", [P, SEQ]) for i in range(2)]
        low = [sb(f"a_low{i}", [P, TILES // 4]) for i in range(2)]
        den = [sb(f"a_den{i}", [P, 1]) for i in range(2)]
        rden = sb("a_rden", [P, 1])
        out = sb("a_out", [P, 2, HD_A])
        probs_t = [sb(f"a_probs_t{i}", [P, CHUNK]) for i in range(3)]
        ps_rows = [pb(f"a_ps_rows{i}", [P, CHUNK]) for i in range(2)]
        ps_s = [pb(f"a_ps_s{i}", [P, CHUNK]) for i in range(2)]
        ps_t = [pb(f"a_ps_t{i}", [P, CHUNK]) for i in range(2)]
        ps_o = [pb(f"a_ps_o{i}", [P, CHUNK]) for i in range(2)]
        bias_in0, bias_in1, store0, store1 = sems.new("a_bias_in0", "a_bias_in1", "a_store0", "a_store1")
        bias_in, store = [bias_in0, bias_in1], [store0, store1]
        (w_hi_done, w_split, q_ready, q_hi_done, q_done, rows_ready, rows_done, v_done, s_ready, s_done, exp_done,
         unit_turned, even_kept, odd_kept, turn_ready, turn_hi, turn_done, pv_done, rden_done, o_done, zeroed) = sems.new(
            "a_w_hi_done", "a_w_split", "a_q_ready", "a_q_hi_done", "a_q_done", "a_rows_ready", "a_rows_done",
            "a_v_done", "a_s_ready", "a_s_done", "a_exp_done", "a_unit_turned", "a_even_kept", "a_odd_kept", "a_turn_ready",
            "a_turn_hi", "a_turn_done", "a_pv_done", "a_rden_done", "a_o_done", "a_zeroed")
        kept = [even_kept, odd_kept]
        stores_of = [TILES // 2 + 1, TILES // 2]
        rows_of = lambda t: P if t < TILES else NSAMP

        with nc.Block() as block:
            @block.sync
            def _(sp):
                with sp.Fori(0, PAIRS) as p:
                    for a in range(2):
                        wait_before(sp, (w_split, 3), s_done, p * n_units)
                        sp.dma_start(bias[a][:, :], g.attn_bias[ds(p * 2 + a, 1), :, :].rearrange("h p c -> (h p) c"))\
                            .then_inc(bias_in[a], 16)
                    for t in range(TILES + 1):
                        s, n = t % 2, rows_of(t)
                        wait_before(sp, (rows_done, 1), rows_done, p * n_rows + t + 1)
                        dst = g.kv_prompt[t * P:(t + 1) * P, :] if t < TILES else g.kv_sample
                        dst = dst.rearrange("n (v c) -> n v c", v=2)[:, :, ds(p * P, P)]
                        sp.dma_start(dst, kv[s][0:n, :, :]).then_inc(store[s], 16)
                for s in range(2):
                    sp.wait_ge(store[s], PAIRS * stores_of[s] * 16)

            @block.gpsimd
            def _(pool):
                pool.wait_ge(w_split, 3)
                with pool.Fori(1, PAIRS) as p:
                    for i in range(3):
                        wait_before(pool, (w_split, 3), w_split, p * 3 + i + 1)
                        attention_weights(pool, g, p, i)

            @block.tensor
            def _(pe):
                with pe.Fori(0, PAIRS) as p:
                    def rows_part(t, k):
                        n = rows_of(t)
                        if k == 0:
                            pe.wait_ge(*((rows_done, p * n_rows + t - 1) if t >= 2 else (q_done, p * n_q + 4 + (t == 0))))
                        toks = slice(t * P, t * P + n)
                        mm = product(nc.tensor, ps_rows[t % 2][0:n, 0:2 * P], g.act_hi[:, k, toks], g.act_lo[:, k, toks],
                                     w_hi[:, k, 1:3, :], w_lo[:, k, 1:3, :], k == 0, k == KT - 1)
                        if k == KT - 1:
                            mm.then_inc(rows_ready, 1)

                    def start_turn(kind, i, odd_units):
                        pe.wait_ge(kept[1], p * half_units + odd_units)
                        pe.wait_ge(turn_done, p * n_turns + turn_no[kind, i])
                        return ps_t[1]

                    def odd_before(t, a):
                        return blocks[block_of(t, a)][0] // 2

                    def turn_k(t):
                        n = rows_of(t)
                        bank = start_turn("K", t, odd_before(t - 1, 0) if t else 0)
                        wait_before(pe, (w_split, 3), rows_done, p * n_rows + t + 1)
                        if t < TILES:
                            for a in range(2):
                                mm = nc.tensor.transpose(bank[:, a * P:(a + 1) * P], k_twice[t % 2][:, a * P:(a + 1) * P],
                                                         g.ident[:, :])
                        else:
                            mm = nc.tensor.transpose(bank[:, 0:n], kv[t % 2][0:n, 0, :], g.ident[0:n, 0:n])
                        mm.then_inc(turn_ready, 1)

                    def turn_out(t):
                        pe.wait_ge(o_done, p * n_blocks + 2 * t + 2)
                        bank = start_turn("X", t, odd_before(t + 1, 1) if t + 1 < TILES else half_units)
                        nc.tensor.transpose(bank[:, 0:P], out[:, :, :].rearrange("p a d -> p (a d)"),
                                            g.ident[:, :]).then_inc(turn_ready, 1)

                    def scores(u):
                        t, a, c, w = units[u]
                        if c == 0:
                            pe.wait_ge(turn_done, p * n_turns + turn_no["K", t] + 1)
                        pe.wait_ge(s_done, p * n_units + max(u - 1, 0))
                        q = q_st[:, a, t * P:(t + 1) * P]
                        keys = slice(c * CHUNK, c * CHUNK + w)
                        nc.tensor.matmul(ps_s[u % 2][:, 0:w], q, k_hi[:, a, keys], start=True, stop=False)
                        nc.tensor.matmul(ps_s[u % 2][:, 0:w], q, k_lo[:, a, keys], start=False,
                                         stop=True).then_inc(s_ready, 1)

                    def turn_probs(u):
                        t, a, c, w = units[u]
                        pe.wait_ge(exp_done, p * n_blocks + block_of(t, a) + 1)
                        pe.wait_ge(kept[u % 2], p * half_units + u // 2)
                        if u % 2:
                            pe.wait_ge(turn_done, p * n_turns + turns_before[u])
                        bank = ps_t[u % 2]
                        for i in range(w // P):
                            at = c * CHUNK + i * P
                            mm = nc.tensor.transpose(bank[:, i * P:(i + 1) * P], probs[a][:, at:at + P], g.ident[:, :])
                        mm.then_inc(unit_turned, 1)

                    def weigh_values(u):
                        t, a, c, w = units[u]
                        pe.wait_ge(kept[u % 2], p * half_units + u // 2 + 1)
                        if c == 0:
                            pe.wait_ge(v_done, p * TILES + t + 1)
                            pe.wait_ge(o_done, p * n_blocks + max(block_of(t, a) - 1, 0))
                        for i in range(w // P):
                            kt = c * 4 + i
                            mm = nc.tensor.matmul(ps_o[a][:, 0:HD_A], probs_t[u % 3][:, i * P:(i + 1) * P],
                                                  v[:, kt, a * HD_A:(a + 1) * HD_A], start=(kt == 0), stop=(kt == t),
                                                  skip_group_check=True)
                        mm.then_inc(pv_done, 1)

                    for i, (c0, n) in enumerate(CHUNKS):
                        if i == 0:
                            pe.wait_ge(w_split, 3 + p * 3 + 1)
                        pe.wait_ge(*((q_done, p * n_q + i - 1) if i >= 2 else (rows_done, p * n_rows)))
                        for k in range(KT):
                            mm = product(nc.tensor, ps_rows[i % 2][:, 0:n], w_hi[:, k, 0, :], w_lo[:, k, 0, :],
                                         g.act_hi[:, k, c0:c0 + n], g.act_lo[:, k, c0:c0 + n], k == 0, k == KT - 1)
                        mm.then_inc(q_ready, 1)
                    pe.wait_ge(w_split, 3 + p * 3 + 3)
                    for t in range(2):
                        for k in range(KT):
                            rows_part(t, k)
                    turn_k(0)
                    scores(0)
                    for j, mine in enumerate(blocks):
                        t, a = units[mine[0]][0:2]
                        ahead = blocks[j + 1] if j + 1 < n_blocks else []
                        for u in ahead[0:1]:
                            scores(u)
                        if j:
                            weigh_values(mine[0] - 1)
                        if t + 2 <= TILES:
                            for k in range(a * KT // 2, (a + 1) * KT // 2):
                                rows_part(t + 2, k)
                        if a == 0:
                            turn_k(t + 1)
                        for i, u in enumerate(mine):
                            for after in ahead[i + 1:i + 2]:
                                scores(after)
                            turn_probs(u)
                            if i:
                                weigh_values(u - 1)
                        for after in ahead[len(mine) + 1:]:
                            scores(after)
                        if a == 0 and t:
                            turn_out(t - 1)
                    weigh_values(n_units - 1)
                    turn_out(TILES - 1)

            @block.scalar
            def _(act):
                with act.Fori(0, PAIRS) as p:
                    def keep_rows(t):
                        n = rows_of(t)
                        act.wait_ge(rows_ready, p * n_rows + t + 1)
                        act.wait_ge(store[t % 2], (p * stores_of[t % 2] + t // 2) * 16)
                        act.wait_ge(v_done, p * TILES + max(t - 1, 0))
                        if t < TILES:
                            k = ps_rows[t % 2][:, 0:P].rearrange("p (a d) -> p a d", a=2)
                            for a in range(2):
                                twice = k[:, a:a + 1, :].to_broadcast([P, 2, HD_A])
                                nc.scalar.activation(k_twice[t % 2][:, a * P:(a + 1) * P]
                                                     .rearrange("p (r d) -> p r d", r=2), twice, ACT.Copy)
                        nc.scalar.activation(kv[t % 2][0:n, :, :], ps_rows[t % 2][0:n, 0:2 * P]
                                             .rearrange("p (v c) -> p v c", v=2), ACT.Copy).then_inc(rows_done, 1)

                    def turned(kind, i):
                        n = turn_no[kind, i]
                        act.wait_ge(turn_ready, p * n_turns + n + 1)
                        return ps_t[1]

                    def keep_k(t):
                        if t < TILES:
                            bank = turned("K", t)
                            nc.scalar.activation(k_hi[:, :, t * P:(t + 1) * P],
                                                 bank[:, 0:2 * P].rearrange("p (a n) -> p a n", a=2),
                                                 ACT.Copy).then_inc(turn_hi, 1)

                    def exponentials(t, a):
                        j = block_of(t, a)
                        act.wait_ge(s_done, p * n_units + blocks[j][-1] + 1)
                        act.wait_ge(o_done, p * n_blocks + max(j - 1, 0))
                        w = (t + 1) * P
                        nc.scalar.activation(probs[a][:, 0:w], probs[a][:, 0:w], ACT.Exp, bias=low[a][:, t // 4:t // 4 + 1],
                                             scale=-1.0, accum_out=den[a][:, :]).then_inc(exp_done, 1)

                    for i in range(3):
                        act.wait_ge(w_in[i], p * 16 + 16)
                        nc.scalar.activation(w_hi[:, :, i, :], w_raw[i][:, :, :], ACT.Copy).then_inc(w_hi_done, 1)
                    for i, (c0, n) in enumerate(CHUNKS):
                        act.wait_ge(q_ready, p * n_q + i + 1)
                        for a in range(2):
                            last = nc.scalar.activation(q_st[0:HD_A, a, c0:c0 + n],
                                                        ps_rows[i % 2][a * HD_A:(a + 1) * HD_A, 0:n], ACT.Copy,
                                                        scale=HD_A ** -0.5)
                        last.then_inc(q_hi_done, 1)
                    keep_rows(0)
                    keep_rows(1)
                    keep_k(0)
                    exponentials(0, 0)
                    for j, mine in enumerate(blocks):
                        t, a = units[mine[0]][0:2]
                        if a == 0:
                            keep_k(t + 1)
                        else:
                            if t:
                                bank = turned("X", t - 1)
                                nc.scalar.activation(g.mix_a_hi[:, ds(p * NTOK + (t - 1) * P, P)], bank[:, 0:P],
                                                     ACT.Copy).then_inc(turn_hi, 1)
                            if t + 2 <= TILES:
                                keep_rows(t + 2)
                        for u in mine:
                            if u % 2 == 0:
                                act.wait_ge(unit_turned, p * n_units + u + 1)
                                act.wait_ge(pv_done, p * n_units + max(u - 2, 0))
                                w = units[u][3]
                                nc.scalar.activation(probs_t[u % 3][:, 0:w], ps_t[0][:, 0:w], ACT.Copy).then_inc(even_kept, 1)
                        if j + 1 < n_blocks:
                            exponentials(*units[blocks[j + 1][0]][0:2])
                    bank = turned("X", TILES - 1)
                    nc.scalar.activation(g.mix_a_hi[:, ds(p * NTOK + (TILES - 1) * P, P)], bank[:, 0:P],
                                         ACT.Copy).then_inc(turn_hi, 1)

            @block.vector
            def _(dve):
                nc.vector.memset(g.q_pairs[:, :], 0.0).then_inc(zeroed, 1)
                dve.wait_ge(zeroed, 1)
                dve.sem_inc(w_split, 3)
                with dve.Fori(0, PAIRS) as p:
                    def keep_v(t):
                        dve.wait_ge(rows_done, p * n_rows + t + 1)
                        nc.vector.tensor_copy(v[:, t, :], kv[t % 2][:, 1, :]).then_inc(v_done, 1)

                    def turned(kind, i):
                        n = turn_no[kind, i]
                        dve.wait_ge(turn_hi, p * (n_turns - 1) + n + 1 - (n > turn_no["K", TILES]))
                        return ps_t[1]

                    def keep_k(t):
                        if t < TILES:
                            bank = turned("K", t)
                            here = slice(t * P, (t + 1) * P)
                            nc.vector.tensor_tensor(k_lo[:, :, here], bank[:, 0:2 * P].rearrange("p (a n) -> p a n", a=2),
                                                    k_hi[:, :, here], ALU.subtract).then_inc(turn_done, 1)
                        else:
                            n = turn_no["K", t]
                            dve.wait_ge(turn_ready, p * n_turns + n + 1)
                            nc.vector.tensor_copy(g.k_new[:, ds(p * NSAMP, NSAMP)],
                                                  ps_t[1][:, 0:NSAMP]).then_inc(turn_done, 1)

                    def mask_scores(u):
                        t, a, c, w = units[u]
                        if t == 0:
                            dve.wait_ge(bias_in[a], p * 16 + 16)
                        if c:
                            dve.wait_ge(s_done, p * n_units + u)
                        wait_before(dve, (bias_in[a], 16), s_ready, p * n_units + u + 1)
                        at = c * CHUNK
                        off = (TILES - 1 - t) * P + at
                        nc.vector.tensor_tensor_reduce(
                            probs[a][:, at:at + w], ps_s[u % 2][:, 0:w], bias[a][:, off:off + w], -1.0,
                            low[a][:, c - 1:c] if c else 3e38, ALU.add, ALU.min, low[a][:, c:c + 1]).then_inc(s_done, 1)

                    def keep_output(t, a):
                        j = block_of(t, a)
                        dve.wait_ge(exp_done, p * n_blocks + j + 1)
                        dve.wait_ge(o_done, p * n_blocks + j)
                        nc.vector.reciprocal(rden[:, :], den[a][:, :]).then_inc(rden_done, 1)
                        dve.wait_ge(pv_done, p * n_units + blocks[j][-1] + 1)
                        dve.wait_ge(rden_done, p * n_blocks + j + 1)
                        nc.vector.tensor_scalar(out[:, a, :], ps_o[a][:, 0:HD_A], rden[:, 0:1], None,
                                                ALU.mult).then_inc(o_done, 1)

                    for i in range(3):
                        dve.wait_ge(w_hi_done, p * 3 + i + 1)
                        nc.vector.tensor_tensor(w_lo[:, :, i, :], w_raw[i][:, :, :], w_hi[:, :, i, :],
                                                ALU.subtract).then_inc(w_split, 1)
                    for i, (c0, n) in enumerate(CHUNKS):
                        dve.wait_ge(q_hi_done, p * n_q + i + 1)
                        for a in range(2):
                            src = ps_rows[i % 2][a * HD_A:(a + 1) * HD_A, 0:n]
                            last = nc.vector.scalar_tensor_tensor(q_st[HD_A:P, a, c0:c0 + n], src, HD_A ** -0.5,
                                                                  q_st[0:HD_A, a, c0:c0 + n], ALU.mult, ALU.subtract)
                            if n < CHUNK:
                                own = g.q_pairs[a * HD_A:(a + 1) * HD_A, ds(p * (DEC_BATCH * HT + 2 * DEC_SEQ), DEC_BATCH * HT)]
                                own = own.rearrange("p (b c) -> p b c", b=DEC_BATCH)[:, :, a * DEC_SEQ:(a + 1) * DEC_SEQ]
                                last = nc.vector.tensor_scalar(own, src.rearrange("p (b t) -> p b t", b=DEC_BATCH),
                                                               HD_A ** -0.5, None, ALU.mult)
                        last.then_inc(q_done, 1)
                    keep_v(0)
                    keep_v(1)
                    keep_k(0)
                    mask_scores(0)
                    for j, mine in enumerate(blocks):
                        t, a = units[mine[0]][0:2]
                        ahead = blocks[j + 1] if j + 1 < n_blocks else []
                        for u in ahead[0:1]:
                            mask_scores(u)
                        if a and t:
                            bank = turned("X", t - 1)
                            at = ds(p * NTOK + (t - 1) * P, P)
                            nc.vector.tensor_tensor(g.mix_a_lo[:, at], bank[:, 0:P], g.mix_a_hi[:, at],
                                                    ALU.subtract).then_inc(turn_done, 1)
                        if j:
                            keep_output(*units[mine[0] - 1][0:2])
                        if a == 0:
                            keep_k(t + 1)
                        for i, u in enumerate(mine):
                            for after in ahead[i + 1:i + 2]:
                                mask_scores(after)
                            if u % 2:
                                dve.wait_ge(unit_turned, p * n_units + u + 1)
                                dve.wait_ge(pv_done, p * n_units + max(u - 2, 0))
                                w = units[u][3]
                                nc.vector.tensor_copy(probs_t[u % 3][:, 0:w], ps_t[1][:, 0:w]).then_inc(odd_kept, 1)
                        for after in ahead[len(mine) + 1:]:
                            mask_scores(after)
                        if a and t + 2 < TILES:
                            keep_v(t + 2)
                    keep_output(TILES - 1, 1)
                    bank = turned("X", TILES - 1)
                    at = ds(p * NTOK + (TILES - 1) * P, P)
                    nc.vector.tensor_tensor(g.mix_a_lo[:, at], bank[:, 0:P], g.mix_a_hi[:, at],
                                            ALU.subtract).then_inc(turn_done, 1)
def stage_sample_attention(nc, g, sems):
    NEW = CACHE_TILES * P
    BIG = CHUNK // P
    with ExitStack() as ctx:
        sb = lambda n, s, d=F32: ctx.enter_context(nc.sbuf_tensor(n, s, d))
        pb = lambda n, s: ctx.enter_context(nc.psum_tensor(n, s, F32))
        two = lambda n, s, d=F32: [sb(f"{n}{i}", s, d) for i in range(2)]
        k_raw, v = two("s_k_raw", [P, CACHE_TILES, D_A]), two("s_v", [P, CACHE_TILES + 1, D_A])
        bias = sb("s_bias", [HT, KEYS])
        k_hi, k_lo = two("s_k_hi", [P, PAIRS, KEYS], BF16), two("s_k_lo", [P, PAIRS, KEYS], BF16)
        q_hi, q_lo = two("s_q_hi", [P, PAIRS, HT], BF16), two("s_q_lo", [P, PAIRS, HT], BF16)
        o_rows = sb("s_o_rows", [2 * DEC_SEQ, DEC_BATCH * D_A])
        probs = two("s_probs", [HT, KEYS])
        low = two("s_low", [HT, 2])
        den, rden = two("s_den", [HT, 1]), two("s_rden", [HT, 1])
        p_t = two("s_p_t", [P, (CACHE_TILES + 1) * HT])
        ps_big = [pb(f"s_ps_big{i}", [P, CHUNK]) for i in range(2)]
        ps_small = [pb(f"s_ps_small{i}", [P, CHUNK]) for i in range(2)]
        ps_s = [pb(f"s_ps_s{i}", [P, CHUNK]) for i in range(2)]
        ps_p, ps_o = pb("s_ps_p", [P, CHUNK]), pb("s_ps_o", [P, CHUNK])
        (k_in0, k_in1, v_in0, v_in1, bias_in, k_turned, big_hi, small_hi, big_done, small_done, q_high, ready,
         s_ready, s_done, exp_done, rden_done, p_done, p_turned, p_kept, o_ready, o_kept, o_done, o_hi, o_lo,
         mix_out) = sems.new(
            "s_k_in0", "s_k_in1", "s_v_in0", "s_v_in1", "s_bias_in", "s_k_turned", "s_big_hi", "s_small_hi",
            "s_big_done", "s_small_done", "s_q_high", "s_operands_ready", "s_s_ready", "s_s_done", "s_exp_done",
            "s_rden_done", "s_p_done", "s_p_turned", "s_p_kept", "s_o_ready", "s_o_kept", "s_o_done", "s_o_hi", "s_o_lo",
            "s_mix_out")
        k_in, v_in = [k_in0, k_in1], [v_in0, v_in1]

        def load(queue, tile, loaded, b, slot, first):
            cols = slice(first, first + D_A)
            far = g.cache_kv[ds(b, 1), 0:FAR, cols].rearrange("o (f n r) c -> (o f) n r c", f=FAR_TILES, r=FAR_STRIDE)
            for f in range(FAR_TILES):
                queue.dma_start(tile[slot][:, f, :], far[f, :, 0:DEC_SEQ, :]).then_inc(loaded[slot], 16)
            near = g.cache_kv[ds(b, 1), FAR:, cols].rearrange("o (t p) c -> p (o t) c", p=P)
            queue.dma_start(tile[slot][:, FAR_TILES:CACHE_TILES, :], near).then_inc(loaded[slot], 16)

        def batches(engine, step):
            with engine.Fori(0, DEC_BATCH // 2 - 1) as two_:
                for slot in range(2):
                    step(two_ * 2 + slot, slot, two_, 2)
            last = DEC_BATCH // 2 - 1
            step(2 * last, 0, last, 1)
            step(2 * last + 1, 1, last, 0)

        with nc.Block() as block:
            @block.sync
            def _(sp):
                mix = [m[:, :].rearrange("p (q n) -> p q n", q=PAIRS) for m in (g.mix_a_hi, g.mix_a_lo)]
                mix_dram = g.mix_a_dram.rearrange("i p (q n) -> i p q n", q=PAIRS)

                load(sp, k_raw, k_in, 0, 0, 0)
                sp.dma_start(bias[:, :], g.sample_bias).then_inc(bias_in, 16)
                load(sp, k_raw, k_in, 1, 1, 0)
                for part in range(2):
                    sp.dma_start(mix_dram[part, :, :, 0:SEQ], mix[part][:, :, 0:SEQ]).then_inc(mix_out, 16)
                sp.wait_ge(bias_in, 16)
                with sp.Fori(1, DEC_BATCH // 2) as two_:
                    for slot in range(2):
                        wait_before(sp, (bias_in, 16), k_turned, (two_ * 2 + slot - 1) * PAIRS)
                        load(sp, k_raw, k_in, two_ * 2 + slot, slot, 0)
                sp.wait_ge(o_hi, 2 * PAIRS)
                sp.wait_ge(o_lo, 2 * PAIRS)
                for part in range(2):
                    sp.dma_start(mix_dram[part, :, :, SEQ:], mix[part][:, :, SEQ:]).then_inc(mix_out, 16)
                sp.wait_ge(mix_out, 64)

            @block.gpsimd
            def _(pool):
                pool.wait_ge(bias_in, 16)

                def values(b, slot):
                    load(pool, v, v_in, b, slot, D_A)
                    pool.dma_start(v[slot][0:DEC_SEQ, CACHE_TILES, :], g.kv_sample[ds(b * DEC_SEQ, DEC_SEQ), D_A:])\
                        .then_inc(v_in[slot], 16)

                values(0, 0)
                values(1, 1)
                with pool.Fori(1, DEC_BATCH // 2) as two_:
                    for slot in range(2):
                        wait_before(pool, (bias_in, 16), o_ready, two_ * 2 + slot - 1)
                        values(two_ * 2 + slot, slot)

            @block.tensor
            def _(pe):
                pe.wait_ge(bias_in, 16)

                def hold(sem, value):
                    wait_before(pe, (bias_in, 16), sem, value)

                def turn_k(b, slot, nth, pair, free=False):
                    if pair == 0:
                        hold(k_in[slot], (nth + 1) * (FAR_TILES + 1) * 16)
                    i, bank = b * PAIRS + pair, (slot * PAIRS + pair) % 2
                    if not free:
                        hold(big_done, i - 1)
                        hold(small_done, i - 1)
                    for tile in range(CACHE_TILES):
                        to = ps_big[bank] if tile < BIG else ps_small[bank]
                        at = tile % BIG * P
                        mm = nc.tensor.transpose(to[:, at:at + P], k_raw[slot][:, tile, pair * P:(pair + 1) * P],
                                                 g.ident[:, :])
                    mm.then_inc(k_turned, 1)

                def scores(b, slot):
                    hold(big_done, b * PAIRS + PAIRS)
                    hold(small_done, b * PAIRS + PAIRS)
                    hold(ready, b + 1)
                    hold(s_done, b * 2)
                    for pair in range(PAIRS):
                        for half, (c0, c1) in enumerate(((0, CHUNK), (CHUNK, KEYS))):
                            mm = product(nc.tensor, ps_s[half][0:HT, 0:c1 - c0], q_hi[slot][:, pair, :], q_lo[slot][:, pair, :],
                                         k_hi[slot][:, pair, c0:c1], k_lo[slot][:, pair, c0:c1], pair == 0,
                                         pair == PAIRS - 1)
                    mm.then_inc(s_ready, 1)

                def attend(b, slot, nth, more):
                    if more:
                        scores(b + 1, 1 - slot)
                    hold(o_kept, b)
                    hold(p_done, b + 1)
                    for tile in range(CACHE_TILES + 1):
                        n = P if tile < CACHE_TILES else DEC_SEQ
                        mm = nc.tensor.transpose(ps_p[0:n, tile * HT:(tile + 1) * HT], probs[slot][:, tile * P:tile * P + n],
                                                 g.ident[0:HT, 0:HT])
                    mm.then_inc(p_turned, 1)
                    if more == 2:
                        turn_k(b + 2, slot, nth + 1, 0)
                    hold(p_kept, b + 1)
                    hold(v_in[slot], (nth + 1) * (FAR_TILES + 2) * 16)
                    for pair in range(PAIRS):
                        cols = slice(pair * P, (pair + 1) * P)
                        for tile in range(CACHE_TILES + 1):
                            n = P if tile < CACHE_TILES else DEC_SEQ
                            own = slice(tile * HT + pair * 2 * DEC_SEQ, tile * HT + (pair + 1) * 2 * DEC_SEQ)
                            mm = nc.tensor.matmul(ps_p[0:2 * DEC_SEQ, cols], p_t[slot][0:n, own], v[slot][0:n, tile, cols],
                                                  start=(tile == 0), stop=(tile == CACHE_TILES), skip_group_check=True)
                        if pair == PAIRS - 1:
                            mm.then_inc(o_ready, 1)
                        if more == 2 and pair < PAIRS - 1:
                            turn_k(b + 2, slot, nth + 1, pair + 1)

                for b in range(2):
                    for pair in range(PAIRS):
                        turn_k(b, b, 0, pair, b == 0 and pair < 2)
                scores(0, 0)
                batches(pe, attend)
                pe.wait_ge(o_kept, DEC_BATCH)
                for i in range(DEC_BATCH * PAIRS):
                    mm = nc.tensor.transpose(ps_o[:, i * 2 * DEC_SEQ:(i + 1) * 2 * DEC_SEQ], o_rows[:, i * P:(i + 1) * P],
                                             g.ident[0:2 * DEC_SEQ, 0:2 * DEC_SEQ])
                mm.then_inc(o_done, 1)

            @block.scalar
            def _(act):
                def keep_k(b, slot):
                    for pair in range(PAIRS):
                        bank = (slot * PAIRS + pair) % 2
                        act.wait_ge(k_turned, b * PAIRS + pair + 1)
                        nc.scalar.activation(k_hi[slot][:, pair, 0:CHUNK], ps_big[bank][:, :], ACT.Copy).then_inc(big_hi, 1)
                        nc.scalar.activation(k_hi[slot][:, pair, CHUNK:NEW], ps_small[bank][:, 0:NEW - CHUNK],
                                             ACT.Copy).then_inc(small_hi, 1)

                def exponential(b, slot):
                    act.wait_ge(s_done, b * 2 + 2)
                    nc.scalar.activation(probs[slot][:, :], probs[slot][:, :], ACT.Exp, bias=low[slot][:, 1:2], scale=-1.0,
                                         accum_out=den[slot][:, :]).then_inc(exp_done, 1)

                def attend(b, slot, nth, more):
                    act.wait_ge(p_turned, b + 1)
                    new = CACHE_TILES * HT
                    nc.scalar.activation(p_t[slot][:, 0:new], ps_p[:, 0:new], ACT.Copy)
                    nc.scalar.activation(p_t[slot][0:DEC_SEQ, new:], ps_p[0:DEC_SEQ, new:new + HT], ACT.Copy).then_inc(p_kept, 1)
                    if more:
                        exponential(b + 1, 1 - slot)
                    if more == 2:
                        keep_k(b + 2, slot)
                    act.wait_ge(o_ready, b + 1)
                    nc.scalar.activation(o_rows[:, ds(b * D_A, D_A)], ps_p[0:2 * DEC_SEQ, 0:D_A], ACT.Copy).then_inc(o_kept, 1)

                keep_k(0, 0)
                keep_k(1, 1)
                exponential(0, 0)
                batches(act, attend)
                act.wait_ge(o_done, 1)
                for a in range(2):
                    rows = slice(a * HD_A, (a + 1) * HD_A)
                    out = ps_o[rows, 0:DEC_BATCH * HT].rearrange("p (b q a t) -> p a q b t", q=PAIRS, a=2, t=DEC_SEQ)
                    for pair in range(PAIRS):
                        to = g.mix_a_hi[rows, pair * NTOK + SEQ:(pair + 1) * NTOK].rearrange("p (b t) -> p b t", t=DEC_SEQ)
                        nc.scalar.activation(to, out[:, a, pair, :, :], ACT.Copy).then_inc(o_hi, 1)

            @block.vector
            def _(dve):
                def prepare(b, slot):
                    for pair in range(PAIRS):
                        bank, at = (slot * PAIRS + pair) % 2, b * PAIRS + pair + 1
                        dve.wait_ge(big_hi, at)
                        nc.vector.tensor_tensor(k_lo[slot][:, pair, 0:CHUNK], ps_big[bank][:, :], k_hi[slot][:, pair, 0:CHUNK],
                                                ALU.subtract).then_inc(big_done, 1)
                        dve.wait_ge(small_hi, at)
                        nc.vector.tensor_tensor(k_lo[slot][:, pair, CHUNK:NEW], ps_small[bank][:, 0:NEW - CHUNK],
                                                k_hi[slot][:, pair, CHUNK:NEW], ALU.subtract).then_inc(small_done, 1)
                    k_new = g.k_new[:, :].rearrange("p (q n) -> p q n", q=PAIRS)[:, :, ds(b * DEC_SEQ, DEC_SEQ)]
                    own = g.q_pairs[:, 0:PAIRS * DEC_BATCH * HT].rearrange("p (q n) -> p q n", q=PAIRS)[:, :, ds(b * HT, HT)]
                    nc.vector.tensor_copy(k_hi[slot][:, :, NEW:], k_new)
                    nc.vector.tensor_copy(q_hi[slot][:, :, :], own).then_inc(q_high, 1)
                    dve.wait_ge(q_high, b + 1)
                    nc.vector.tensor_tensor(k_lo[slot][:, :, NEW:], k_new, k_hi[slot][:, :, NEW:], ALU.subtract)
                    nc.vector.tensor_tensor(q_lo[slot][:, :, :], own, q_hi[slot][:, :, :], ALU.subtract).then_inc(ready, 1)

                def mask_scores(b, slot):
                    wait_before(dve, (bias_in, 16), s_ready, b + 1)
                    for half, (c0, c1) in enumerate(((0, CHUNK), (CHUNK, KEYS))):
                        if half:
                            wait_before(dve, (bias_in, 16), s_done, b * 2 + 1)
                        nc.vector.tensor_tensor_reduce(
                            probs[slot][:, c0:c1], ps_s[half][0:HT, 0:c1 - c0], bias[:, c0:c1], -1.0,
                            low[slot][:, 0:1] if half else 3e38, ALU.add, ALU.min, low[slot][:, half:half + 1])\
                            .then_inc(s_done, 1)

                def normalise(b, slot):
                    dve.wait_ge(exp_done, b + 1)
                    nc.vector.reciprocal(rden[slot][:, :], den[slot][:, :]).then_inc(rden_done, 1)
                    dve.wait_ge(rden_done, b + 1)
                    nc.vector.tensor_scalar(probs[slot][:, :], probs[slot][:, :], rden[slot][:, 0:1], None,
                                            ALU.mult).then_inc(p_done, 1)

                def attend(b, slot, nth, more):
                    if more:
                        mask_scores(b + 1, 1 - slot)
                        normalise(b + 1, 1 - slot)
                    if more == 2:
                        prepare(b + 2, slot)

                dve.wait_ge(bias_in, 16)
                prepare(0, 0)
                prepare(1, 1)
                mask_scores(0, 0)
                normalise(0, 0)
                batches(dve, attend)
                dve.wait_ge(o_hi, 2 * PAIRS)
                for a in range(2):
                    rows = slice(a * HD_A, (a + 1) * HD_A)
                    out = ps_o[rows, 0:DEC_BATCH * HT].rearrange("p (b q a t) -> p a q b t", q=PAIRS, a=2, t=DEC_SEQ)
                    for pair in range(PAIRS):
                        here = slice(pair * NTOK + SEQ, (pair + 1) * NTOK)
                        nc.vector.tensor_tensor(g.mix_a_lo[rows, here].rearrange("p (b t) -> p b t", t=DEC_SEQ),
                                                out[:, a, pair, :, :],
                                                g.mix_a_hi[rows, here].rearrange("p (b t) -> p b t", t=DEC_SEQ),
                                                ALU.subtract).then_inc(o_lo, 1)


TAB_LOG, TAB_SIZE = 0, 4
TAB_DECAY = (TILES + 1) * TAB_SIZE
TAB_CONV = TAB_DECAY + SEGMENTS
TAB_GAIN = TAB_CONV + 2 * CONV_W
TAB_HIST = TAB_GAIN + 1
TAB_N = TAB_HIST + 2 * DEC_BATCH * HIST
TAB = TAB_N + DEC_BATCH
K_SCALE = HD_M ** -0.5
ROW_W, ROW_E, ROW_M = 32, 64, 96


def stage_gates(nc, g, sems):
    with ExitStack() as ctx:
        sb = lambda n, s, d=F32: ctx.enter_context(nc.sbuf_tensor(n, s, d))
        pb = lambda n, s: ctx.enter_context(nc.psum_tensor(n, s, F32))
        gates = g.gates
        row = lambda n, w=NTOK: sb(n, [H_M, w])
        fgate, soft, lf, carries, b, m, u = [row(f"g_{n}") for n in ("fgate", "soft", "lf", "carries", "b", "m", "u")]
        log_w, log_e = row("g_log_w"), row("g_log_e")
        m_state = row("g_m_state", DEC_BATCH)
        m_in, m_end, b_end, shift, decay = [row(f"g_{n}", SEGMENTS) for n in ("m_in", "m_end", "b_end", "shift", "decay")]
        own = sb("g_own", [H_M, H_M, SEGMENTS])
        own_decay = sb("g_own_decay", [H_M, H_M, SEGMENTS])
        ones = sb("g_ones", [H_M, P])
        stack = sb("g_stack", [P, NTOK])
        conv_rows = sb("g_conv_rows", [CONV_W * 2 * H_M, P])
        gain_rows = sb("g_gain_rows", [H_M, P])
        hist_rows = sb("g_hist_rows", [DEC_BATCH * HIST, 2 * D_M])
        n_rows = sb("g_n_rows", [DEC_BATCH * H_M, HD_M])
        ps_a, ps_b, ps_c = pb("g_ps_a", [P, CHUNK]), pb("g_ps_b", [P, CHUNK]), pb("g_ps_c", [P, CHUNK])
        ps_tok = [pb(f"g_ps_tok{i}", [P, CHUNK]) for i in range(2)]
        tab_dma, zeroed, vec, act_done, tables_ready, tok_ready, tok_done, decay_ready, out_dma, tables_done = sems.new(
            "g_tab_dma", "g_zeroed", "g_vec", "g_act_done", "g_tables_ready", "g_tok_ready", "g_tok_done", "g_decay_ready",
            "g_out_dma", "g_tables_done")
        prompt = lambda r: r[:, 0:SEQ].rearrange("h (s n) -> h s n", n=P)
        sample = lambda r: r[:, SEQ:].rearrange("h (s n) -> h s n", n=DEC_SEQ)
        tab = g.table
        groups = [list(range(t, t + 4)) for t in range(0, TILES, 4)] + [[TILES]]

        with nc.Block() as block:
            @block.sync
            def _(sp):
                with nc.allow_non_contiguous_dma(reason="a transposed state of 40 numbers"):
                    sp.dma_start(m_state[:, :], g.state_m.rearrange("b h -> h b")).then_inc(tab_dma, 16)
                sp.dma_start(carries[:, :], g.carries).then_inc(tab_dma, 16)
                sp.dma_start(own[:, :, :], g.own_head).then_inc(tab_dma, 16)
                conv_src = g.w_conv.rearrange("i (c p) -> i c p", p=P)
                for i in range(CONV_W):
                    sp.dma_start(conv_rows[i * 2 * H_M:(i + 1) * 2 * H_M, :], conv_src[i, :, :]).then_inc(tab_dma, 16)
                sp.dma_start(gain_rows[:, :], g.g_mh).then_inc(tab_dma, 16)
                sp.dma_start(hist_rows[:, :], g.state_conv).then_inc(tab_dma, 16)
                sp.dma_start(n_rows[:, :], g.state_n).then_inc(tab_dma, 16)
                sp.wait_ge(vec, 3 + DEC_BATCH + 8)
                sp.dma_start(g.u_dram, u[:, :]).then_inc(out_dma, 16)
                with nc.allow_non_contiguous_dma(reason="45 numbers"):
                    sp.dma_start(g.m_prompt.rearrange("o h -> h o"), m_end[:, TILES - 1:TILES]).then_inc(out_dma, 16)
                    sp.dma_start(g.m_sample.rearrange("b h -> h b"), m_end[:, TILES:]).then_inc(out_dma, 16)
                sp.wait_ge(out_dma, 48)

            @block.gpsimd
            def _(pool):
                nc.gpsimd.memset(tab[:, :, TILES * TAB_SIZE:TAB_DECAY], 0.0).then_inc(zeroed, 1)
                nc.gpsimd.memset(ones[:, :], 1.0).then_inc(zeroed, 1)
                nc.gpsimd.memset(stack[:, :], 0.0).then_inc(zeroed, 1)

            @block.tensor
            def _(pe):
                pe.wait_ge(tab_dma, 160)
                nc.tensor.transpose(ps_a[:, 0:CONV_W * 2 * H_M], conv_rows[:, :], g.ident[0:CONV_W * 2 * H_M, 0:CONV_W * 2 * H_M])
                nc.tensor.transpose(ps_a[:, 64:64 + H_M], gain_rows[:, :], g.ident[0:H_M, 0:H_M])
                nc.tensor.transpose(ps_a[:, 128:128 + DEC_BATCH * H_M], n_rows[:, :],
                                    g.ident[0:DEC_BATCH * H_M, 0:DEC_BATCH * H_M]).then_inc(tables_ready, 1)
                n = DEC_BATCH * HIST
                for c in range(2 * H_M):
                    mm = nc.tensor.transpose(ps_b[:, c * n:(c + 1) * n], hist_rows[:, c * P:(c + 1) * P], g.ident[0:n, 0:n])
                mm.then_inc(tables_ready, 1)
                pe.wait_ge(zeroed, 2)
                pe.wait_ge(vec, 3 + DEC_BATCH + 12)
                nc.tensor.matmul(ps_c[:, 0:H_M * SEGMENTS], ones[:, :], own_decay[:, :, :].rearrange("k h s -> k (h s)"),
                                 start=True, stop=True).then_inc(decay_ready, 1)
                pe.wait_ge(act_done, 7)
                for i, group in enumerate(groups):
                    if i >= 2:
                        pe.wait_ge(tok_done, i - 1)
                    for j, t in enumerate(group):
                        n = P if t < TILES else NSAMP
                        mm = nc.tensor.transpose(ps_tok[i % 2][0:n, j * P:(j + 1) * P], stack[:, t * P:t * P + n], g.ident[:, :])
                    mm.then_inc(tok_ready, 1)

            @block.scalar
            def _(act):
                nc.scalar.activation(soft[:, :], gates[F_GATE_ROW:, :], ACT.Abs).then_inc(act_done, 1)
                act.wait_ge(act_done, 1)
                nc.scalar.activation(soft[:, :], soft[:, :], ACT.Exp, scale=-1.0).then_inc(act_done, 1)
                act.wait_ge(act_done, 2)
                nc.scalar.activation(soft[:, :], soft[:, :], ACT.Ln, bias=1.0).then_inc(act_done, 1)
                act.wait_ge(vec, 3 + DEC_BATCH + 9)
                nc.scalar.activation(decay[:, :], decay[:, :], ACT.Exp).then_inc(act_done, 1)
                act.wait_ge(zeroed, 3)
                nc.scalar.activation(stack[ROW_M:ROW_M + H_M, :], m[:, :], ACT.Exp, scale=-1.0).then_inc(act_done, 1)
                act.wait_ge(vec, 3 + DEC_BATCH + 10)
                nc.scalar.activation(stack[ROW_W:ROW_W + H_M, :], log_w[:, :], ACT.Exp).then_inc(act_done, 1)
                act.wait_ge(vec, 3 + DEC_BATCH + 11)
                nc.scalar.activation(stack[ROW_E:ROW_E + H_M, :], log_e[:, :], ACT.Exp).then_inc(act_done, 1)

            @block.vector
            def _(dve):
                done = [0]

                def step(*instructions):
                    instructions[-1].then_inc(vec, 1)
                    done[0] += 1
                    dve.wait_ge(vec, done[0])

                step(nc.vector.tensor_copy(fgate[:, :], gates[F_GATE_ROW:, :]))
                dve.wait_ge(tables_ready, 2)
                taps = ps_a[:, 0:CONV_W * 2 * H_M].rearrange("p (i j h) -> p h j i", i=CONV_W, j=2)
                conv = tab[:, :, TAB_CONV:TAB_CONV + 2 * CONV_W].rearrange("p h (j i) -> p h j i", j=2)
                nc.vector.tensor_scalar(conv[:, :, 0, :], taps[:, :, 0, :], 0.5, None, ALU.mult)
                nc.vector.tensor_scalar(conv[:, :, 1, :], taps[:, :, 1, :], 0.5 * K_SCALE, None, ALU.mult)
                nc.vector.tensor_scalar(tab[:, :, TAB_GAIN], ps_a[:, 64:64 + H_M], 0.5, None, ALU.mult)
                nc.vector.tensor_copy(tab[:, :, TAB_N:], ps_a[:, 128:128 + DEC_BATCH * H_M].rearrange("p (b h) -> p h b", h=H_M))
                hist = ps_b[:, 0:2 * H_M * DEC_BATCH * HIST].rearrange("p (j h r) -> p j h r", j=2, h=H_M)
                for j in range(2):
                    at = TAB_HIST + j * DEC_BATCH * HIST
                    last = nc.vector.tensor_copy(tab[:, :, at:at + DEC_BATCH * HIST], hist[:, j, :, :])
                last.then_inc(tables_done, 1)
                dve.wait_ge(act_done, 3)
                step(nc.vector.scalar_tensor_tensor(lf[:, :], fgate[:, :], 0.0, soft[:, :], ALU.min, ALU.subtract))
                igate = gates[0:H_M, :]
                step(nc.vector.tensor_tensor_scan(m[:, 0:SEQ], lf[:, 0:SEQ], igate[:, 0:SEQ], 0.0, ALU.add, ALU.max))
                for s in range(DEC_BATCH):
                    here = slice(SEQ + s * DEC_SEQ, SEQ + (s + 1) * DEC_SEQ)
                    step(nc.vector.tensor_tensor_scan(m[:, here], lf[:, here], igate[:, here], m_state[:, s:s + 1],
                                                      ALU.add, ALU.max))
                step(nc.vector.tensor_tensor_scan(b[:, :], carries[:, :], lf[:, :], 0.0, ALU.mult, ALU.add))
                step(nc.vector.memset(m_in[:, 0:1], 0.0))
                nc.vector.tensor_copy(m_in[:, 1:TILES], prompt(m)[:, 0:TILES - 1, P - 1])
                step(nc.vector.tensor_copy(m_in[:, TILES:], m_state[:, :]))
                nc.vector.tensor_copy(m_end[:, 0:TILES], prompt(m)[:, :, P - 1])
                step(nc.vector.tensor_copy(m_end[:, TILES:], sample(m)[:, :, DEC_SEQ - 1]))
                nc.vector.tensor_copy(b_end[:, 0:TILES], prompt(b)[:, :, P - 1])
                step(nc.vector.tensor_copy(b_end[:, TILES:], sample(b)[:, :, DEC_SEQ - 1]))
                step(nc.vector.tensor_tensor(shift[:, :], b_end[:, :], m_end[:, :], ALU.subtract))
                dve.wait_ge(zeroed, 3)
                step(nc.vector.tensor_tensor(stack[0:H_M, :], igate, b[:, :], ALU.subtract))
                step(nc.vector.tensor_tensor(u[:, :], b[:, :], m[:, :], ALU.subtract))
                step(nc.vector.tensor_tensor(decay[:, :], shift[:, :], m_in[:, :], ALU.add))
                for row_, plus, out in ((stack, shift, log_w), (u, m_in, log_e)):
                    rows = row_[0:H_M, :]
                    nc.vector.tensor_tensor(prompt(out), prompt(rows),
                                            plus[:, 0:TILES].unsqueeze(2).to_broadcast([H_M, TILES, P]), ALU.add)
                    step(nc.vector.tensor_tensor(sample(out), sample(rows),
                                                 plus[:, TILES:].unsqueeze(2).to_broadcast([H_M, DEC_BATCH, DEC_SEQ]), ALU.add))
                dve.wait_ge(act_done, 4)
                step(nc.vector.tensor_tensor(own_decay[:, :, :], own[:, :, :],
                                             decay[:, :].unsqueeze(1).to_broadcast([H_M, H_M, SEGMENTS]), ALU.mult))
                dve.wait_ge(decay_ready, 1)
                nc.vector.tensor_copy(tab[:, :, TAB_DECAY:TAB_DECAY + SEGMENTS],
                                      ps_c[:, 0:H_M * SEGMENTS].rearrange("p (h s) -> p h s", h=H_M))
                for i, group in enumerate(groups):
                    n = P if group[0] < TILES else NSAMP
                    dve.wait_ge(tok_ready, i + 1)
                    src = ps_tok[i % 2][0:n, 0:len(group) * P].rearrange("p (t q r) -> p r t q", t=len(group), q=TAB_SIZE)
                    dst = tab[0:n, :, group[0] * TAB_SIZE:(group[-1] + 1) * TAB_SIZE]
                    nc.vector.tensor_copy(dst.rearrange("p h (t q) -> p h t q", q=TAB_SIZE), src[:, 0:H_M, :, :])\
                        .then_inc(tok_done, 1)
def stage_mlstm(nc, g, sems):
    n_units, n_steps = 2 * NC, TILES + 1
    SAMPLE = SEQ
    V_SLOTS = 3
    with ExitStack() as ctx:
        sb = lambda n, s, d=F32: ctx.enter_context(nc.sbuf_tensor(n, s, d))
        pb = lambda n, s: ctx.enter_context(nc.psum_tensor(n, s, F32))
        two = lambda n, s, d=F32: [sb(f"{n}{i}", s, d) for i in range(2)]
        w_raw = two("m_w_raw", [P, KT, P])
        w_hi, w_lo = sb("m_w_hi", [P, KT, 4, P], BF16), sb("m_w_lo", [P, KT, 4, P], BF16)
        hd = sb("m_hd", [P, TAB])
        causal, sample_causal = sb("m_causal", [P, P]), sb("m_sample_causal", [NSAMP, NSAMP])
        member = sb("m_member", [NSAMP, DEC_BATCH])
        power = sb("m_power", [P, 1])
        no_past = sb("m_no_past", [P, HIST])
        z = two("m_z", [P, HIST + CHUNK])
        zs = sb("m_zs", [P, DEC_BATCH, HIST + DEC_SEQ])
        y, th = two("m_y", [P, CHUNK]), two("m_th", [P, CHUNK])
        last_rows = sb("m_last_rows", [P, HIST + DEC_BATCH * HIST])
        conv_out = two("m_conv_out", [HIST + DEC_BATCH * HIST, P])
        qk = two("m_qk", [P, NTOK])
        q, k = qk
        u = sb("m_u", [P, NTOK])
        v1 = sb("m_v1", [P, V_SLOTS, HD_M + 1])
        o_tanh = sb("m_o_tanh", [P, V_SLOTS, HD_M])
        state = sb("m_state", [P, HD_M + 1])
        expd, sm, kn = two("m_expd", [P, P]), two("m_sm", [P, P]), two("m_kn", [P, P])
        wv, inter, tot = two("m_wv", [P, HD_M + 1]), two("m_inter", [P, HD_M + 1]), two("m_tot", [P, HD_M + 1])
        x, hn = two("m_x", [P, HD_M]), two("m_hn", [P, HD_M])
        squares = sb("m_squares", [P, HD_M])
        den, rden, ss, msq, ms, rs, r = [two(f"m_{n}", [P, 1]) for n in ("den", "rden", "ss", "msq", "ms", "rs", "r")]
        c_state, c_turned = sb("m_c_state", [P, DEC_BATCH, HD_M]), sb("m_c_turned", [P, DEC_BATCH, HD_M])
        own_w = sb("m_own_w", [NSAMP, DEC_BATCH])
        own_wv = sb("m_own_wv", [NSAMP, DEC_BATCH, HD_M])
        inter_t = sb("m_inter_t", [P, NSAMP])
        den_all, den_own = sb("m_den_all", [NSAMP, DEC_BATCH]), sb("m_den_own", [NSAMP, 1])
        n_decayed, n_new = sb("m_n_decayed", [P, DEC_BATCH]), sb("m_n_new", [P, DEC_BATCH])
        n_out, c_out = sb("m_n_out", [DEC_BATCH, HD_M]), sb("m_c_out", [P, HD_M])
        ps_p = [pb(f"m_ps_p{i}", [P, CHUNK]) for i in range(2)]
        ps_s, ps_k, ps_i, ps_n, ps_u, ps_h = [pb(f"m_ps_{n}", [P, CHUNK]) for n in "skinuh"]

        w_in0, w_in1, u_in, const_in, c_in, conv_dma0, conv_dma1, c_store, n_store, cp_store, np_store = sems.new(
            "m_w_in0", "m_w_in1", "m_u_in", "m_const_in", "m_c_in", "m_conv_dma0", "m_conv_dma1", "m_c_store", "m_n_store",
            "m_cp_store", "m_np_store")
        w_in, conv_dma = [w_in0, w_in1], [conv_dma0, conv_dma1]
        (w_hi_done, w_split, set_up, power_ready, hd_ready, u_ready, unit_ready, unit_kept, first_tap, taps_done, y_ready,
         th_ready, silu_done, last_ready, last_turned, conv_kept, rows_ready, rows_done, s_ready, kn_ready,
         in_ready, exp_done, sm_done, kn_done, wv_done, num_ready, upd_ready, state_done, inter_done, tot_done,
         den_done, rden_done, ss_done, msq_done, ms_done, rs_done, r_done, x_done, hn_done, ht_ready, mh_done,
         ml_done, ct_ready, ct_done_a, ct_done_v, it_ready, it_done, itt_ready, own_done, own_den_done,
         nt_ready, decayed, n_done, n_turned, n_kept, cs_done, fin_ready, fin_kept) = sems.new(
            "m_w_hi_done", "m_w_split", "m_set_up", "m_power_ready", "m_hd_ready", "m_u_ready", "m_unit_ready",
            "m_unit_kept", "m_first_tap", "m_taps_done", "m_y_ready", "m_th_ready", "m_silu_done", "m_last_ready",
            "m_last_turned", "m_conv_kept", "m_rows_ready", "m_rows_done", "m_s_ready", "m_kn_ready",
            "m_in_ready", "m_exp_done", "m_sm_done", "m_kn_done", "m_wv_done", "m_num_ready", "m_upd_ready",
            "m_state_done", "m_inter_done", "m_tot_done", "m_den_done", "m_rden_done", "m_ss_done",
            "m_msq_done", "m_ms_done", "m_rs_done", "m_r_done", "m_x_done", "m_hn_done", "m_ht_ready",
            "m_mh_done", "m_ml_done", "m_ct_ready", "m_ct_done_a", "m_ct_done_v", "m_it_ready", "m_it_done",
            "m_itt_ready", "m_own_done", "m_own_den_done", "m_nt_ready", "m_decayed", "m_n_done", "m_n_turned",
            "m_n_kept", "m_cs_done", "m_fin_ready", "m_fin_kept")

        def heads(engine, body):
            with engine.Fori(0, H_M - 1) as h:
                body(h, True)
            body(H_M - 1, False)

        with nc.Block() as block:
            @block.sync
            def _(sp):
                sp.dma_start(causal[:, :], g.causal).then_inc(const_in, 16)
                sp.dma_start(sample_causal[:, :], g.sample_causal).then_inc(const_in, 16)
                sp.dma_start(member[:, :], g.member).then_inc(const_in, 16)
                sp.dma_start(g.w_out_first[:, :], g.w_out[0:P, :]).then_inc(g.w_out_first_in, 16)
                with sp.Fori(0, H_M) as h:
                    def weights(i, col):
                        wait_before(sp, (const_in, 48), w_split, h * 4 + i + 1)
                        sp.dma_start(w_raw[i % 2][:, :, :], g.w_in[:, ds(h * P + col, P)]
                                     .rearrange("(k p) c -> p k c", p=P)).then_inc(w_in[i % 2], 16)
                    weights(0, COL_Q)
                    weights(1, COL_K)
                    wait_before(sp, (const_in, 48), exp_done, h * n_steps)
                    sp.dma_start(u[:, :], g.u_dram[ds(h, 1), :].to_broadcast([P, NTOK])).then_inc(u_in, 16)
                    weights(2, COL_V)
                    weights(3, COL_O)
                    wait_before(sp, (const_in, 48), c_store, h * 16)
                    sp.dma_start(c_state[:, :, :], g.state_C[:, ds(h, 1), :, :].rearrange("b h v k -> v (b h) k"))\
                        .then_inc(c_in, 16)

            @block.tensor
            def _(pe):
                def hold(sem, value):
                    wait_before(pe, (const_in, 48), sem, value)

                def head(h, more):
                    def unit(i, h=h):
                        j, (c0, n) = i // NC, CHUNKS[i % NC]
                        if i % NC == 0:
                            pe.wait_ge(w_split, 2 + h * 4 + j + 1)
                        if i < 2:
                            pe.wait_ge(cs_done, h * 2 if i else h * 2 - 1)
                        else:
                            pe.wait_ge(unit_kept, h * n_units + i - 1)
                        for kt in range(KT):
                            mm = product(nc.tensor, ps_p[i % 2][:, 0:n], w_hi[:, kt, j, :], w_lo[:, kt, j, :],
                                         g.act_hi[:, kt, c0:c0 + n], g.act_lo[:, kt, c0:c0 + n], kt == 0, kt == KT - 1)
                        mm.then_inc(unit_ready, 1)

                    def turn_last(j):
                        if j == 0:
                            hold(n_done, h)
                        else:
                            hold(n_kept, h)
                        hold(last_ready, h * 2 + j + 1)
                        n = HIST + DEC_BATCH * HIST
                        nc.tensor.transpose((ps_k, ps_h)[j][0:n, 0:P], last_rows[:, :], g.ident[:, :]).then_inc(last_turned, 1)

                    def rows(t, k0, k1):
                        n = P if t < TILES else NSAMP
                        if k0 == 0:
                            if t == 0:
                                pe.wait_ge(w_split, 2 + h * 4 + 4)
                            pe.wait_ge(*((rows_done, h * n_steps + t - 1) if t >= 2 else
                                         (unit_kept, h * n_units + 9 + t)))
                        for kt in range(k0, k1):
                            mm = product(nc.tensor, ps_p[t % 2][0:n, 0:2 * P], g.act_hi[:, kt, t * P:t * P + n],
                                         g.act_lo[:, kt, t * P:t * P + n], w_hi[:, kt, 2:4, :], w_lo[:, kt, 2:4, :],
                                         kt == 0, kt == KT - 1)
                        if k1 == KT:
                            mm.then_inc(rows_ready, 1)

                    def turn_h(t):
                        n = P if t < TILES else NSAMP
                        if t == 0:
                            hold(conv_kept, h * 2 + 2)
                        hold(ml_done, h * n_steps + t)
                        hold(hn_done, h * n_steps + t + 1)
                        nc.tensor.transpose(ps_h[:, 0:n], hn[t % 2][0:n, :], g.ident[0:n, 0:n]).then_inc(ht_ready, 1)

                    for i in range(1, n_units):
                        unit(i)
                        if i == NC + 2:
                            turn_last(0)
                    rows(0, 0, KT)
                    base = h * n_steps
                    for t in range(TILES):
                        s, here = t % 2, slice(t * P, (t + 1) * P)
                        if here.start % CHUNK == 0:
                            pe.wait_ge(silu_done, h * n_units + NC + here.start // CHUNK + 1)
                        if t == 0:
                            pe.wait_ge(fin_kept, h)
                            pe.wait_ge(conv_kept, h * 2 + 1)
                        pe.wait_ge(sm_done, base + t)
                        nc.tensor.matmul(ps_s[:, 0:P], k[:, here], q[:, here], start=True, stop=True).then_inc(s_ready, 1)
                        pe.wait_ge(kn_done, base + t)
                        nc.tensor.transpose(ps_k[:, 0:P], k[:, here], g.ident[:, :]).then_inc(kn_ready, 1)
                        pe.wait_ge(inter_done, base + t)
                        pe.wait_ge(state_done, h * (TILES + 1) + t + 1)
                        nc.tensor.matmul(ps_i[:, 0:HD_M + 1], q[:, here], state[:, :], start=True,
                                         stop=True).then_inc(in_ready, 1)
                        rows(t + 1, 0, KT // 2)
                        pe.wait_ge(sm_done, base + t + 1)
                        pe.wait_ge(tot_done, base + t)
                        nc.tensor.matmul(ps_n[:, 0:HD_M + 1], sm[s][:, :], v1[:, t % V_SLOTS, :], start=True,
                                         stop=True).then_inc(num_ready, 1)
                        pe.wait_ge(kn_done, base + t + 1)
                        pe.wait_ge(wv_done, base + t + 1)
                        nc.tensor.matmul(ps_u[:, 0:HD_M + 1], kn[s][:, :], wv[s][:, :], start=True,
                                         stop=True).then_inc(upd_ready, 1)
                        rows(t + 1, KT // 2, KT)
                        if t:
                            turn_h(t - 1)
                        else:
                            turn_last(1)
                    t, s = TILES, TILES % 2
                    q_s, k_s = q[:, SAMPLE:], k[:, SAMPLE:]
                    hold(silu_done, (h + 1) * n_units)
                    hold(sm_done, base + t)
                    hold(c_in, h * 16 + 16)
                    nc.tensor.matmul(ps_s[0:NSAMP, 0:NSAMP], k_s, q_s, start=True, stop=True).then_inc(s_ready, 1)
                    hold(kn_done, base + t)
                    nc.tensor.transpose(ps_k[0:NSAMP, 0:P], k_s, g.ident[:, :]).then_inc(kn_ready, 1)
                    hold(inter_done, base + t)
                    nc.tensor.matmul(ps_i[0:NSAMP, 0:DEC_BATCH], q_s, hd[:, TAB_N:], start=True, stop=True).then_inc(in_ready, 1)
                    hold(rows_done, base + t + 1)
                    for half in range(2):
                        for b in range(4):
                            mm = nc.tensor.transpose(ps_p[half][:, b * P:(b + 1) * P], c_state[:, half * 4 + b, :], g.ident[:, :])
                        mm.then_inc(ct_ready, 1)
                    hold(ct_done_a, h + 1)
                    hold(ct_done_v, h + 1)
                    hold(kn_done, base + t + 1)
                    hold(own_done, h + 1)
                    nc.tensor.matmul(ps_k[:, 0:DEC_BATCH], kn[s][0:NSAMP, :], own_w[:, :], start=True,
                                     stop=True).then_inc(nt_ready, 1)
                    for b in range(DEC_BATCH):
                        mm = nc.tensor.matmul(ps_p[b // 4][:, b % 4 * P:(b % 4 + 1) * P], own_wv[:, b, :], kn[s][0:NSAMP, :],
                                              start=True, stop=True)
                    mm.then_inc(upd_ready, 1)
                    hold(state_done, h * (TILES + 1) + TILES + 1)
                    for b in range(DEC_BATCH):
                        at = b * DEC_SEQ
                        mm = nc.tensor.matmul(ps_u[:, at:at + DEC_SEQ], c_turned[:, b, :], q_s[:, at:at + DEC_SEQ], start=True,
                                              stop=True)
                    mm.then_inc(it_ready, 1)
                    turn_h(TILES - 1)
                    hold(sm_done, base + t + 1)
                    hold(tot_done, base + t)
                    nc.tensor.matmul(ps_n[0:NSAMP, 0:HD_M + 1], sm[s][0:NSAMP, 0:NSAMP], v1[0:NSAMP, t % V_SLOTS, :], start=True,
                                     stop=True).then_inc(num_ready, 1)
                    hold(own_den_done, h * 2 + 1)
                    hold(it_done, h + 1)
                    nc.tensor.transpose(ps_i[0:NSAMP, P:2 * P], inter_t[:, :], g.ident[:, :]).then_inc(itt_ready, 1)
                    nc.tensor.transpose(ps_s[:, 0:P], state[:, 0:HD_M], g.ident[:, :]).then_inc(fin_ready, 1)
                    if more:
                        unit(0, h + 1)
                    turn_h(TILES)
                    hold(ml_done, base + t + 1)
                    hold(n_done, h + 1)
                    nc.tensor.transpose(ps_h[0:DEC_BATCH, 0:P], n_new[:, :], g.ident[:, :]).then_inc(n_turned, 1)

                pe.wait_ge(w_split, 2 + 1)
                for kt in range(KT):
                    mm = product(nc.tensor, ps_p[0][:, :], w_hi[:, kt, 0, :], w_lo[:, kt, 0, :], g.act_hi[:, kt, 0:CHUNK],
                                 g.act_lo[:, kt, 0:CHUNK], kt == 0, kt == KT - 1)
                mm.then_inc(unit_ready, 1)
                heads(pe, head)

            @block.scalar
            def _(act):
                def split(h, i, quarters=range(4)):
                    act.wait_ge(w_in[i % 2], (h * 2 + i // 2 + 1) * 16)
                    for q in quarters:
                        part = slice(q * KT // 4, (q + 1) * KT // 4)
                        nc.scalar.activation(w_hi[:, part, i, :], w_raw[i % 2][:, part, :], ACT.Copy).then_inc(w_hi_done, 1)

                def head(h, more):
                    base = h * n_steps

                    def keep_unit(i):
                        j, c = i // NC, i % NC
                        act.wait_ge(unit_ready, h * n_units + i + 1)
                        act.wait_ge(y_ready, h * n_units + max(i - 1, 0))
                        if c == NC - 1:
                            nc.scalar.activation(zs[:, :, HIST:], ps_p[i % 2][:, 0:NSAMP]
                                                 .rearrange("p (b t) -> p b t", b=DEC_BATCH), ACT.Copy).then_inc(unit_kept, 1)
                            return
                        if c == 0:
                            nc.scalar.activation(z[0][:, 0:HIST], no_past[:, :], ACT.Copy)
                        else:
                            act.wait_ge(unit_kept, h * n_units + i)
                            nc.scalar.activation(z[c % 2][:, 0:HIST], z[1 - c % 2][:, CHUNK:], ACT.Copy)
                        nc.scalar.activation(z[c % 2][:, HIST:], ps_p[i % 2][:, :], ACT.Copy).then_inc(unit_kept, 1)
                        act.wait_ge(unit_kept, h * n_units + i + 1)
                        act.wait_ge(silu_done, h * n_units + max(i - 1, 0))
                        nc.scalar.activation(y[i % 2][:, :], z[c % 2][:, 0:CHUNK], ACT.Copy,
                                             scale=hd[:, TAB_CONV + j * CONV_W:TAB_CONV + j * CONV_W + 1])\
                            .then_inc(first_tap, 1)

                    def tanh_unit(i):
                        j, n = i // NC, CHUNKS[i % NC][1]
                        act.wait_ge(y_ready, h * n_units + i + 1)
                        act.wait_ge(silu_done, h * n_units + max(i - 1, 0))
                        nc.scalar.activation(th[i % 2][:, 0:n], y[i % 2][:, 0:n], ACT.Tanh,
                                             scale=1.0 if j == 0 else 1.0 / K_SCALE).then_inc(th_ready, 1)

                    def keep_last(j):
                        act.wait_ge(last_turned, h * 2 + j + 1)
                        act.wait_ge(conv_dma[j], h * 32)
                        n = HIST + DEC_BATCH * HIST
                        nc.scalar.activation(conv_out[j][:, :], (ps_k, ps_h)[j][0:n, 0:P], ACT.Copy).then_inc(conv_kept, 1)

                    def keep_rows(t):
                        n = P if t < TILES else NSAMP
                        act.wait_ge(rows_ready, base + t + 1)
                        act.wait_ge(hn_done, base + max(t - V_SLOTS + 1, 0))
                        nc.scalar.activation(v1[0:n, t % V_SLOTS, 0:HD_M], ps_p[t % 2][0:n, 0:P], ACT.Copy)
                        nc.scalar.activation(o_tanh[0:n, t % V_SLOTS, :], ps_p[t % 2][0:n, P:2 * P], ACT.Tanh,
                                             scale=0.5).then_inc(rows_done, 1)

                    def exponential(t):
                        n = P if t < TILES else NSAMP
                        act.wait_ge(u_ready, h + 1)
                        act.wait_ge(sm_done, base + max(t - 1, 0))
                        nc.scalar.activation(expd[t % 2][0:n, 0:n], u[0:n, t * P:t * P + n], ACT.Exp,
                                             bias=hd[0:n, t * TAB_SIZE:t * TAB_SIZE + 1]).then_inc(exp_done, 1)

                    def scale_inter(t):
                        n = P if t < TILES else NSAMP
                        width = HD_M + 1 if t < TILES else HD_M
                        at = 0 if t < TILES else P
                        act.wait_ge(*((in_ready, base + t + 1) if t < TILES else (itt_ready, h + 1)))
                        act.wait_ge(tot_done, base + max(t - 1, 0))
                        col = t * TAB_SIZE + 2
                        nc.scalar.activation(inter[t % 2][0:n, 0:width], ps_i[0:n, at:at + width], ACT.Copy,
                                             scale=hd[0:n, col:col + 1]).then_inc(inter_done, 1)

                    def sum_squares(t):
                        n = P if t < TILES else NSAMP
                        act.wait_ge(tot_done, base + t + 1)
                        act.wait_ge(msq_done, base + max(t - 1, 0))
                        act.wait_ge(ss_done, base + t)
                        nc.scalar.activation(squares[0:n, :], tot[t % 2][0:n, 0:HD_M], ACT.Square,
                                             accum_out=ss[t % 2][0:n, :]).then_inc(ss_done, 1)

                    def normalise(t):
                        n = P if t < TILES else NSAMP
                        act.wait_ge(r_done, base + t + 1)
                        act.wait_ge(hn_done, base + max(t - 1, 0))
                        nc.scalar.activation(x[t % 2][0:n, :], tot[t % 2][0:n, 0:HD_M], ACT.Copy,
                                             scale=r[t % 2][0:n, 0:1]).then_inc(x_done, 1)

                    def keep_h(t):
                        n = P if t < TILES else NSAMP
                        act.wait_ge(ht_ready, base + t + 1)
                        nc.scalar.activation(g.mix_m_hi[:, ds(h * NTOK + t * P, n)], ps_h[:, 0:n], ACT.Copy,
                                             scale=hd[:, TAB_GAIN:TAB_GAIN + 1]).then_inc(mh_done, 1)

                    act.wait_ge(hd_ready, h + 1)
                    for i in range(n_units):
                        keep_unit(i)
                        if i:
                            tanh_unit(i - 1)
                        if i in (2, 4):
                            split(h, i // 2 + 1)
                        if i == NC + 3:
                            keep_last(0)
                    tanh_unit(n_units - 1)
                    act.wait_ge(set_up, 2)
                    keep_rows(0)
                    for t in range(TILES):
                        exponential(t)
                        scale_inter(t)
                        if t:
                            normalise(t - 1)
                        keep_rows(t + 1)
                        sum_squares(t)
                        if t:
                            keep_h(t - 1)
                        else:
                            keep_last(1)
                        if more and t in range(4, 12):
                            split(h + 1, t // 4 - 1, [t % 4])
                    t = TILES
                    exponential(t)
                    normalise(t - 1)
                    act.wait_ge(ct_ready, h * 2 + 1)
                    nc.scalar.activation(c_turned[:, 0:4, :], ps_p[0][:, :].rearrange("p (b k) -> p b k", b=4),
                                         ACT.Copy).then_inc(ct_done_a, 1)
                    keep_h(t - 1)
                    act.wait_ge(it_ready, h + 1)
                    nc.scalar.activation(inter_t[:, :], ps_u[:, 0:NSAMP], ACT.Copy).then_inc(it_done, 1)
                    scale_inter(t)
                    sum_squares(t)
                    act.wait_ge(fin_ready, h + 1)
                    act.wait_ge(cp_store, h * 16)
                    nc.scalar.activation(c_out[:, :], ps_s[:, 0:P], ACT.Copy).then_inc(fin_kept, 1)
                    normalise(t)
                    keep_h(t)
                    act.wait_ge(n_turned, h + 1)
                    act.wait_ge(n_store, h * 16)
                    nc.scalar.activation(n_out[:, :], ps_h[0:DEC_BATCH, 0:P], ACT.Copy).then_inc(n_kept, 1)

                split(0, 0)
                split(0, 1)
                heads(act, head)

            @block.gpsimd
            def _(pool):
                nc.gpsimd.memset(power[:, :], -0.5).then_inc(power_ready, 1)
                pool.wait_ge(power_ready, 1)
                with pool.Fori(0, H_M) as h:
                    base = h * n_steps
                    for j in range(2):
                        wait_before(pool, (power_ready, 1), conv_kept, h * 2 + j + 1)
                        cols = ds(h * P + j * D_M, P)
                        pool.dma_start(g.conv_prompt[:, cols], conv_out[j][0:HIST, :]).then_inc(conv_dma[j], 16)
                        pool.dma_start(g.conv_sample[:, cols], conv_out[j][HIST:, :]).then_inc(conv_dma[j], 16)
                    for t in range(n_steps):
                        n, s = (P if t < TILES else NSAMP), t % 2
                        wait_before(pool, (power_ready, 1), rs_done, base + max(t - 1, 0))
                        wait_before(pool, (power_ready, 1), msq_done, base + t + 1)
                        nc.gpsimd.tensor_scalar(ms[s][0:n, :], msq[s][0:n, :], 1.0 / HD_M, EPS, ALU.mult,
                                                ALU.add).then_inc(ms_done, 1)
                        pool.wait_ge(ms_done, base + t + 1)
                        pool.wait_ge(r_done, base + max(t - 1, 0))
                        nc.gpsimd.tensor_tensor(rs[s][0:n, :], ms[s][0:n, :], power[0:n, :], ALU.pow).then_inc(rs_done, 1)
                        pool.wait_ge(rs_done, base + t + 1)
                        pool.wait_ge(x_done, base + max(t - 1, 0))
                        nc.gpsimd.tensor_tensor(r[s][0:n, :], rs[s][0:n, :], rden[s][0:n, :], ALU.mult).then_inc(r_done, 1)
                    wait_before(pool, (power_ready, 1), fin_kept, h + 1)
                    pool.dma_start(g.C_prompt[ds(h, 1), :, :].rearrange("h v k -> (h v) k"), c_out[:, :]).then_inc(cp_store, 16)
                    with nc.allow_non_contiguous_dma(reason="one column of 128 numbers"):
                        pool.dma_start(g.n_prompt[ds(h, 1), :].rearrange("h k -> k h"), state[:, HD_M:]).then_inc(np_store, 16)
                    wait_before(pool, (power_ready, 1), cs_done, h * 2 + 2)
                    pool.dma_start(g.C_sample[:, ds(h, 1), :, :].rearrange("b h v k -> v (b h) k"),
                                   c_state[:, :, :]).then_inc(c_store, 16)
                    wait_before(pool, (power_ready, 1), n_kept, h + 1)
                    pool.dma_start(g.n_sample[:, ds(h, 1), :].rearrange("b h k -> (b h) k"), n_out[:, :]).then_inc(n_store, 16)
                for sem, n in ((cp_store, 1), (np_store, 1), (n_store, 1), (c_store, 1), (conv_dma0, 2), (conv_dma1, 2)):
                    pool.wait_ge(sem, H_M * n * 16)

            @block.vector
            def _(dve):
                nc.vector.memset(no_past[:, :], 0.0)
                nc.vector.memset(v1[:, :, HD_M:], 1.0).then_inc(set_up, 1)
                nc.vector.memset(last_rows[:, :], 0.0).then_inc(set_up, 1)
                dve.wait_ge(const_in, 48)
                dve.wait_ge(set_up, 2)
                dve.sem_inc(w_split, 2)

                def split(h, i, quarters=range(4)):
                    for q in quarters:
                        part = slice(q * KT // 4, (q + 1) * KT // 4)
                        dve.wait_ge(w_hi_done, (h * 4 + i) * 4 + q + 1)
                        ins = nc.vector.tensor_tensor(w_lo[:, part, i, :], w_raw[i % 2][:, part, :], w_hi[:, part, i, :],
                                                      ALU.subtract)
                        if q == 3:
                            ins.then_inc(w_split, 1)

                def head(h, more):
                    base = h * n_steps

                    def convolve(i):
                        j, c = i // NC, i % NC
                        (c0, n), at = CHUNKS[c], h * n_units + i
                        dve.wait_ge(unit_kept, at + 1)
                        dve.wait_ge(silu_done, h * n_units + max(i - 1, 0))
                        out = y[i % 2][:, 0:n]
                        if c == NC - 1:
                            dve.wait_ge(last_turned, h * 2 + j)
                            col = TAB_HIST + j * DEC_BATCH * HIST
                            nc.vector.tensor_copy(zs[:, :, 0:HIST], hd[:, col:col + DEC_BATCH * HIST]
                                                  .rearrange("p (b r) -> p b r", b=DEC_BATCH)).then_inc(taps_done, 1)
                            nc.vector.tensor_copy(last_rows[:, 0:HIST], z[(NC - 2) % 2][:, CHUNK:])
                            nc.vector.tensor_copy(last_rows[:, HIST:].rearrange("p (b r) -> p b r", b=DEC_BATCH),
                                                  zs[:, :, DEC_SEQ:]).then_inc(last_ready, 1)
                            out = out.rearrange("p (b t) -> p b t", b=DEC_BATCH)
                        own_taps = range(1 if c < NC - 1 else 0, CONV_W)
                        taps_at = (h * 2 + j) * ((NC - 1) * (CONV_W - 2) + CONV_W) + c * (CONV_W - 2) + (c == NC - 1)
                        if c == NC - 1:
                            dve.wait_ge(taps_done, taps_at)
                        else:
                            dve.wait_ge(first_tap, (h * 2 + j) * (NC - 1) + c + 1)
                        for made, tap in enumerate(own_taps):
                            src = z[c % 2][:, tap:tap + n] if c < NC - 1 else zs[:, :, tap:tap + DEC_SEQ]
                            w = hd[:, TAB_CONV + j * CONV_W + tap:TAB_CONV + j * CONV_W + tap + 1]
                            if tap == 0:
                                ins = nc.vector.tensor_scalar(out, src, w, None, ALU.mult)
                            else:
                                if made:
                                    dve.wait_ge(taps_done, taps_at + made)
                                ins = nc.vector.scalar_tensor_tensor(out, src, w, out, ALU.mult, ALU.add)
                            if tap < CONV_W - 1:
                                ins.then_inc(taps_done, 1)
                        ins.then_inc(y_ready, 1)

                    def silu(i):
                        j, (c0, n) = i // NC, CHUNKS[i % NC]
                        dve.wait_ge(th_ready, h * n_units + i + 1)
                        nc.vector.scalar_tensor_tensor(qk[j][:, c0:c0 + n], th[i % 2][:, 0:n], 1.0, y[i % 2][:, 0:n], ALU.add,
                                                       ALU.mult).then_inc(silu_done, 1)

                    def total(t):
                        n, s = (P if t < TILES else NSAMP), t % 2
                        dve.wait_ge(inter_done, base + t + 1)
                        dve.wait_ge(num_ready, base + t + 1)
                        dve.wait_ge(x_done, base + max(t - 1, 0))
                        nc.vector.tensor_tensor(tot[s][0:n, :], ps_n[0:n, 0:HD_M + 1], inter[s][0:n, :],
                                                ALU.add).then_inc(tot_done, 1)
                        dve.wait_ge(tot_done, base + t + 1)
                        dve.wait_ge(rden_done, base + max(t - 1, 0))
                        col = t * TAB_SIZE + 3
                        nc.vector.scalar_tensor_tensor(den[s][0:n, :], tot[s][0:n, HD_M:], -1.0, hd[0:n, col:col + 1],
                                                       ALU.mult, ALU.max).then_inc(den_done, 1)
                        dve.wait_ge(den_done, (base + t) * 2 + 1)
                        nc.vector.tensor_tensor(den[s][0:n, :], den[s][0:n, :], tot[s][0:n, HD_M:],
                                                ALU.max).then_inc(den_done, 1)
                        dve.wait_ge(den_done, (base + t) * 2 + 2)
                        dve.wait_ge(r_done, base + max(t - 1, 0))
                        nc.vector.reciprocal(rden[s][0:n, :], den[s][0:n, :]).then_inc(rden_done, 1)

                    def mean_square(t):
                        n, s = (P if t < TILES else NSAMP), t % 2
                        dve.wait_ge(rden_done, base + t + 1)
                        dve.wait_ge(ss_done, base + t + 1)
                        dve.wait_ge(ms_done, base + max(t - 1, 0))
                        nc.vector.scalar_tensor_tensor(msq[s][0:n, :], ss[s][0:n, :], rden[s][0:n, 0:1], rden[s][0:n, :],
                                                       ALU.mult, ALU.mult).then_inc(msq_done, 1)

                    def gate_output(t):
                        n, s = (P if t < TILES else NSAMP), t % 2
                        dve.wait_ge(x_done, base + t + 1)
                        dve.wait_ge(ht_ready, base + max(t - 1, 0))
                        dve.wait_ge(rows_done, base + t + 1)
                        nc.vector.scalar_tensor_tensor(hn[s][0:n, :], o_tanh[0:n, t % V_SLOTS, :], 1.0, x[s][0:n, :], ALU.add,
                                                       ALU.mult).then_inc(hn_done, 1)

                    def keep_low(t):
                        n = P if t < TILES else NSAMP
                        dve.wait_ge(mh_done, base + t + 1)
                        at = ds(h * NTOK + t * P, n)
                        nc.vector.scalar_tensor_tensor(g.mix_m_lo[:, at], ps_h[:, 0:n], hd[:, TAB_GAIN:TAB_GAIN + 1],
                                                       g.mix_m_hi[:, at], ALU.mult, ALU.subtract).then_inc(ml_done, 1)

                    def weigh(t):
                        n, s = (P if t < TILES else NSAMP), t % 2
                        dve.wait_ge(s_ready, base + t + 1)
                        dve.wait_ge(exp_done, base + t + 1)
                        dve.wait_ge(num_ready, base + max(t - 1, 0))
                        nc.vector.tensor_tensor(sm[s][0:n, 0:n], ps_s[0:n, 0:n], expd[s][0:n, 0:n], ALU.mult).then_inc(sm_done, 1)
                        dve.wait_ge(kn_ready, base + t + 1)
                        dve.wait_ge(upd_ready, base + max(t - 1, 0))
                        nc.vector.tensor_copy(kn[s][0:n, :], ps_k[0:n, 0:P]).then_inc(kn_done, 1)

                    dve.wait_ge(ml_done, base)
                    dve.wait_ge(cs_done, h * 2)
                    dve.wait_ge(n_kept, h)
                    nc.vector.tensor_copy(hd[:, :], g.table[:, ds(h, 1), :].rearrange("p h c -> p (h c)")).then_inc(hd_ready, 1)
                    dve.wait_ge(np_store, h * 16)
                    dve.wait_ge(fin_ready, h)
                    nc.vector.memset(state[:, :], 0.0).then_inc(state_done, 1)
                    dve.wait_ge(hd_ready, h + 1)
                    for i in range(n_units):
                        convolve(i)
                        if i:
                            silu(i - 1)
                        if i in (2, 4):
                            split(h, i // 2 + 1)
                        if i == NC:
                            dve.wait_ge(u_in, h * 16 + 16)
                            up = u[:, 0:SEQ].rearrange("p (t n) -> p t n", n=P)
                            nc.vector.tensor_tensor(up, up, causal[:, :].unsqueeze(1).to_broadcast([P, TILES, P]), ALU.add)
                            nc.vector.tensor_tensor(u[0:NSAMP, SAMPLE:], u[0:NSAMP, SAMPLE:], sample_causal[:, :],
                                                    ALU.add).then_inc(u_ready, 1)
                    silu(n_units - 1)
                    for t in range(TILES):
                        s = t % 2
                        weigh(t)
                        dve.wait_ge(rows_done, base + t + 1)
                        col = t * TAB_SIZE + 1
                        nc.vector.tensor_scalar(wv[s][:, :], v1[:, t % V_SLOTS, :], hd[:, col:col + 1], None,
                                                ALU.mult).then_inc(wv_done, 1)
                        if t:
                            gate_output(t - 1)
                        dve.wait_ge(upd_ready, base + t + 1)
                        dve.wait_ge(in_ready, base + t + 1)
                        dve.wait_ge(state_done, h * (TILES + 1) + t + 1)
                        nc.vector.scalar_tensor_tensor(state[:, :], state[:, :], hd[:, TAB_DECAY + t:TAB_DECAY + t + 1],
                                                       ps_u[:, 0:HD_M + 1], ALU.mult, ALU.add).then_inc(state_done, 1)
                        total(t)
                        mean_square(t)
                        if t:
                            keep_low(t - 1)
                        if more and t in range(4, 12):
                            split(h + 1, t // 4 - 1, [t % 4])
                    t, s = TILES, TILES % 2
                    dve.wait_ge(rows_done, base + t + 1)
                    col = t * TAB_SIZE + 1
                    nc.vector.tensor_scalar(own_w[:, :], member[:, :], hd[0:NSAMP, col:col + 1], None,
                                            ALU.mult).then_inc(wv_done, 1)
                    dve.wait_ge(wv_done, base + t + 1)
                    nc.vector.tensor_tensor(own_wv[:, :, :],
                                            v1[0:NSAMP, t % V_SLOTS:t % V_SLOTS + 1, 0:HD_M].to_broadcast([NSAMP, DEC_BATCH, HD_M]),
                                            own_w[:, :].unsqueeze(2).to_broadcast([NSAMP, DEC_BATCH, HD_M]),
                                            ALU.mult).then_inc(own_done, 1)
                    weigh(t)
                    dve.wait_ge(ct_ready, h * 2 + 2)
                    nc.vector.tensor_copy(c_turned[:, 4:, :], ps_p[1][:, :].rearrange("p (b k) -> p b k", b=4))\
                        .then_inc(ct_done_v, 1)
                    gate_output(t - 1)
                    dve.wait_ge(in_ready, base + t + 1)
                    nc.vector.tensor_tensor_reduce(den_all[:, :], ps_i[0:NSAMP, 0:DEC_BATCH], member[:, :], 1.0, 0.0, ALU.mult,
                                                   ALU.add, den_own[:, :]).then_inc(own_den_done, 1)
                    dve.wait_ge(own_den_done, h * 2 + 1)
                    nc.vector.tensor_scalar(inter[s][0:NSAMP, HD_M:], den_own[:, :], hd[0:NSAMP, col + 1:col + 2], None,
                                            ALU.mult).then_inc(own_den_done, 1)
                    nc.vector.tensor_tensor(n_decayed[:, :], hd[:, TAB_N:], hd[:, TAB_DECAY + TILES:TAB_DECAY + SEGMENTS],
                                            ALU.mult).then_inc(decayed, 1)
                    dve.wait_ge(decayed, h + 1)
                    dve.wait_ge(nt_ready, h + 1)
                    nc.vector.tensor_tensor(n_new[:, :], ps_k[:, 0:DEC_BATCH], n_decayed[:, :], ALU.add).then_inc(n_done, 1)
                    dve.wait_ge(upd_ready, base + t + 1)
                    for b in range(DEC_BATCH):
                        at = TAB_DECAY + TILES + b
                        last = nc.vector.scalar_tensor_tensor(c_state[:, b, :], c_state[:, b, :], hd[:, at:at + 1],
                                                              ps_p[b // 4][:, b % 4 * P:(b % 4 + 1) * P], ALU.mult, ALU.add)
                        if b % 4 == 3:
                            last.then_inc(cs_done, 1)
                    keep_low(t - 1)
                    dve.wait_ge(own_den_done, h * 2 + 2)
                    total(t)
                    mean_square(t)
                    gate_output(t)
                    keep_low(t)

                split(0, 0)
                split(0, 1)
                heads(dve, head)


def token_rows(prompt, sample, t, n):
    return prompt[ds(t * P, P), :] if n == P else sample


def stage_mix_out(nc, g, sems):
    HALVES = D_MODEL // CHUNK
    with ExitStack() as ctx:
        sb = lambda n, s, d=F32: ctx.enter_context(nc.sbuf_tensor(n, s, d))
        two = lambda n, s, d=F32: [sb(f"{n}{i}", s, d) for i in range(2)]
        mix_a = [sb("o_mix_a_hi", [P, PAIRS * NTOK], BF16), sb("o_mix_a_lo", [P, PAIRS * NTOK], BF16)]
        w_hi, w_lo = sb("o_w_hi", [P, KT, D_MODEL], BF16), sb("o_w_lo", [P, KT, D_MODEL], BF16)
        gain_post, gain_pre = sb("o_gain_post", [P, D_MODEL]), sb("o_gain_pre", [P, D_MODEL])
        x, x1, xn = two("o_x", [P, D_MODEL]), two("o_x1", [P, D_MODEL]), two("o_xn", [P, D_MODEL])
        raw = [g.w_out_first] + x1 + xn
        power = sb("o_power", [P, 1])
        ss_y, ms_y, rstd_y, ss_x, ms_x, rstd_x = [two(f"o_{n}", [P, 1]) for n in
                                                  ("ss_y", "ms_y", "rstd_y", "ss_x", "ms_x", "rstd_x")]
        ps_y = [ctx.enter_context(nc.psum_tensor(f"o_ps_y{i}", [P, D_MODEL], F32)) for i in range(2)]
        turned = [ctx.enter_context(nc.psum_tensor(f"o_turned{i}", [P, KT, P], F32)) for i in range(2)]
        (x_in0, x_in1, raw_in1, raw_in2, raw_in3, raw_in4, mix_in, mix_rest_in, gain_in, store0, store1,
         w_hi_done, w_split, power_ready, y_ready, y_free,
         ss_y_done, ms_y_done, rstd_y_done, scaled, x1_done, ss_x_done, ms_x_done, rstd_x_done, xn_done, turned_ready,
         hi_done, turned_free) = sems.new(
            "o_x_in0", "o_x_in1", "o_raw_in1", "o_raw_in2", "o_raw_in3", "o_raw_in4", "o_mix_in", "o_mix_rest_in", "o_gain_in",
            "o_store0", "o_store1", "o_w_hi_done",
            "o_w_split", "o_power_ready", "o_y_ready", "o_y_free", "o_ss_y_done", "o_ms_y_done", "o_rstd_y_done",
            "o_scaled", "o_x1_done", "o_ss_x_done", "o_ms_x_done", "o_rstd_x_done", "o_xn_done", "o_turned_ready",
            "o_hi_done", "o_turned_free")
        x_in, raw_in, store = [x_in0, x_in1], [g.w_out_first_in, raw_in1, raw_in2, raw_in3, raw_in4], [store0, store1]
        mix_hi = lambda k, t, n: (g.mix_m_hi[:, ds(k * NTOK + t * P, n)] if k < H_M else
                                  mix_a[0][:, ds((k - H_M) * NTOK + t * P, n)])
        mix_lo = lambda k, t, n: (g.mix_m_lo[:, ds(k * NTOK + t * P, n)] if k < H_M else
                                  mix_a[1][:, ds((k - H_M) * NTOK + t * P, n)])

        with nc.Block() as block:
            @block.sync
            def _(sp):
                mix = [m[:, :].rearrange("p (q n) -> p q n", q=PAIRS) for m in mix_a]
                mix_dram = g.mix_a_dram.rearrange("i p (q n) -> i p q n", q=PAIRS)
                for k in range(1, KT):
                    if k >= len(raw):
                        sp.wait_ge(w_split, k - len(raw) + 1)
                    sp.dma_start(raw[k % len(raw)][:, :], g.w_out[k * P:(k + 1) * P, :]).then_inc(raw_in[k % len(raw)], 16)
                    if k == len(raw) - 1:
                        for part in range(2):
                            sp.dma_start(mix[part][:, :, 0:2 * P], mix_dram[part, :, :, 0:2 * P]).then_inc(mix_in, 16)
                sp.dma_start(x[0][:, :], g.x_prompt[0:P, :]).then_inc(x_in[0], 16)
                sp.dma_start(gain_post[:, :], g.g_mix_post.to_broadcast([P, D_MODEL])).then_inc(gain_in, 16)
                sp.dma_start(gain_pre[:, :], g.g_ffn_pre.to_broadcast([P, D_MODEL])).then_inc(gain_in, 16)
                sp.dma_start(x[1][:, :], g.x_prompt[P:2 * P, :]).then_inc(x_in[1], 16)
                for part in range(2):
                    sp.dma_start(mix[part][:, :, 2 * P:], mix_dram[part, :, :, 2 * P:]).then_inc(mix_rest_in, 16)
                sp.wait_ge(gain_in, 32)

                def move(t, s, n, more):
                    wait_before(sp, (gain_in, 32), x1_done, t + 1)
                    sp.dma_start(token_rows(g.x1_dram[0:SEQ, :], g.x1_dram[SEQ:, :], t, n), x1[s][0:n, :]).then_inc(store[s], 16)
                    if more == P:
                        sp.dma_start(x[s][:, :], g.x_prompt[ds((t + 2) * P, P), :]).then_inc(x_in[s], 16)
                    elif more:
                        sp.dma_start(x[s][0:NSAMP, :], g.x_sample).then_inc(x_in[s], 16)

                with sp.Fori(0, TILES // 2 - 1) as pair:
                    for s in range(2):
                        move(pair * 2 + s, s, P, P)
                move(TILES - 2, 0, P, NSAMP)
                move(TILES - 1, 1, P, 0)
                move(TILES, 0, NSAMP, 0)
                sp.wait_ge(store[0], (TILES // 2 + 1) * 16)
                sp.wait_ge(store[1], TILES // 2 * 16)

            @block.tensor
            def _(pe):

                def turn(t, s, n):
                    wait_before(pe, (w_split, KT), xn_done, t + 1)
                    wait_before(pe, (w_split, KT), turned_free, t + 1)
                    for k in range(KT):
                        mm = nc.tensor.transpose(turned[s][:, k, 0:n], xn[s][0:n, k * P:(k + 1) * P], g.ident[0:n, 0:n])
                    mm.then_inc(turned_ready, 1)

                def step(t, s, n, nth, first):
                    pe.wait_ge(y_free, t + 1)
                    for k in range(KT):
                        if first:
                            pe.wait_ge(w_split, k + 1)
                            if k == H_M:
                                pe.wait_ge(mix_in, 32)
                        for half in range(HALVES):
                            cols = slice(half * CHUNK, (half + 1) * CHUNK)
                            mm = product(nc.tensor, ps_y[s][0:n, cols], mix_hi(k, t, n), mix_lo(k, t, n), w_hi[:, k, cols],
                                         w_lo[:, k, cols], k == 0, k == KT - 1)
                    mm.then_inc(y_ready, 1)
                    if not first:
                        turn(t - 1, 1 - s, P)
                        if isinstance(nth, int) and nth == 0:
                            pe.wait_ge(mix_rest_in, 32)
                token_tiles_in_turn(pe, step)
                turn(TILES, 0, NSAMP)

            @block.scalar
            def _(act):
                for k in range(KT):
                    act.wait_ge(raw_in[k % len(raw)], (k // len(raw) + 1) * 16)
                    nc.scalar.activation(w_hi[:, k, :], raw[k % len(raw)][:, :], ACT.Copy).then_inc(w_hi_done, 1)

                def keep_high(t, s, n):
                    act.wait_ge(turned_ready, t + 1)
                    nc.scalar.activation(g.act_hi[:, :, ds(t * P, n)], turned[s][:, :, 0:n], ACT.Copy).then_inc(hi_done, 1)

                def step(t, s, n, nth, first):
                    act.wait_ge(y_ready, t + 1)
                    act.wait_ge(store[s], nth * 16)
                    nc.scalar.activation(x1[s][0:n, :], ps_y[s][0:n, :], ACT.Square,
                                         accum_out=ss_y[s][0:n, :]).then_inc(ss_y_done, 1)
                    if not first:
                        keep_high(t - 1, 1 - s, P)
                    act.wait_ge(x1_done, t + 1)
                    nc.scalar.activation(xn[s][0:n, :], x1[s][0:n, :], ACT.Square,
                                         accum_out=ss_x[s][0:n, :]).then_inc(ss_x_done, 1)
                token_tiles_in_turn(act, step)
                keep_high(TILES, 0, NSAMP)

            @block.gpsimd
            def _(pool):
                nc.gpsimd.memset(power[:, :], -0.5).then_inc(power_ready, 1)
                pool.wait_ge(power_ready, 1)

                def step(t, s, n, nth, first):
                    for ss, ms, rstd, given, half_way, done in ((ss_y, ms_y, rstd_y, ss_y_done, ms_y_done, rstd_y_done),
                                                                (ss_x, ms_x, rstd_x, ss_x_done, ms_x_done, rstd_x_done)):
                        wait_before(pool, (power_ready, 1), given, t + 1)
                        nc.gpsimd.tensor_scalar(ms[s][0:n, :], ss[s][0:n, :], 1.0 / D_MODEL, EPS, ALU.mult,
                                                ALU.add).then_inc(half_way, 1)
                        pool.wait_ge(half_way, t + 1)
                        nc.gpsimd.tensor_tensor(rstd[s][0:n, :], ms[s][0:n, :], power[0:n, :], ALU.pow).then_inc(done, 1)
                token_tiles_in_turn(pool, step)

            @block.vector
            def _(dve):
                dve.sem_inc(y_free, 2)
                dve.sem_inc(turned_free, 2)
                for k in range(KT):
                    dve.wait_ge(w_hi_done, k + 1)
                    nc.vector.tensor_tensor(w_lo[:, k, :], raw[k % len(raw)][:, :], w_hi[:, k, :],
                                            ALU.subtract).then_inc(w_split, 1)
                dve.wait_ge(gain_in, 32)

                def keep_low(t, s, n):
                    dve.wait_ge(hi_done, t + 1)
                    cols = ds(t * P, n)
                    nc.vector.tensor_tensor(g.act_lo[:, :, cols], turned[s][:, :, 0:n], g.act_hi[:, :, cols],
                                            ALU.subtract).then_inc(turned_free, 1)

                def step(t, s, n, nth, first):
                    dve.wait_ge(rstd_y_done, t + 1)
                    nc.vector.scalar_tensor_tensor(x1[s][0:n, :], ps_y[s][0:n, :], rstd_y[s][0:n, 0:1], gain_post[0:n, :],
                                                   ALU.mult, ALU.mult).then_inc(y_free, 1)
                    dve.wait_ge(x_in[s], (nth + 1) * 16)
                    dve.wait_ge(y_free, t + 3)
                    nc.vector.tensor_tensor(x1[s][0:n, :], x1[s][0:n, :], x[s][0:n, :], ALU.add).then_inc(x1_done, 1)
                    if not first:
                        keep_low(t - 1, 1 - s, P)
                    dve.wait_ge(rstd_x_done, t + 1)
                    nc.vector.scalar_tensor_tensor(xn[s][0:n, :], x1[s][0:n, :], rstd_x[s][0:n, 0:1], gain_pre[0:n, :],
                                                   ALU.mult, ALU.mult).then_inc(xn_done, 1)
                token_tiles_in_turn(dve, step)
                keep_low(TILES, 0, NSAMP)


HIDDEN_TILES = D_FF // P
PARTS = [4, 6, 6, 6]
PART_MAX = max(PARTS)
assert sum(PARTS) == HIDDEN_TILES and all(n % 2 == 0 for n in PARTS)


def stage_ffn(nc, g, sems):
    HALVES = D_MODEL // CHUNK
    n_down = TILES + 1
    firsts = [sum(PARTS[:i]) for i in range(len(PARTS))]
    LAST = len(PARTS) - 1
    with ExitStack() as ctx:
        sb = lambda n, s, d=F32: ctx.enter_context(nc.sbuf_tensor(n, s, d))
        two = lambda n, s, d=F32: [sb(f"{n}{i}", s, d) for i in range(2)]
        raw = [sb(f"f_raw_{n}", [P, D_MODEL]) for n in ("gate", "up", "down")]
        w_hi = [two(f"f_w_hi_{s}_", [P, KT, P], BF16) for s in range(2)]
        w_lo = [two(f"f_w_lo_{s}_", [P, KT, P], BF16) for s in range(2)]
        down_hi, down_lo = sb("f_down_hi", [P, PART_MAX, D_MODEL], BF16), sb("f_down_lo", [P, PART_MAX, D_MODEL], BF16)
        h_hi, h_lo = sb("f_h_hi", [P, PART_MAX * NTOK], BF16), sb("f_h_lo", [P, PART_MAX * NTOK], BF16)
        act_out, hidden = two("f_silu", [P, CHUNK]), two("f_hidden", [P, CHUNK])
        total, x1 = two("f_total", [P, D_MODEL]), two("f_x1", [P, D_MODEL])
        squares = sb("f_squares", [P, D_MODEL], BF16)
        gain = sb("f_gain", [P, D_MODEL])
        power = sb("f_power", [P, 1])
        ss, ms, rstd = two("f_ss", [P, 1]), two("f_ms", [P, 1]), two("f_rstd", [P, 1])
        pb = lambda n, w: ctx.enter_context(nc.psum_tensor(n, [P, w], F32))
        ps_gate, ps_up = [pb(f"f_ps_gate{i}", CHUNK) for i in range(2)], [pb(f"f_ps_up{i}", CHUNK) for i in range(2)]
        ps_y = [pb(f"f_ps_y{i}", D_MODEL) for i in range(2)]
        (raw_in0, raw_in1, raw_in2, gain_in, part_in0, part_in1, x1_in0, x1_in1, store0, store1, w_hi_done, w_split,
         down_hi_done, down_split, unit_ready, silu_done, hidden_done, h_hi_done, h_done, y_ready, total_done, power_ready,
         ss_done, ms_done, rstd_done, scaled, y_done) = sems.new(
            "f_raw_in0", "f_raw_in1", "f_raw_in2", "f_gain_in", "f_part_in0", "f_part_in1", "f_x1_in0", "f_x1_in1",
            "f_store0", "f_store1", "f_w_hi_done", "f_w_split", "f_down_hi_done", "f_down_split", "f_unit_ready",
            "f_silu_done", "f_hidden_done", "f_h_hi_done", "f_h_done", "f_y_ready", "f_total_done", "f_power_ready",
            "f_ss_done", "f_ms_done", "f_rstd_done", "f_scaled", "f_y_done")
        raw_in, part_in, x1_in, store = [raw_in0, raw_in1, raw_in2], [part_in0, part_in1], [x1_in0, x1_in1], [store0, store1]
        uses = [TILES // 2 + 1, TILES // 2]
        kt_rows = lambda raw_: raw_[:, :].rearrange("p (k c) -> p k c", k=KT)

        with nc.Block() as block:
            @block.sync
            def _(sp):
                def weights(m):
                    if not isinstance(m, int) or m:
                        wait_before(sp, (gain_in, 16), w_split, m * 2 + 2)
                    for i, src in enumerate((g.w_gate, g.w_up)):
                        sp.dma_start(kt_rows(raw[i]), src[:, ds(m * P, P)].rearrange("(k p) c -> p k c", p=P))\
                            .then_inc(raw_in[i], 16)
                    if not isinstance(m, int) or m:
                        wait_before(sp, (gain_in, 16), down_split, m + 1)
                    sp.dma_start(raw[2][:, :], g.w_down[ds(m * P, P), :]).then_inc(raw_in[2], 16)

                def down_loads(part, t, s, n, nth):
                    if part:
                        src = token_rows(g.y_part[0:SEQ, :], g.y_part[SEQ:, :], t, n)
                        sp.dma_start(total[s][0:n, :], src).then_inc(part_in[s], 16)
                    if part == LAST:
                        src = token_rows(g.x1_dram[0:SEQ, :], g.x1_dram[SEQ:, :], t, n)
                        sp.dma_start(x1[s][0:n, :], src).then_inc(x1_in[s], 16)

                def down_store(part, t, s, n):
                    if part < LAST:
                        wait_before(sp, (gain_in, 16), total_done, part * n_down + t + 1)
                        dst = token_rows(g.y_part[0:SEQ, :], g.y_part[SEQ:, :], t, n)
                        sp.dma_start(dst, total[s][0:n, :]).then_inc(store[s], 16)
                    else:
                        wait_before(sp, (gain_in, 16), y_done, t + 1)
                        sp.dma_start(token_rows(g.y_prompt, g.y_sample, t, n), x1[s][0:n, :]).then_inc(store[s], 16)

                weights(0)
                sp.dma_start(gain[:, :], g.g_ffn_post.to_broadcast([P, D_MODEL])).then_inc(gain_in, 16)
                sp.wait_ge(gain_in, 16)
                for part, n_tiles in enumerate(PARTS):
                    with sp.Fori(0, n_tiles - 1) as m:
                        weights(m + firsts[part] + 1)
                    if part < LAST:
                        weights(firsts[part + 1])
                    for s in range(2):
                        if part:
                            sp.wait_ge(store[0], part * uses[0] * 16)
                            sp.wait_ge(store[1], part * uses[1] * 16)
                        down_loads(part, s, s, P, 0)

                    def move(t, s, nth, more):
                        down_store(part, t, s, P)
                        if part and more:
                            wait_before(sp, (gain_in, 16), store[s], (part * uses[s] + nth + 1) * 16)
                            down_loads(part, t + 2, s, more, nth + 1)
                    with sp.Fori(0, TILES // 2 - 1) as pair:
                        for s in range(2):
                            move(pair * 2 + s, s, pair, P)
                    move(TILES - 2, 0, TILES // 2 - 1, NSAMP)
                    move(TILES - 1, 1, TILES // 2 - 1, 0)
                    down_store(part, TILES, 0, NSAMP)
                for s in range(2):
                    sp.wait_ge(store[s], len(PARTS) * uses[s] * 16)

            @block.tensor
            def _(pe):
                for part, n_tiles in enumerate(PARTS):
                    def up(m, slot):
                        for c, (c0, n) in enumerate(CHUNKS):
                            unit = m * NC + c
                            u = (slot * NC + c) % 2
                            pe.wait_ge(hidden_done, unit + 1)
                            for i, ps in enumerate((ps_gate, ps_up)):
                                if c == 0:
                                    pe.wait_ge(w_split, m * 2 + 3 + i)
                                for k in range(KT):
                                    mm = product(nc.tensor, ps[u][:, 0:n], w_hi[slot][i][:, k, :], w_lo[slot][i][:, k, :],
                                                 g.act_hi[:, k, c0:c0 + n], g.act_lo[:, k, c0:c0 + n], k == 0, k == KT - 1)
                            mm.then_inc(unit_ready, 1)
                    with pe.Fori(0, n_tiles // 2) as pair:
                        for slot in range(2):
                            up(pair * 2 + (firsts[part] + slot), slot)

                    def down(t, s, n, nth):
                        if part or not isinstance(t, int) or t > 1:
                            pe.wait_ge(total_done, part * n_down + t - 1)
                        for k in range(n_tiles):
                            for half in range(HALVES):
                                cols = slice(half * CHUNK, (half + 1) * CHUNK)
                                at = ds(k * NTOK + t * P, n)
                                mm = product(nc.tensor, ps_y[s][0:n, cols], h_hi[:, at], h_lo[:, at], down_hi[:, k, cols],
                                             down_lo[:, k, cols], k == 0, k == n_tiles - 1)
                        mm.then_inc(y_ready, 1)
                    pe.wait_ge(down_split, 1 + firsts[part] + n_tiles)
                    pe.wait_ge(h_done, (firsts[part] + n_tiles) * NC)
                    down(0, 0, P, 0)
                    down(1, 1, P, 0)
                    with pe.Fori(1, TILES // 2) as pair:
                        for s in range(2):
                            down(pair * 2 + s, s, P, pair)
                    down(TILES, 0, NSAMP, TILES // 2)

            @block.scalar
            def _(act):
                def split_up(m, slot):
                    for i in range(2):
                        act.wait_ge(raw_in[i], (m + 1) * 16)
                        if not isinstance(m, int) or m > 1:
                            act.wait_ge(unit_ready, m * NC - NC)
                        nc.scalar.activation(w_hi[slot][i][:, :, :], kt_rows(raw[i]), ACT.Copy).then_inc(w_hi_done, 1)

                def split_down(m, k):
                    act.wait_ge(raw_in[2], (m + 1) * 16)
                    nc.scalar.activation(down_hi[:, ds(k, 1), :].rearrange("p o c -> p (o c)"), raw[2][:, :],
                                         ACT.Copy).then_inc(down_hi_done, 1)

                def units(m, slot, k):
                    for c, (c0, n) in enumerate(CHUNKS):
                        unit = m * NC + c
                        u = (slot * NC + c) % 2
                        act.wait_ge(unit_ready, unit + 1)
                        nc.scalar.activation(act_out[u][:, 0:n], ps_gate[u][:, 0:n], ACT.Silu).then_inc(silu_done, 1)
                        act.wait_ge(hidden_done, unit + 3)
                        nc.scalar.activation(h_hi[:, ds(k * NTOK + c0, n)], hidden[u][:, 0:n], ACT.Copy).then_inc(h_hi_done, 1)

                split_up(0, 0)
                for part, n_tiles in enumerate(PARTS):
                    first = firsts[part]
                    if part:
                        act.wait_ge(y_ready, part * n_down)

                    def tile(m, slot, k, more):
                        if more:
                            split_up(m + 1, 1 - slot)
                        split_down(m, k)
                        units(m, slot, k)
                    with act.Fori(0, n_tiles // 2 - 1) as pair:
                        for slot in range(2):
                            tile(pair * 2 + (first + slot), slot, pair * 2 + slot, True)
                    tile(first + n_tiles - 2, 0, n_tiles - 2, True)
                    tile(first + n_tiles - 1, 1, n_tiles - 1, part < LAST)
                    if part == LAST:
                        def square(t, s, n, nth, one):
                            act.wait_ge(total_done, part * n_down + t + 1)
                            act.wait_ge(ss_done, t)
                            nc.scalar.activation(squares[0:n, :], total[s][0:n, :], ACT.Square,
                                                 accum_out=ss[s][0:n, :]).then_inc(ss_done, 1)
                        token_tiles_in_turn(act, square)

            @block.gpsimd
            def _(pool):
                nc.gpsimd.memset(power[:, :], -0.5).then_inc(power_ready, 1)
                pool.wait_ge(power_ready, 1)

                def finish(t, s, n, nth, first):
                    wait_before(pool, (power_ready, 1), ss_done, t + 1)
                    nc.gpsimd.tensor_scalar(ms[s][0:n, :], ss[s][0:n, :], 1.0 / D_MODEL, EPS, ALU.mult,
                                            ALU.add).then_inc(ms_done, 1)
                    pool.wait_ge(ms_done, t + 1)
                    nc.gpsimd.tensor_tensor(rstd[s][0:n, :], ms[s][0:n, :], power[0:n, :], ALU.pow).then_inc(rstd_done, 1)
                token_tiles_in_turn(pool, finish)

            @block.vector
            def _(dve):
                def split_up(m, slot):
                    for i in range(2):
                        dve.wait_ge(w_hi_done, m * 2 + i + 1)
                        nc.vector.tensor_tensor(w_lo[slot][i][:, :, :], kt_rows(raw[i]), w_hi[slot][i][:, :, :],
                                                ALU.subtract).then_inc(w_split, 1)

                def split_down(m, k):
                    dve.wait_ge(down_hi_done, m + 1)
                    row = lambda w: w[:, ds(k, 1), :].rearrange("p o c -> p (o c)")
                    nc.vector.tensor_tensor(row(down_lo), raw[2][:, :], row(down_hi), ALU.subtract).then_inc(down_split, 1)

                def units(m, slot, k):
                    for c, (c0, n) in enumerate(CHUNKS):
                        unit = m * NC + c
                        u = (slot * NC + c) % 2
                        dve.wait_ge(silu_done, unit + 1)
                        nc.vector.tensor_tensor(hidden[u][:, 0:n], act_out[u][:, 0:n], ps_up[u][:, 0:n],
                                                ALU.mult).then_inc(hidden_done, 1)
                        dve.wait_ge(h_hi_done, unit + 1)
                        at = ds(k * NTOK + c0, n)
                        nc.vector.tensor_tensor(h_lo[:, at], hidden[u][:, 0:n], h_hi[:, at], ALU.subtract).then_inc(h_done, 1)

                dve.sem_inc(w_split, 2)
                dve.sem_inc(down_split, 1)
                dve.sem_inc(hidden_done, 2)
                split_up(0, 0)
                for part, n_tiles in enumerate(PARTS):
                    first = firsts[part]

                    def tile(m, slot, k, more):
                        if more:
                            split_up(m + 1, 1 - slot)
                        split_down(m, k)
                        units(m, slot, k)
                    with dve.Fori(0, n_tiles // 2 - 1) as pair:
                        for slot in range(2):
                            tile(pair * 2 + (first + slot), slot, pair * 2 + slot, True)
                    tile(first + n_tiles - 2, 0, n_tiles - 2, True)
                    tile(first + n_tiles - 1, 1, n_tiles - 1, part < LAST)

                    def down(t, s, n, nth, one):
                        y = part * n_down + t
                        dve.wait_ge(y_ready, y + 1)
                        if part == 0:
                            dve.wait_ge(store[s], nth * 16)
                            nc.vector.tensor_copy(total[s][0:n, :], ps_y[s][0:n, :]).then_inc(total_done, 1)
                        else:
                            dve.wait_ge(part_in[s], ((part - 1) * uses[s] + nth + 1) * 16)
                            nc.vector.tensor_tensor(total[s][0:n, :], total[s][0:n, :], ps_y[s][0:n, :],
                                                    ALU.add).then_inc(total_done, 1)
                        if part == LAST:
                            if one:
                                dve.wait_ge(gain_in, 16)
                            dve.wait_ge(rstd_done, t + 1)
                            nc.vector.scalar_tensor_tensor(total[s][0:n, :], total[s][0:n, :], rstd[s][0:n, 0:1], gain[0:n, :],
                                                           ALU.mult, ALU.mult).then_inc(scaled, 1)
                            dve.wait_ge(scaled, t + 1)
                            dve.wait_ge(x1_in[s], (nth + 1) * 16)
                            nc.vector.tensor_tensor(x1[s][0:n, :], x1[s][0:n, :], total[s][0:n, :], ALU.add).then_inc(y_done, 1)
                    token_tiles_in_turn(dve, down)




N_IN = 4 * D_M + 2 * H_M + 3 * D_A


def views():
    return {
        "x_prompt": (SEQ, D_MODEL), "x_sample": (NSAMP, D_MODEL), "cache_kv": (DEC_BATCH, PAST_LEN, 2 * D_A),
        "state_C": (DEC_BATCH, H_M, HD_M, HD_M), "state_n": (DEC_BATCH * H_M, HD_M), "state_m": (DEC_BATCH, H_M),
        "state_conv": (DEC_BATCH * HIST, 2 * D_M), "g_mix_pre": (1, D_MODEL), "g_mix_post": (1, D_MODEL),
        "g_ffn_pre": (1, D_MODEL), "g_ffn_post": (1, D_MODEL), "w_in": (D_MODEL, N_IN), "b_gates": (2 * H_M, 1),
        "w_conv": (CONV_W, 2 * D_M), "g_mh": (H_M, HD_M), "w_out": (D_MODEL, D_MODEL), "w_gate": (D_MODEL, D_FF),
        "w_up": (D_MODEL, D_FF), "w_down": (D_FF, D_MODEL),
    }


def output_shapes():
    return {
        "y_prompt": (SEQ, D_MODEL), "y_sample": (NSAMP, D_MODEL), "kv_prompt": (SEQ, 2 * D_A),
        "kv_sample": (NSAMP, 2 * D_A), "C_prompt": (H_M, HD_M, HD_M), "n_prompt": (H_M, HD_M), "m_prompt": (1, H_M),
        "conv_prompt": (HIST, 2 * D_M), "C_sample": (DEC_BATCH, H_M, HD_M, HD_M), "n_sample": (DEC_BATCH, H_M, HD_M),
        "m_sample": (DEC_BATCH, H_M), "conv_sample": (DEC_BATCH * HIST, 2 * D_M),
    }


def returned_shapes():
    return {
        "y_prompt": (1, SEQ, D_MODEL), "y_sample": (DEC_BATCH, DEC_SEQ, D_MODEL), "kv_prompt": (1, 1, SEQ, 2, H_A, HD_A),
        "kv_sample": (1, DEC_BATCH, DEC_SEQ, 2, H_A, HD_A), "C_prompt": (1, 1, H_M, HD_M, HD_M),
        "n_prompt": (1, 1, H_M, HD_M), "m_prompt": (1, 1, H_M), "conv_prompt": (1, 1, HIST, 2 * D_M),
        "C_sample": (1, DEC_BATCH, H_M, HD_M, HD_M), "n_sample": (1, DEC_BATCH, H_M, HD_M),
        "m_sample": (1, DEC_BATCH, H_M), "conv_sample": (1, DEC_BATCH, HIST, 2 * D_M),
    }


def shape_constants():
    import numpy as np

    far_away = -1e30
    slopes = 2.0 ** (-8.0 * np.arange(1, H_A + 1) / H_A)

    def weight_log(dist):
        count = ((dist >= 0) & (dist <= 128)).astype(np.int64)
        count += (dist >= 0) & (dist <= 512) & (dist % 4 == 0)
        count += (dist >= 0) & (dist <= 2048) & (dist % 16 == 0)
        return np.where(count > 0, np.log(np.maximum(count, 1)), far_away)

    dist = np.arange(P)[:, None] + (TILES - 1) * P - np.arange(SEQ)[None, :]
    bias = np.stack([np.where(weight_log(dist) > far_away / 2, weight_log(dist) - s * dist, far_away) for s in slopes])
    far = [FAR_STRIDE * (j // DEC_SEQ) + j % DEC_SEQ for j in range(FAR_TILES * P)]
    keys = np.array(far + list(range(FAR, PAST_LEN + DEC_SEQ)))
    dist = (PAST_LEN + np.arange(DEC_SEQ))[:, None] - keys[None, :]
    w = weight_log(dist)
    sbias = np.concatenate([np.where(w > far_away / 2, w - s * dist, far_away) for s in slopes])
    causal = np.where(np.arange(P)[:, None] <= np.arange(P)[None, :], 0.0, far_away)
    a = np.arange(NSAMP)
    sees = (a[:, None] <= a[None, :]) & (a[:, None] // DEC_SEQ == a[None, :] // DEC_SEQ)
    member = (a[:, None] // DEC_SEQ == np.arange(DEC_BATCH)[None, :])
    chunk_of = np.concatenate([np.arange(SEQ) % P, a % DEC_SEQ]) != 0
    own = np.zeros((H_M, H_M, SEGMENTS))
    for h in range(H_M):
        own[h, h] = 1.0
    return {
        "ident": np.eye(P), "attn_bias": bias, "sample_bias": sbias, "causal": causal,
        "sample_causal": np.where(sees, 0.0, far_away), "member": member,
        "carries": np.broadcast_to(chunk_of, (H_M, NTOK)), "own_head": own,
    }


def stage_attention(nc, g, sems):
    with ExitStack() as ctx:
        sb = lambda n, s, d=F32: ctx.enter_context(nc.sbuf_tensor(n, s, d))
        g.mix_a_hi, g.mix_a_lo = [sb(f"mix_a_{n}", [P, PAIRS * NTOK], BF16) for n in ("hi", "lo")]
        g.q_pairs = sb("q_pairs", [P, PAIRS * DEC_BATCH * HT + (PAIRS - 1) * 2 * DEC_SEQ])
        g.k_new = sb("k_new", [P, PAIRS * NSAMP])
        stage_prompt_attention(nc, g, sems)
        stage_sample_attention(nc, g, sems)
        sems.give_back()


def build(nc, dram):
    with ExitStack() as ctx:
        sems = Sems(nc)
        g = Program(dram)
        internal = lambda name, shape, d=F32: nc.dram_tensor(name, shape, d, kind="Internal").ap()
        g.u_dram = internal("u_rows", (H_M, NTOK))
        g.mix_a_dram = internal("mix_a_rows", (2, P, PAIRS * NTOK), BF16)
        g.x1_dram, g.y_part = internal("x1_rows", (NTOK, D_MODEL)), internal("y_part_rows", (NTOK, D_MODEL))
        sb = lambda scope, n, s, d=F32: scope.enter_context(nc.sbuf_tensor(n, s, d))
        g.ident = sb(ctx, "ident", [P, P])
        g.act_hi, g.act_lo = sb(ctx, "act_hi", [P, KT, NTOK], BF16), sb(ctx, "act_lo", [P, KT, NTOK], BF16)
        with ExitStack() as mix:
            g.table = sb(mix, "table", [P, H_M, TAB])
            with ExitStack() as early:
                g.gates = sb(early, "gates", [GATE_ROWS, NTOK])
                g.a_w_raw = [sb(early, f"a_w_raw{i}", [P, KT, P]) for i in range(3)]
                g.a_w_in = sems.new("a_w_in0", "a_w_in1", "a_w_in2")
                stage_normalise_inputs(nc, g, sems)
                stage_attention(nc, g, sems)
                stage_gates(nc, g, sems)
            g.mix_m_hi, g.mix_m_lo = [sb(mix, f"mix_m_{n}", [P, H_M * NTOK], BF16) for n in ("hi", "lo")]
            g.w_out_first = sb(mix, "w_out_first", [P, D_MODEL])
            [g.w_out_first_in] = sems.new("w_out_first_in")
            stage_mlstm(nc, g, sems)
            stage_mix_out(nc, g, sems)
        stage_ffn(nc, g, sems)


def kernel(**inputs):
    import numpy as np
    import concourse.bacc as bacc
    from concourse.bass_utils import run_bass_kernel_spmd

    nc = bacc.Bacc("TRN2", target_bir_lowering=False, num_devices=1)
    arrays, dram = {}, {}
    for name, shape in views().items():
        arrays[f"in_{name}"] = np.ascontiguousarray(inputs[name]).reshape(shape)
        dram[name] = nc.dram_tensor(f"in_{name}", shape, F32, kind="ExternalInput").ap()
    for name, table in shape_constants().items():
        arrays[f"const_{name}"] = np.ascontiguousarray(table, dtype=np.float32)
        dram[name] = nc.dram_tensor(f"const_{name}", table.shape, F32, kind="ExternalInput").ap()
    for name, shape in output_shapes().items():
        dram[name] = nc.dram_tensor(f"out_{name}", shape, F32, kind="ExternalOutput").ap()
    build(nc, dram)
    got = run_bass_kernel_spmd(nc, [arrays], core_ids=[0]).results[0]
    return tuple(np.asarray(got[f"out_{name}"]).reshape(shape) for name, shape in returned_shapes().items())
```
